# Optimizing a Trainium2 kernel written in Bass

```python
import jax
import jax.numpy as jnp
from jax import lax
import numpy as np

D_MODEL = 1024
BATCH = 1
SEQ = 1024
DEPTH = 2

GRID_W = 64
CTX_LEN = 256
HEAD_DIM = 64
ATT_WIDTH = D_MODEL // 2
ATT_HEADS = ATT_WIDTH // HEAD_DIM
LRU_WIDTH = D_MODEL // 2
LRU_BLOCKS = 8
LRU_BLOCK = LRU_WIDTH // LRU_BLOCKS
LRU_CONV = 4
LRU_PAD = (2, 1)
LRU_C = 8.0
IN_WIDTH_EVEN = 3 * ATT_WIDTH + 2 * LRU_WIDTH
WIN_ROWS_MAX = 8
WIN_COLS = 16
Q_ROWS = 2
SC_WIDTH = D_MODEL
SC_CONV = 3
SC_PAD = (1, 1)
FFN_HIDDEN = ((8 * D_MODEL + 3 * 256 - 1) // (3 * 256)) * 256
N_EVEN = (DEPTH + 1) // 2
N_ODD = DEPTH // 2
EPS = 1e-6

kernel_name = "hybrid_na_rglru_shortconv_dit"

def rmsnorm(x, g):
    xf = x.astype(jnp.float32)
    y = xf * lax.rsqrt(jnp.mean(xf * xf, axis=-1, keepdims=True) + EPS)
    return (y * g.astype(jnp.float32)).astype(x.dtype)

def adaln(cond, w, b):
    m = jax.nn.silu(cond) @ w + b
    return jnp.split(m[..., None, :], 6, axis=-1)

def modulate(x, shift, scale):
    return x * (1 + scale) + shift

def dwconv(x, w, pad):
    ch = x.shape[-1]
    return lax.conv_general_dilated(x, w[:, None, :].astype(x.dtype), window_strides=(1,),
                                    padding=[pad], dimension_numbers=("NWC", "WIO", "NWC"),
                                    feature_group_count=ch)

def swiglu(h, w_gu, w_down):
    gt, up = jnp.split(h @ w_gu, 2, axis=-1)
    return (jax.nn.silu(gt) * up) @ w_down

def linear_scan(a, b, h0, reverse):
    if reverse:
        b = b.at[:, -1].add(a[:, -1] * h0)
    else:
        b = b.at[:, 0].add(a[:, 0] * h0)

    def combine(l, r):
        return l[0] * r[0], r[0] * l[1] + r[1]

    _, h = lax.associative_scan(combine, (a, b), reverse=reverse, axis=1)
    return h

def rglru_coeffs(xc, w_r, b_r, w_i, b_i, lam):
    bsz, s, _ = xc.shape
    xb = xc.reshape(bsz, s, LRU_BLOCKS, LRU_BLOCK)
    f32 = jnp.float32
    r = jax.nn.sigmoid(jnp.einsum("bsgi,gij->bsgj", xb, w_r.astype(f32)).reshape(bsz, s, LRU_WIDTH) + b_r.astype(f32))
    i = jax.nn.sigmoid(jnp.einsum("bsgi,gij->bsgj", xb, w_i.astype(f32)).reshape(bsz, s, LRU_WIDTH) + b_i.astype(f32))
    log_a = -LRU_C * r * jax.nn.softplus(-lam.astype(f32))
    return jnp.exp(log_a), jnp.sqrt(-jnp.expm1(2.0 * log_a)) * (i * xc)

def bidir_rglru(xl, xc, w_r, b_r, w_i, b_i, lam, ctx_out):
    xl32 = xl.astype(jnp.float32)
    xc32 = xc.astype(jnp.float32)
    lat, con = [], []
    for d, rev in enumerate((False, True)):
        a_c, u_c = rglru_coeffs(xc32, w_r[d], b_r[d], w_i[d], b_i[d], lam[d])
        h_c = linear_scan(a_c, u_c, jnp.zeros_like(xc32[:, 0]), rev)
        h0 = h_c[:, 0] if rev else h_c[:, -1]
        a_l, u_l = rglru_coeffs(xl32, w_r[d], b_r[d], w_i[d], b_i[d], lam[d])
        lat.append(linear_scan(a_l, u_l, h0, rev))
        con.append(h_c)
    yl = (lat[0] + lat[1]).astype(xl.dtype)
    yc = (con[0] + con[1]).astype(xc.dtype) if ctx_out else None
    return yl, yc

def neighbourhood_attention(q, k, v, k_ctx, v_ctx, rpb):
    bsz, s, nh, dh = q.shape
    rows = s // GRID_W
    wr = min(WIN_ROWS_MAX, rows)
    qg = (q * (dh ** -0.5)).reshape(bsz, rows, GRID_W, nh, dh)
    kg = k.reshape(bsz, rows, GRID_W, nh, dh)
    vg = v.reshape(bsz, rows, GRID_W, nh, dh)
    row_start = jnp.clip(jnp.arange(rows) - wr // 2, 0, rows - wr)
    row_idx = row_start[:, None] + jnp.arange(wr)
    col_start = jnp.clip(jnp.arange(GRID_W) - WIN_COLS // 2, 0, GRID_W - WIN_COLS)
    col_idx = col_start[:, None] + jnp.arange(WIN_COLS)
    dc = col_idx - jnp.arange(GRID_W)[:, None] + (WIN_COLS - 1)
    n_keys_win = wr * WIN_COLS

    def block(i):
        r0 = i * Q_ROWS
        qb = lax.dynamic_slice_in_dim(qg, r0, Q_ROWS, axis=1)
        ridx = lax.dynamic_slice_in_dim(row_idx, r0, Q_ROWS, axis=0)
        kw = jnp.take(jnp.take(kg, ridx, axis=1), col_idx, axis=3)
        vw = jnp.take(jnp.take(vg, ridx, axis=1), col_idx, axis=3)
        dr = ridx - (r0 + jnp.arange(Q_ROWS))[:, None] + (WIN_ROWS_MAX - 1)
        bias = rpb[:, dr[:, None, :, None], dc[None, :, None, :]]
        s_win = jnp.einsum("bqjhd,bqrjchd->bhqjrc", qb, kw) + bias[None]
        s_ctx = jnp.einsum("bqjhd,bnhd->bhqjn", qb, k_ctx)
        logits = jnp.concatenate([s_win.reshape(s_win.shape[:4] + (n_keys_win,)), s_ctx], axis=-1)
        p = jax.nn.softmax(logits.astype(jnp.float32), axis=-1).astype(v.dtype)
        p_win = p[..., :n_keys_win].reshape(s_win.shape)
        p_ctx = p[..., n_keys_win:]
        return (jnp.einsum("bhqjrc,bqrjchd->bqjhd", p_win, vw)
                + jnp.einsum("bhqjn,bnhd->bqjhd", p_ctx, v_ctx))

    out = lax.map(block, jnp.arange(rows // Q_ROWS))
    return jnp.moveaxis(out, 0, 1).reshape(bsz, s, nh * dh)

def context_attention(q, k, v):
    s = jnp.einsum("bnhd,bmhd->bhnm", q, k) * (q.shape[-1] ** -0.5)
    p = jax.nn.softmax(s.astype(jnp.float32), axis=-1).astype(v.dtype)
    out = jnp.einsum("bhnm,bmhd->bnhd", p, v)
    return out.reshape(out.shape[0], out.shape[1], -1)

def hybrid_mixer(hl, hc, w_in, w_out, conv_w, conv_b, lru_wr, lru_br, lru_wi, lru_bi, lru_lam, rpb, ctx_out):
    splits = [ATT_WIDTH, 2 * ATT_WIDTH, 3 * ATT_WIDTH, 3 * ATT_WIDTH + LRU_WIDTH]

    def heads(t):
        return t.reshape(t.shape[0], t.shape[1], ATT_HEADS, HEAD_DIM)

    q, k, v, xr, gr = jnp.split(hl @ w_in, splits, axis=-1)
    w_q, w_k, w_v, w_x, w_g = jnp.split(w_in, splits, axis=1)
    kc, vc = heads(hc @ w_k), heads(hc @ w_v)
    att = neighbourhood_attention(heads(q), heads(k), heads(v), kc, vc, rpb)
    xr = dwconv(xr, conv_w, LRU_PAD) + conv_b
    xc = dwconv(hc @ w_x, conv_w, LRU_PAD) + conv_b
    rec, rec_c = bidir_rglru(xr, xc, lru_wr, lru_br, lru_wi, lru_bi, lru_lam, ctx_out)
    y = jnp.concatenate([att, rec * jax.nn.gelu(gr)], axis=-1) @ w_out
    if not ctx_out:
        return y, None
    att_c = context_attention(heads(hc @ w_q), kc, vc)
    yc = jnp.concatenate([att_c, rec_c * jax.nn.gelu(hc @ w_g)], axis=-1) @ w_out
    return y, yc

def short_conv_mixer(h, w_in, w_conv, w_out):
    bg, cg, xv = jnp.split(h @ w_in, 3, axis=-1)
    return (bg * dwconv(cg * xv, w_conv, SC_PAD)) @ w_out

def setup_inputs(seed: int = 0) -> dict:
    key = jax.random.key(seed)
    ks = iter(jax.random.split(key, 32))
    D = D_MODEL
    f32 = jnp.float32

    def nrm(shape, s):
        return s * jax.random.normal(next(ks), shape, f32)

    u = jax.random.uniform(next(ks), (N_EVEN, 2, LRU_WIDTH), f32, minval=0.9, maxval=0.999)
    p = u ** (1.0 / LRU_C)
    lam = jnp.log(p) - jnp.log1p(-p)
    return {
        "x": nrm((BATCH, SEQ, D), 1.0),
        "c": nrm((BATCH, D), 1.0),
        "ctx": nrm((BATCH, CTX_LEN, D), 1.0),
        "c_ctx": nrm((D,), 1.0),
        "mod_w": nrm((DEPTH, D, 6 * D), D ** -0.5),
        "mod_b": nrm((DEPTH, 6 * D), 0.02),
        "norm1_g": 1.0 + nrm((DEPTH, D), 0.05),
        "norm2_g": 1.0 + nrm((DEPTH, D), 0.05),
        "ffn_w_gu": nrm((DEPTH, D, 2 * FFN_HIDDEN), D ** -0.5),
        "ffn_w_down": nrm((DEPTH, FFN_HIDDEN, D), FFN_HIDDEN ** -0.5),
        "e_w_in": nrm((N_EVEN, D, IN_WIDTH_EVEN), D ** -0.5),
        "e_w_out": nrm((N_EVEN, ATT_WIDTH + LRU_WIDTH, D), (ATT_WIDTH + LRU_WIDTH) ** -0.5),
        "e_conv_w": nrm((N_EVEN, LRU_CONV, LRU_WIDTH), LRU_CONV ** -0.5),
        "e_conv_b": nrm((N_EVEN, LRU_WIDTH), 0.02),
        "e_lru_wr": nrm((N_EVEN, 2, LRU_BLOCKS, LRU_BLOCK, LRU_BLOCK), LRU_BLOCK ** -0.5),
        "e_lru_br": nrm((N_EVEN, 2, LRU_WIDTH), 0.02),
        "e_lru_wi": nrm((N_EVEN, 2, LRU_BLOCKS, LRU_BLOCK, LRU_BLOCK), LRU_BLOCK ** -0.5),
        "e_lru_bi": nrm((N_EVEN, 2, LRU_WIDTH), 0.02),
        "e_lru_lam": lam,
        "e_rpb": nrm((N_EVEN, ATT_HEADS, 2 * WIN_ROWS_MAX - 1, 2 * WIN_COLS - 1), 0.1),
        "o_w_in": nrm((N_ODD, D, 3 * SC_WIDTH), D ** -0.5),
        "o_conv_w": nrm((N_ODD, SC_CONV, SC_WIDTH), SC_CONV ** -0.5),
        "o_w_out": nrm((N_ODD, SC_WIDTH, D), SC_WIDTH ** -0.5),
        "final_g": 1.0 + nrm((D,), 0.05),
    }

def reference(x, c, ctx, c_ctx, mod_w, mod_b, norm1_g, norm2_g, ffn_w_gu, ffn_w_down,
              e_w_in, e_w_out, e_conv_w, e_conv_b, e_lru_wr, e_lru_br, e_lru_wi, e_lru_bi,
              e_lru_lam, e_rpb, o_w_in, o_conv_w, o_w_out, final_g):
    h, hc = x, ctx
    for l in range(DEPTH):
        even = l % 2 == 0
        ctx_out = any(j % 2 == 0 for j in range(l + 1, DEPTH))
        sh1, sc1, g1, sh2, sc2, g2 = adaln(c, mod_w[l], mod_b[l])
        n_lat = modulate(rmsnorm(h, norm1_g[l]), sh1, sc1)
        if even or ctx_out:
            csh1, csc1, cg1, csh2, csc2, cg2 = adaln(c_ctx, mod_w[l], mod_b[l])
            n_ctx = modulate(rmsnorm(hc, norm1_g[l]), csh1, csc1)
        if even:
            e = l // 2
            y, yc = hybrid_mixer(n_lat, n_ctx, e_w_in[e], e_w_out[e], e_conv_w[e], e_conv_b[e],
                                 e_lru_wr[e], e_lru_br[e], e_lru_wi[e], e_lru_bi[e], e_lru_lam[e],
                                 e_rpb[e], ctx_out)
        else:
            o = l // 2
            y = short_conv_mixer(n_lat, o_w_in[o], o_conv_w[o], o_w_out[o])
            yc = short_conv_mixer(n_ctx, o_w_in[o], o_conv_w[o], o_w_out[o]) if ctx_out else None
        h = h + g1 * y
        h = h + g2 * swiglu(modulate(rmsnorm(h, norm2_g[l]), sh2, sc2), ffn_w_gu[l], ffn_w_down[l])
        if ctx_out:
            hc = hc + cg1 * yc
            hc = hc + cg2 * swiglu(modulate(rmsnorm(hc, norm2_g[l]), csh2, csc2), ffn_w_gu[l], ffn_w_down[l])
    return rmsnorm(h, final_g)


_drawn_inputs = setup_inputs


def setup_inputs(seed=0):
    import zlib

    import numpy as np

    out = dict(_drawn_inputs(seed))
    spreads = {}
    factors = {'norm2_g': 2.744, 'e_lru_br': 8.0, 'e_lru_bi': 8.0, 'e_rpb': 8.0}
    for name, (base, spread) in spreads.items():
        noise = np.random.default_rng([zlib.crc32(name.encode()), seed]).standard_normal(out[name].shape)
        drawn = base * np.exp(spread * noise) if base else spread * noise
        out[name] = jnp.asarray(drawn.astype(out[name].dtype))
    for name, factor in factors.items():
        out[name] = (out[name] * factor).astype(out[name].dtype)
    return out
```

```python
from contextlib import ExitStack

import concourse.bass as bass
from concourse import mybir

ALU = mybir.AluOpType
ACT = mybir.ActivationFunctionType
AX_X = mybir.AxisListType.X
F32 = mybir.dt.float32
F32R = mybir.dt.float32r

P = 128
EPS = 1e-6
FAR = 1e30
GRID = 64
HALF = 512
UNIT = 1024


class Steps:

    def __init__(self, eng, sem):
        self.eng, self.sem, self.n, self.base = eng, sem, 0, 0

    def run(self, ins):
        ins.then_inc(self.sem, 1)
        self.n += 1
        self.eng.wait_ge(self.sem, self.base + self.n)

    def begin_loop(self, i, per):
        self.start, self.base, self.per = self.n, i * per, per

    def end_loop(self, rounds):
        assert self.n - self.start == self.per, (self.n - self.start, self.per)
        self.n, self.base = self.start + rounds * self.per, 0


def backbone(nc, t):
    x, context, out = t["x"], t["ctx"], t["out"]
    _, SEQ, D = x.shape
    CTX = context.shape[1]
    FT = D // P
    TT = SEQ // P
    CT = CTX // P
    KEYS = CTX + SEQ
    LT = t["e_conv_b"].shape[1] // P
    HID = t["ffn_w_down"].shape[1]
    ROUNDS = HID // (2 * P)
    _, HEADS, NR, NC = t["e_rpb"].shape
    MODS = 6
    SH1, SC1, G1, SH2, SC2, G2 = range(MODS)
    assert (SEQ, D, CTX, LT, HEADS, NR, NC) == (2 * HALF, 1024, 256, 4, 8, 15, 31)

    es = ExitStack()
    with es:
        def sem(name):
            return es.enter_context(nc.semaphore(name))

        def keep(name, shape, dt=F32):
            return es.enter_context(nc.sbuf_tensor(name, shape, dt))

        def at(kb, name, shape, dt=F32):
            with ExitStack() as s:
                if kb:
                    s.enter_context(nc.sbuf_tensor("below_" + name, [P, int(kb * 256)], F32))
                return s.enter_context(nc.sbuf_tensor(name, shape, dt))

        h_spill = nc.dram_tensor("h_spill", (P, FT, SEQ), F32, kind="Internal").ap()
        q_spill = nc.dram_tensor("q_spill", (LT, P, SEQ), F32, kind="Internal").ap()
        k_spill = nc.dram_tensor("k_spill", (LT, P, KEYS), F32, kind="Internal").ap()
        r_spill = nc.dram_tensor("r_spill", (LT, P, SEQ), F32, kind="Internal").ap()
        PAD = 64
        RPB = HEADS * NR * NC
        rpb_pad = nc.dram_tensor("rpb_pad", (1, PAD + RPB + PAD), F32, kind="Internal").ap()
        rpb_wide = nc.dram_tensor("rpb_wide", (HEADS, NR, GRID, GRID), F32, kind="Internal").ap()

        act_hi = keep("act_hi", [P, FT, SEQ], F32R)
        mod_ring = at(0, "mod_ring", [P, 4, UNIT])
        mod_row = at(16, "mod_row", [2, UNIT])
        fin = at(0, "fin", [P, FT, SEQ])
        act_lo = keep("act_lo", [P, FT, SEQ], F32R)
        w_hi4 = keep("w_hi4", [P, 4, UNIT], F32R)
        w_lo4 = keep("w_lo4", [P, 4, UNIT], F32R)
        raw = keep("raw", [P, 2, UNIT])
        ident = keep("ident", [P, P])
        ones = keep("ones", [P, P])
        mod_bias = keep("mod_bias", [P, 2 * MODS, FT])
        mods = keep("mods", [P, 2 * MODS, FT])
        mods_ctx = keep("mods_ctx", [P, 2 * MODS, FT])
        par = keep("par", [P, 124])
        cond = keep("cond", [P, FT, 2])
        gains = keep("gains", [P, 5, FT])
        half_b = keep("half_b", [P, 16])
        sp2 = keep("sp2", [P, 8])
        sp_t = keep("sp_t", [P, 5, 8])
        eps_t = keep("eps_t", [P, 1])
        std = keep("std", [P, 2, 4])

        h = at(0, "h", [P, FT, SEQ])
        w_hi2 = at(32, "w_hi2", [P, 2, UNIT], F32R)
        w_lo2 = at(40, "w_lo2", [P, 2, UNIT], F32R)
        sq = at(48, "sq", [P, 2, HALF])
        sumsq = at(52, "sumsq", [P, HALF])
        diag = at(54, "diag", [P, 4, P])
        scaled = at(56, "scaled", [P, 2, HALF])
        normed = at(60, "normed", [P, 2, HALF])
        x_in = at(64, "x_in", [P, 2, D])
        ctx_t = at(72, "ctx_t", [P, FT, CTX])
        par_rows = at(80, "par_rows", [124, P])
        b_rows = at(80.5, "b_rows", [96, P])
        zero_row = at(81, "zero_row", [1, PAD])
        hid_hi = at(64, "hid_hi", [P, 2, SEQ], F32R)
        hid_lo = at(72, "hid_lo", [P, 2, SEQ], F32R)
        silu_g = at(80, "silu_g", [P, 2, HALF])
        hid_f = at(84, "hid_f", [P, 2, HALF])
        z_hi = at(64, "z_hi", [P, SEQ], F32R)
        z_lo = at(68, "z_lo", [P, SEQ], F32R)
        cg_sb = at(72, "cg_sb", [P, 2, HALF])
        conv_t = at(76, "conv_t", [P, SEQ])
        z_f = at(80, "z_f", [P, 2, HALF])
        t_pad = at(84, "t_pad", [P, SEQ + 2])
        fin_rows = at(88, "fin_rows", [P, 2, D])
        lru_r = at(0, "lru_r", [P, 2, KEYS])
        lru_i = at(10, "lru_i", [P, 2, KEYS])
        lru_q = at(20, "lru_q", [P, 2, KEYS])
        gate_w = at(30, "gate_w", [P, 4, P])
        qk_out = at(32, "qk_out", [P, 5, HALF])
        g_gelu = at(42, "g_gelu", [P, SEQ])
        v_tok = at(48, "v_tok", [P, TT + CT, LT * P])
        x_pad = at(68, "x_pad", [P, KEYS + 6])
        x_conv = at(73.5, "x_conv", [P, KEYS])
        ctx_hi = at(80, "ctx_hi", [P, FT, CTX], F32R)
        ctx_lo = at(88, "ctx_lo", [P, FT, CTX], F32R)
        EDGE = 14 * GRID
        MID = 9 * GRID
        WIDE = MID + CTX
        r_in = at(0, "r_in", [P, 2, SEQ])
        probs_t = at(12, "probs_t", [P, 2, 7, P])
        bias_0 = at(20, "bias_0", [P, 2, EDGE + MID])
        bias_1 = at(32, "bias_1", [P, 2, EDGE + MID])
        o_tok = at(44, "o_tok", [P, 2, P])
        stat = at(45, "stat", [P, 4, 6])
        k_att = at(68, "k_att", [P, 2, KEYS])
        q_att = at(78, "q_att", [P, 2, SEQ])
        probs = at(86, "probs", [P, 2, WIDE])
        bias_t = (bias_0, bias_1)

        bank = es.enter_context(nc.psum_tensor("bank", [P, 8, HALF], F32))
        bank_f = bank[:, :, :].rearrange("p b n -> p (b n)")

        def w_slot(s):
            return (w_hi4[:, s, :], w_lo4[:, s, :]) if s < 4 else (w_hi2[:, s - 4, :], w_lo2[:, s - 4, :])

        U_P = 0
        U_V = U_P + 4 * LT
        U_O = U_V + 4
        U_F0 = U_O + 2 * FT
        U_S = U_F0 + 6 * ROUNDS
        U_F1 = U_S + 4 * FT
        U_END = U_F1 + 6 * ROUNDS

        s_par, s_ident, s_turn, s_par_t = sem("par_landed"), sem("ident_made"), sem("x_turned"), sem("par_turned")
        s_cond, s_param = sem("cond_ready"), sem("par_placed")
        s_x = (sem("x_landed0"), sem("x_landed1"))
        s_xpa, s_xpd = sem("x_placed_by_act"), sem("x_placed_by_dve")
        s_mod = [sem(f"mod_landed{j}") for j in range(4)]
        s_modmm, s_modrow, s_modt, s_modset = sem("mod_summed"), sem("mod_row_ready"), sem("mod_turned"), sem("mod_set")
        s_const = sem("constants_ready")
        s_raw = (sem("raw_landed0"), sem("raw_landed1"))
        s_hi, s_split = sem("unit_hi"), sem("unit_split")
        s_sq, s_sum, s_ss, s_sqrt, s_rstd = sem("squared"), sem("summed"), sem("sumsq_in_psum"), sem("rms_ready"), sem("diag_ready")
        s_bc, s_scal, s_nf, s_nhi, s_norm = sem("rstd_spread"), sem("scaled_ready"), sem("normed_ready"), sem("normed_hi"), sem("norm_done")
        s_spill, s_reload = sem("h_spilled"), sem("h_reloaded")
        s_proj, s_projev = sem("proj_done"), sem("proj_evacuated")
        s_qk = sem("qk_stored")
        s_pad, s_conv = sem("pads_zero"), sem("x_convolved")
        s_gw, s_gwz = sem("gate_w_landed"), sem("gate_w_zero")
        s_gate, s_gatev = sem("gate_done"), sem("gate_evacuated")
        s_s, s_rs, s_lru = sem("decay_ready"), sem("root_ready"), sem("lru_done")
        s_rfree = sem("lru_result_free")
        s_rst, s_rin = sem("lru_stored"), (sem("lru_reloaded0"), sem("lru_reloaded1"))
        s_v, s_vev = sem("v_done"), sem("v_evacuated")
        s_ylh, s_yll = sem("lru_hi"), sem("lru_lo")
        s_rpb, s_zero = sem("rpb_padded"), sem("zero_row_ready")
        s_wide = sem("bias_widened")
        s_braw = (sem("bias_landed0"), sem("bias_landed1"))
        s_bias = sem("bias_built")
        s_bstep = sem("pool_step")
        s_kq = (sem("qk_landed0"), sem("qk_landed1"))
        s_sc, s_min, s_exp = sem("scores_done"), sem("min_ready"), sem("probs_ready")
        s_pt, s_pta, s_ptd = sem("probs_turned"), sem("turned_by_act"), sem("turned_by_dve")
        s_pv, s_on, s_yt = sem("pv_done"), sem("o_scaled"), sem("o_turned")
        s_yh, s_yl = sem("y_hi"), sem("y_lo")
        s_out, s_hup = sem("out_done"), sem("h_updated")
        s_gu, s_silu, s_hidf = sem("gate_up_done"), sem("silu_ready"), sem("hidden_ready")
        s_hidh, s_hid = sem("hidden_hi"), sem("hidden_split")
        s_sg, s_cg, s_t, s_cv = sem("short_done"), sem("cg_ready"), sem("t_ready"), sem("short_convolved")
        s_zf, s_zh, s_z = sem("z_ready"), sem("z_hi_ready"), sem("z_split")
        s_tz = sem("t_pads_zero")
        s_fin, s_fturn, s_store = sem("fin_ready"), sem("fin_turned"), (sem("stored0"), sem("stored1"))
        s_fra, s_frd = sem("fin_row_by_act"), sem("fin_row_by_dve")
        s_dve, s_act = sem("dve_step"), sem("exp_ready")
        s_alone = sem("waits_alone")

        def alone(eng):
            eng.sem_inc(s_alone, 1)

        NORMS = ([(h, 0, HALF, 0, mods, SH1), (h, 1, HALF, 0, mods, SH1), (ctx_t, 0, CTX, 1, mods_ctx, SH1)]
                 + [(h, a, HALF, 2, mods, SH2) for a in (0, 1)]
                 + [(h, a, HALF, 3, mods, MODS + SH1) for a in (0, 1)]
                 + [(h, a, HALF, 4, mods, MODS + SH2) for a in (0, 1)]
                 + [(h, a, HALF, None, None, None) for a in (0, 1)])
        N_X, N_CTX, N_F0, N_S, N_F1, N_END = 0, 2, 3, 5, 7, 9

        def cols(n):
            a, half, w, *_ = NORMS[n]
            return slice(half * HALF, half * HALF + w)

        PAR = dict(n1=0, n2=16, nf=32, conv_w=40, conv_b=56, br=60, bi=68, lam=76, short_w=84, c=108)

        def window(b):
            lo = [min(max(r - 4, 0), SEQ // GRID - 8) for r in (2 * b, 2 * b + 1)]
            return lo[0] * GRID, lo[0] != lo[1]

        V_TILES = TT + CT

        def used_p(i, j):
            return s_proj, 10 * i + (3, 5, 8, 10)[j]

        def used_o(j):
            return s_out, j + 1

        def used_f(layer, i, j):
            if j < 4:
                return s_gu, 8 * ROUNDS * layer + 8 * i + 5 + j
            return s_out, OUT_F[layer] + 16 * i + 16

        def used_s(i, j):
            return (s_sg, 6 * i + (3, 4, 6)[j]) if j < 3 else (s_out, OUT_S + 16 * i + 16)

        OUT_F = (2 * FT, 2 * FT + 16 * (ROUNDS + FT))
        OUT_S = 2 * FT + 16 * ROUNDS

        block = es.enter_context(nc.Block())

        @block.sync
        def _(sp):
            w_in, w_out = t["e_w_in"][0], t["e_w_out"][0]
            AW = LT * P

            def load_unit(u, parity, src):
                if not isinstance(u, int) or u >= 2:
                    sp.wait_ge(s_split, u - 1)
                    if not isinstance(u, int):
                        alone(sp)
                dst = raw[:, parity, :]
                if len(src.shape) == 3:
                    dst = dst.rearrange("p (k m) -> p k m", k=src.shape[1])
                sp.dma_start(dst, src).then_inc(s_raw[parity], 16)

            def column_unit(w, col):
                return w[:, bass.ds(col, P)].rearrange("(k p) m -> p k m", p=P)

            r = 0
            for src in (t["norm1_g"].rearrange("l (r c) -> (l r) c", c=P),
                        t["norm2_g"].rearrange("l (r c) -> (l r) c", c=P),
                        t["final_g"].rearrange("(r c) -> r c", c=P),
                        t["e_conv_w"][0].rearrange("j (r c) -> (j r) c", c=P),
                        t["e_conv_b"][0].rearrange("(r c) -> r c", c=P),
                        t["e_lru_br"][0].rearrange("d (r c) -> (d r) c", c=P),
                        t["e_lru_bi"][0].rearrange("d (r c) -> (d r) c", c=P),
                        t["e_lru_lam"][0].rearrange("d (r c) -> (d r) c", c=P),
                        t["o_conv_w"][0].rearrange("j (r c) -> (j r) c", c=P),
                        t["c"][0].rearrange("(r c) -> r c", c=P),
                        t["c_ctx"].rearrange("(r c) -> r c", c=P)):
                sp.dma_start(par_rows[r:r + src.shape[0], :], src).then_inc(s_par, 16)
                r += src.shape[0]
            assert r == 124
            sp.dma_start(b_rows[:], t["mod_b"].rearrange("l (r c) -> (l r) c", c=P)).then_inc(s_par, 16)

            order_p = (3 * AW, 0, AW, 4 * AW)
            for j in range(2):
                load_unit(j, j, column_unit(w_in, order_p[j]))
            sp.wait_ge(s_zero, 1)
            sp.dma_start(rpb_pad[0:1, 0:PAD], zero_row[:]).then_inc(s_rpb, 16)
            sp.dma_start(rpb_pad[0:1, PAD + RPB:], zero_row[:]).then_inc(s_rpb, 16)
            sp.dma_start(rpb_pad[0:1, PAD:PAD + RPB], t["e_rpb"].rearrange("a h r c -> a (h r c)")).then_inc(s_rpb, 16)

            sp.wait_ge(s_rpb, 48)
            for head in range(HEADS):
                src = bass.AP(tensor=rpb_pad.tensor, offset=PAD + head * NR * NC + NC // 2, ap=[[NC, NR], [-1, GRID], [1, GRID]])
                sp.dma_start(rpb_wide[head], src).then_inc(s_wide, 16)

            mod_w = t["mod_w"].rearrange("l (k p) (w n) -> l w k p n", p=P, n=UNIT)
            for layer in range(2):
                with sp.Fori(0, MODS) as c:
                    for k in range(FT):
                        sp.wait_ge(s_modmm, c * FT + (layer * MODS * FT + k + 1))
                        alone(sp)
                        sp.dma_start(mod_ring[:, k % 4, :], mod_w[layer, bass.ds(c, 1), k].rearrange("a p n -> p (a n)")
                                     ).then_inc(s_mod[k % 4], 16)
            for j in range(2, 4):
                load_unit(j, j % 2, column_unit(w_in, order_p[j]))

            def load_gates(i):
                for d in range(2):
                    for g, w in enumerate((t["e_lru_wr"], t["e_lru_wi"])):
                        for a in range(2):
                            sp.dma_start(gate_w[64 * a:64 * a + 64, 2 * d + g, 64 * a:64 * a + 64],
                                         w[0, d, bass.ds(2 * i + a, 1)].rearrange("a p n -> p (a n)")).then_inc(s_gw, 16)

            sp.wait_ge(s_gwz, 1)
            load_gates(0)
            with sp.Fori(1, LT) as i:
                for j in range(4):
                    load_unit(4 * i + j, j % 2, column_unit(w_in, i * P + order_p[j]))
                sp.wait_ge(s_gate, i * 12)
                alone(sp)
                load_gates(i)
            wv = w_in.rearrange("(k p) n -> p k n", p=P)
            for j in range(4):
                load_unit(U_V + j, j % 2, wv[:, 2 * j:2 * j + 2, 2 * AW:3 * AW])
            for j in range(6):
                load_unit(U_O + j, j % 2, column_unit(w_out, (j % FT) * P))

            def load_bias(pair):
                for hh in range(2):
                    for a in range(2):
                        src = rpb_wide[2 * pair + hh, 1 - a:15 - a].rearrange("j c k -> c j k")
                        sp.dma_start(bias_t[pair % 2][64 * a:64 * a + 64, hh, 0:EDGE]
                                     .rearrange("p (j c) -> p j c", c=GRID), src).then_inc(s_braw[pair % 2], 16)

            def load_pair(pair):
                sp.dma_start(q_att[:, pair % 2, :], q_spill[pair]).then_inc(s_kq[pair % 2], 16)
                sp.dma_start(k_att[:, pair % 2, :], k_spill[pair]).then_inc(s_kq[pair % 2], 16)

            sp.wait_ge(s_wide, 16 * HEADS)
            sp.wait_ge(s_projev, 5 + 10 * LT)
            sp.wait_ge(s_lru, 1 + LT)
            sp.wait_ge(s_qk, 16 + 80 * LT)
            sp.wait_ge(s_rfree, 1 + LT)
            load_bias(0)
            load_bias(1)
            for j in range(2):
                sp.dma_start(r_in[:, j, :], r_spill[j]).then_inc(s_rin[j], 16)
            sp.wait_ge(s_v, V_TILES)
            load_pair(0)
            load_pair(1)
            for j in range(2, LT):
                sp.wait_ge(s_yll, j - 1)
                sp.dma_start(r_in[:, j % 2, :], r_spill[j]).then_inc(s_rin[j % 2], 16)
            steps_per_pair = 2 * TT
            for pair in (2, 3):
                sp.wait_ge(s_exp, 2 + steps_per_pair * (pair - 1))
                load_pair(pair)
                load_bias(pair)
            sp.wait_ge(s_yl, 4 + TT * LT)
            sp.wait_ge(s_yll, LT)
            for f in range(FT):
                sp.dma_start(h[:, f, :], h_spill[:, f, :]).then_inc(s_reload, 16)
            for j in range(6, 2 * FT):
                load_unit(U_O + j, j % 2, column_unit(w_out, (j % FT) * P))

            def ffn_loads(layer, u0):
                gu, down = t["ffn_w_gu"][layer], t["ffn_w_down"][layer]
                with sp.Fori(0, ROUNDS) as i:
                    for j, off in enumerate((0, HID, P, HID + P)):
                        load_unit(6 * i + (u0 + j), j % 2, column_unit(gu, i * (2 * P) + off))
                    for j in range(2):
                        load_unit(6 * i + (u0 + 4 + j), j % 2, down[bass.ds(i * (2 * P) + j * P, P), :])

            ffn_loads(0, U_F0)
            with sp.Fori(0, FT) as i:
                for j, off in enumerate((D, 2 * D, 0)):
                    load_unit(4 * i + (U_S + j), j % 2, column_unit(t["o_w_in"][0], i * P + off))
                load_unit(4 * i + (U_S + 3), 1, t["o_w_out"][0][bass.ds(i * P, P), :])
            ffn_loads(1, U_F1)

            for tt in range(TT):
                sp.wait_ge(s_fra, tt + 1)
                sp.wait_ge(s_frd, tt + 1)
                sp.dma_start(out[0, tt * P:(tt + 1) * P, :], fin_rows[:, tt % 2, :]).then_inc(s_store[tt % 2], 16)
            for tt in range(2):
                sp.wait_ge(s_store[tt], 16 * TT // 2)

        @block.gpsimd
        def _(pool):
            steps = Steps(pool, s_bstep)
            steps.run(nc.gpsimd.memset(ident[:], 0.0))
            nc.gpsimd.affine_select(out=ident[:], in_=ident[:], compare_op=ALU.not_equal, fill=1.0, base=0,
                                    pattern=[[-1, P]], channel_multiplier=1).then_inc(s_ident, 1)
            nc.gpsimd.memset(eps_t[:], EPS).then_inc(s_ident, 1)
            nc.gpsimd.memset(ones[:], 1.0).then_inc(s_ident, 1)
            nc.gpsimd.memset(zero_row[:], 0.0).then_inc(s_zero, 1)
            pool.sem_inc(s_rfree, 1)
            pool.wait_ge(s_ident, 3)

            def split(u, slot, parity, free=None):
                w_hi, w_lo = w_slot(slot)
                pool.wait_ge(s_raw[parity], 8 * u + (16 - 8 * parity))
                if free is not None:
                    pool.wait_ge(*free)
                nc.gpsimd.tensor_tensor(w_hi, raw[:, parity, :], ones[:, 0:1].to_broadcast([P, UNIT]),
                                        ALU.mult).then_inc(s_hi, 1)
                pool.wait_ge(s_hi, u + 1)
                nc.gpsimd.tensor_tensor(w_lo, raw[:, parity, :], w_hi, ALU.subtract).then_inc(s_split, 1)

            def store_lru(i):
                pool.wait_ge(s_lru, i + 2)
                nc.gpsimd.dma_start(r_spill[i], lru_q[:, 0, 0:SEQ]).then_inc(s_rst, 16)
                pool.wait_ge(s_rst, 16 * (i + 1))
                pool.sem_inc(s_rfree, 1)

            for j in range(4):
                split(j, j, j % 2)
            pool.wait_ge(s_spill, 16)
            pool.wait_ge(s_norm, 8 * (N_CTX + 1))
            nc.gpsimd.memset(gate_w[:], 0.0).then_inc(s_gwz, 1)
            for lo, w in ((0, 2), (CTX + 2, 3), (KEYS + 5, 1)):
                nc.gpsimd.memset(x_pad[:, lo:lo + w], 0.0).then_inc(s_pad, 1)
            for i in range(1, LT):
                for j in range(4):
                    split(4 * i + j, j, j % 2, used_p(i - 1, j))
                    if j == 1 and i >= 2:
                        store_lru(i - 2)
            for j in range(4):
                split(U_V + j, j, j % 2, used_p(LT - 1, j))
                if j == 1:
                    store_lru(LT - 2)
            store_lru(LT - 1)
            for j in range(4):
                split(U_O + j, j, j % 2, (s_v, V_TILES))

            def build_bias(pair):
                pool.wait_ge(s_braw[pair % 2], 64 * (pair // 2 + 1))
                tab = bias_t[pair % 2]
                for hh in range(2):
                    edge = tab[:, hh, 0:EDGE].rearrange("p (j c) -> p j c", c=GRID)
                    mid = tab[:, hh, EDGE:EDGE + MID].rearrange("p (j c) -> p j c", c=GRID)
                    steps.run(nc.gpsimd.tensor_scalar(edge, edge, -1.0, None, ALU.mult))
                    for r in (0, 64):
                        steps.run(nc.gpsimd.affine_select(
                            out=edge[r:r + 64, :, 0:48], in_=edge[r:r + 64, :, 0:48], compare_op=ALU.is_ge,
                            fill=FAR, base=8, pattern=[[0, 14], [1, 48]], channel_multiplier=-1))
                        steps.run(nc.gpsimd.affine_select(
                            out=edge[r:r + 64, :, 16:64], in_=edge[r:r + 64, :, 16:64], compare_op=ALU.is_ge,
                            fill=FAR, base=7 - 16, pattern=[[0, 14], [-1, 48]], channel_multiplier=1))
                    steps.run(nc.gpsimd.tensor_copy(mid, edge[:, 2:11, :]))
                    steps.run(nc.gpsimd.memset(mid[0:64, 8, :], FAR))
                    nc.gpsimd.memset(mid[64:P, 0, :], FAR).then_inc(s_bias, 1)
                    pool.wait_ge(s_bias, 2 * pair + hh + 1)

            for pair in range(LT):
                build_bias(pair)
            for j in range(4, 2 * FT):
                split(U_O + j, j % 4, j % 2, used_o(j - 4))
            for j in range(6):
                split(U_F0 + j, j, j % 2, used_o(12 + j) if j < 4 else None)
            with pool.Fori(1, ROUNDS) as i:
                for j in range(6):
                    split(6 * i + (U_F0 + j), j, j % 2, used_f(0, i - 1, j))
            for j in range(4):
                split(U_S + j, j, j % 2, used_f(0, ROUNDS - 1, j))
            with pool.Fori(1, FT) as i:
                for j in range(4):
                    split(4 * i + (U_S + j), j, j % 2, used_s(i - 1, j))
            for j in range(6):
                split(U_F1 + j, j, j % 2, used_s(FT - 1, j) if j < 4 else used_f(0, ROUNDS - 1, j))
            with pool.Fori(1, ROUNDS) as i:
                for j in range(6):
                    split(6 * i + (U_F1 + j), j, j % 2, used_f(1, i - 1, j))

        @block.tensor
        def _(pe):
            def product(dst, w, x_hi, x_lo, first, last):
                w_hi, w_lo = w
                pe.matmul(dst, w_hi, x_hi, start=first, stop=False)
                pe.matmul(dst, w_lo, x_hi, start=False, stop=False)
                return pe.matmul(dst, w_hi, x_lo, start=False, stop=last)

            def columns(dst, slot, a_hi, a_lo, sl, norm=None):
                w_hi, w_lo = w_slot(slot)
                for k in range(FT):
                    if norm is not None:
                        pe.wait_ge(s_norm, 8 * norm + k + 1)
                    w = (w_hi[:, k * P:(k + 1) * P], w_lo[:, k * P:(k + 1) * P])
                    mm = product(dst, w, a_hi[:, k, sl], a_lo[:, k, sl], k == 0, k == FT - 1)
                return mm

            def norm_sum(n):
                pe.wait_ge(s_sum, 8 * (n + 1))
                for j in range(NORMS[n][2] // P):
                    mm = pe.matmul(bank[:, 7, j:j + 1], sumsq[:, j * P:(j + 1) * P], ones[:, 0:1], start=True, stop=True)
                mm.then_inc(s_ss, 1)

            def norm_spread(n):
                pe.wait_ge(s_rstd, n + 1)
                for j in range(NORMS[n][2] // P):
                    mm = pe.matmul(bank[:, 6, j * P:(j + 1) * P], ones[:, :], diag[:, j, :], start=True, stop=True)
                mm.then_inc(s_bc, 1)

            def out_groups(n0, group, norm=None):
                for idx in range(16):
                    half, m = divmod(idx, FT)
                    pe.wait_ge(s_hup, n0 + idx + 1)
                    group(half, m, bank[:, 4 + m % 2, :]).then_inc(s_out, 1)
                    if norm is not None and idx == 9:
                        norm_sum(norm)
                    if norm is not None and idx == 11:
                        norm_spread(norm)
                if norm is not None:
                    norm_sum(norm + 1)
                    norm_spread(norm + 1)

            pe.sem_inc(s_modmm, 4)
            pe.wait_ge(s_ident, 3)
            pe.wait_ge(s_par, 16 * 12)
            pe.transpose(bank[:, 0, 0:124], par_rows[:], ident[0:124, 0:124])
            pe.transpose(bank[:, 0, 128:224], b_rows[:], ident[0:96, 0:96]).then_inc(s_par_t, 1)
            pe.wait_ge(s_param, 2)
            for tt in range(TT + CT):
                pe.wait_ge(s_x[tt % 2], 16 * (tt // 2 + 1))
                if tt >= 2:
                    pe.wait_ge(s_xpa, tt - 1)
                    pe.wait_ge(s_xpd, tt - 1)
                for f in range(FT):
                    b = 2 * (tt % 2) + f // 4
                    mm = pe.transpose(bank[:, b, (f % 4) * P:(f % 4 + 1) * P], x_in[:, tt % 2, f * P:(f + 1) * P], ident[:])
                    if f % 4 == 3:
                        mm.then_inc(s_turn, 1)

            pe.wait_ge(s_cond, 2)
            pe.wait_ge(s_xpa, TT + CT)
            pe.wait_ge(s_xpd, TT + CT)
            with pe.Fori(0, 2 * MODS) as c:
                for k in range(FT):
                    pe.wait_ge(s_mod[k % 4], c * 32 + 16 * (k // 4 + 1))
                    for a in range(2):
                        mm = pe.matmul(bank[0:2, a, :], cond[:, k, :], mod_ring[:, k % 4, a * HALF:(a + 1) * HALF],
                                       start=(k == 0), stop=(k == FT - 1))
                    mm.then_inc(s_modmm, 1)
                pe.wait_ge(s_modrow, 2 * c + 2)
                pe.wait_ge(s_modset, 2 * c + 2)
                alone(pe)
                for m in range(FT):
                    mm = pe.transpose(bank[:, 2, 2 * m:2 * m + 2], mod_row[:, m * P:(m + 1) * P], ident[0:2, 0:2])
                mm.then_inc(s_modt, 1)

            for n in (0, 1, 2):
                norm_sum(n)
                norm_spread(n)

            pe.wait_ge(s_modset, 2 + 2 * 2 * MODS)
            GROUPS = ((0, 0), (0, 1), (0, 2), (1, 0), (1, 1), (2, 0), (2, 1), (2, 2), (3, 0), (3, 1))
            with pe.Fori(0, LT) as i:
                for g, (unit, part) in enumerate(GROUPS):
                    if part == 0:
                        pe.wait_ge(s_split, 4 * i + unit + 1)
                    pe.wait_ge(s_projev, 10 * i + g + 1)
                    if part == 2:
                        mm = columns(bank[:, g % 5, 0:CTX], unit, ctx_hi, ctx_lo, slice(0, CTX), N_CTX)
                    else:
                        mm = columns(bank[:, g % 5, :], unit, act_hi, act_lo, slice(part * HALF, (part + 1) * HALF), part)
                    mm.then_inc(s_proj, 1)
                pe.wait_ge(s_conv, i + 2)
                pe.wait_ge(s_gw, i * 128 + 128)
                for g in range(12):
                    lo = (g % 3) * HALF
                    w = min(HALF, KEYS - lo)
                    pe.wait_ge(s_gatev, 12 * i + g + 1)
                    pe.matmul(bank[:, 5 + g % 3, 0:w], gate_w[:, g // 3, :], x_conv[:, lo:lo + w],
                              start=True, stop=True).then_inc(s_gate, 1)

            pe.wait_ge(s_projev, 5 + 10 * LT)
            for tt in range(V_TILES):
                if tt == 0:
                    pe.wait_ge(s_split, U_V + 4)
                if tt >= 4:
                    pe.wait_ge(s_vev, tt - 3)
                a_hi, a_lo, c0 = (act_hi, act_lo, tt * P) if tt < TT else (ctx_hi, ctx_lo, (tt - TT) * P)
                for k in range(FT):
                    w_hi, w_lo = w_slot(k // 2)
                    sl = slice((k % 2) * HALF, (k % 2 + 1) * HALF)
                    mm = product(bank[:, tt % 4, :], (a_hi[:, k, c0:c0 + P], a_lo[:, k, c0:c0 + P]),
                                 w_hi[:, sl], w_lo[:, sl], k == 0, k == FT - 1)
                mm.then_inc(s_v, 1)

            pe.wait_ge(s_vev, V_TILES)
            pe.wait_ge(s_gatev, 3 + 12 * LT)
            N = 4 * TT

            def scores(i, s):
                slot, b, hh = s // (2 * TT), (s // 2) % TT, s % 2
                k0, wide = window(b)
                if s % (2 * TT) == 0:
                    pe.wait_ge(s_kq[slot], 32 * i + 32)
                pe.wait_ge(s_exp, N * i + s + 1)
                o = 2 * (s % 2) * HALF
                hd = slice(64 * hh, 64 * hh + 64)
                q = q_att[hd, slot, b * P:(b + 1) * P]
                pe.matmul(bank_f[:, o:o + HALF], q, k_att[hd, slot, CTX + k0:CTX + k0 + HALF], start=True, stop=True)
                if wide:
                    pe.matmul(bank_f[:, o + HALF:o + MID], q, k_att[hd, slot, CTX + k0 + HALF:CTX + k0 + MID], start=True, stop=True)
                pe.matmul(bank_f[:, o + MID:o + WIDE], q, k_att[hd, slot, 0:CTX], start=True, stop=True).then_inc(s_sc, 1)

            def turn_probs(i, s):
                wide = window((s // 2) % TT)[1]
                pe.wait_ge(s_exp, N * i + s + 3)
                pe.wait_ge(s_pta, N * i + s + 1)
                pe.wait_ge(s_ptd, N * i + s + 1)
                for c in range(4):
                    pe.transpose(bank_f[:, 4 * HALF + c * P:4 * HALF + (c + 1) * P], probs[:, s % 2, c * P:(c + 1) * P], ident[:])
                if wide:
                    pe.transpose(bank_f[0:64, 5 * HALF + 2 * P:5 * HALF + 3 * P], probs[:, s % 2, HALF:MID], ident[:])
                for c in range(2):
                    mm = pe.transpose(bank_f[:, 5 * HALF + c * P:5 * HALF + (c + 1) * P],
                                      probs[:, s % 2, MID + c * P:MID + (c + 1) * P], ident[:])
                mm.then_inc(s_pt, 1)

            def values(i, s):
                slot, b, hh = s // (2 * TT), (s // 2) % TT, s % 2
                k0, wide = window(b)
                pe.wait_ge(s_pta, N * i + s + 2)
                pe.wait_ge(s_ptd, N * i + s + 2)
                pe.wait_ge(s_on, N * i + s + 2)
                col = i * (2 * P) + (slot * P + hh * 64)
                chunks = [(c, k0 // P + c, P) for c in range(4)] + [(4 + c, TT + c, P) for c in range(CT)]
                if wide:
                    chunks.append((6, k0 // P + 4, 64))
                for n, (c, tile, rows) in enumerate(chunks):
                    mm = pe.matmul(bank[:, 6, 64 * (s % 2):64 * (s % 2) + 64], probs_t[0:rows, s % 2, c, :],
                                   v_tok[0:rows, tile, bass.ds(col, 64)], start=(n == 0), stop=(n == len(chunks) - 1))
                mm.then_inc(s_pv, 1)

            def turn_out(i, s):
                b = (s // 2) % TT
                pe.wait_ge(s_on, N * i + s + 3)
                pe.wait_ge(s_yl, (N // 2) * i + s // 2 + 4)
                q = (s // 2) % 4
                pe.transpose(bank[:, 7, q * P:(q + 1) * P], o_tok[:, b % 2, :], ident[:]).then_inc(s_yt, 1)

            with pe.Fori(0, LT // 2) as i:
                for s in range(N + 3):
                    if s < N:
                        scores(i, s)
                    if 0 <= s - 1 < N:
                        turn_probs(i, s - 1)
                    if 0 <= s - 2 < N:
                        values(i, s - 2)
                    if 0 <= s - 3 < N and (s - 3) % 2:
                        turn_out(i, s - 3)

            pe.wait_ge(s_yll, LT)
            pe.wait_ge(s_yl, 4 + TT * LT)

            def project_out(half, m, dst):
                pe.wait_ge(s_split, U_O + half * FT + m + 1)
                return columns(dst, m % 4, act_hi, act_lo, slice(half * HALF, (half + 1) * HALF))

            out_groups(0, project_out, N_F0)

            def ffn_round(layer, i, u0, norm_in, norm_out=None):
                q0 = 4 * ROUNDS * layer
                for q in range(4):
                    half, tile = divmod(q, 2)
                    pe.wait_ge(s_hidf, 4 * i + (q0 + q + 1))
                    for a in range(2):
                        if half == 0:
                            pe.wait_ge(s_split, 6 * i + (u0 + 2 * tile + a + 1))
                        columns(bank[:, 2 * tile + a, :], 2 * tile + a, act_hi, act_lo,
                                slice(half * HALF, (half + 1) * HALF), norm_in + half).then_inc(s_gu, 1)

                def down(half, m, dst):
                    if m == 0:
                        pe.wait_ge(s_split, 6 * i + (u0 + 6))
                        pe.wait_ge(s_hid, 4 * i + (q0 + 2 * half + 2))
                    sl = slice(half * HALF, (half + 1) * HALF)
                    for k in range(2):
                        w_hi, w_lo = w_slot(4 + k)
                        w = (w_hi[:, m * P:(m + 1) * P], w_lo[:, m * P:(m + 1) * P])
                        mm = product(dst, w, hid_hi[:, k, sl], hid_lo[:, k, sl], k == 0, k == 1)
                    return mm

                out_groups(16 * i + OUT_F[layer], down, norm_out)

            with pe.Fori(0, ROUNDS - 1) as i:
                ffn_round(0, i, U_F0, N_F0)
            ffn_round(0, ROUNDS - 1, U_F0, N_F0, N_S)

            def short_round(i, norm_out=None):
                for g, (unit, half) in enumerate(((0, 0), (1, 0), (0, 1), (1, 1), (2, 0), (2, 1))):
                    if half == 0:
                        pe.wait_ge(s_split, 4 * i + (U_S + unit + 1))
                    if g < 2:
                        pe.wait_ge(s_zf, 2 * i + g + 1)
                    elif g == 4:
                        pe.wait_ge(s_cg, 2 * i + 1)
                    elif g == 5:
                        pe.wait_ge(s_t, 2 * i + 1)
                    columns(bank[:, g % 4, :], unit, act_hi, act_lo, slice(half * HALF, (half + 1) * HALF),
                            N_S + half).then_inc(s_sg, 1)

                def down(half, m, dst):
                    if m == 0:
                        pe.wait_ge(s_split, 4 * i + (U_S + 4))
                        pe.wait_ge(s_z, 2 * i + half + 1)
                    w_hi, w_lo = w_slot(3)
                    w = (w_hi[:, m * P:(m + 1) * P], w_lo[:, m * P:(m + 1) * P])
                    sl = slice(half * HALF, (half + 1) * HALF)
                    return product(dst, w, z_hi[:, sl], z_lo[:, sl], True, True)

                out_groups(16 * i + OUT_S, down, norm_out)

            pe.wait_ge(s_hidf, 2 + 4 * ROUNDS)
            with pe.Fori(0, FT - 1) as i:
                short_round(i)
            short_round(FT - 1, N_F1)

            pe.wait_ge(s_zf, 2 + 2 * FT)
            with pe.Fori(0, ROUNDS - 1) as i:
                ffn_round(1, i, U_F1, N_F1)
            ffn_round(1, ROUNDS - 1, U_F1, N_F1, N_END)

            pe.wait_ge(s_hidf, 2 + 8 * ROUNDS)
            for tt in range(TT):
                if tt % 4 == 0:
                    pe.wait_ge(s_fin, FT * (tt // 4 + 1))
                if tt >= 2:
                    pe.wait_ge(s_fra, tt - 1)
                    pe.wait_ge(s_frd, tt - 1)
                for f in range(FT):
                    b = 2 * (tt % 2) + f // 4
                    mm = pe.transpose(bank[:, b, (f % 4) * P:(f % 4 + 1) * P], fin[:, f, tt * P:(tt + 1) * P], ident[:])
                    if f % 4 == 3:
                        mm.then_inc(s_fturn, 1)

        @block.scalar
        def _(act):
            def square(n, f, ready=None):
                src, half, w, *_ = NORMS[n]
                if ready is not None:
                    act.wait_ge(*ready)
                if 8 * n + f >= 2:
                    act.wait_ge(s_sum, 8 * n + f - 1)
                nc.scalar.activation(sq[:, f % 2, 0:w], src[:, f, cols(n)], ACT.Square).then_inc(s_sq, 1)

            def rms(n):
                act.wait_ge(s_ss, n + 1)
                nc.scalar.activation(std[:, 0, 0:NORMS[n][2] // P], bank[:, 7, 0:NORMS[n][2] // P], ACT.Sqrt,
                                     bias=eps_t[:, 0:1], scale=1.0 / D).then_inc(s_sqrt, 1)

            def modulate(n, f):
                _, half, w, gain, shift, which = NORMS[n]
                act.wait_ge(s_scal, 8 * n + f + 1)
                if gain is None:
                    nc.scalar.activation(fin[:, f, cols(n)], scaled[:, f % 2, 0:w], ACT.Identity,
                                         scale=par[:, PAR["nf"] + f:PAR["nf"] + f + 1]).then_inc(s_fin, 1)
                    return
                if 8 * n + f >= 2:
                    act.wait_ge(s_norm, 8 * n + f - 1)
                g, b = gains[:, gain, f:f + 1], shift[:, which, f:f + 1]
                nc.scalar.activation(normed[:, f % 2, 0:w], scaled[:, f % 2, 0:w], ACT.Identity, bias=b, scale=g).then_inc(s_nf, 1)
                dst = (ctx_hi if n == N_CTX else act_hi)[:, f, cols(n)]
                nc.scalar.activation(dst, scaled[:, f % 2, 0:w], ACT.Identity, bias=b, scale=g).then_inc(s_nhi, 1)

            def norm_pair(n, n0):
                for f in range(FT):
                    square(n, f, (s_hup, n0 + f + 3))
                rms(n)
                for f in range(2):
                    square(n + 1, f, (s_hup, n0 + FT + f + 3))
                for f in range(FT):
                    modulate(n, f)
                    if f + 2 < FT:
                        square(n + 1, f + 2, (s_hup, n0 + FT + f + 5))
                rms(n + 1)
                for f in range(FT):
                    modulate(n + 1, f)

            act.sem_inc(s_projev, 5)
            act.sem_inc(s_gatev, 3)
            act.sem_inc(s_exp, 2)
            act.sem_inc(s_pta, 1)
            act.sem_inc(s_qk, 16)

            def load_x(tt):
                src = x[0, tt * P:(tt + 1) * P, :] if tt < TT else context[0, (tt - TT) * P:(tt - TT + 1) * P, :]
                act.dma_start(x_in[:, tt % 2, :], src).then_inc(s_x[tt % 2], 16)

            load_x(0)
            load_x(1)
            act.wait_ge(s_param, 1)
            for j in range(2):
                nc.scalar.activation(cond[:, :, j], par[:, PAR["c"] + j * FT:PAR["c"] + (j + 1) * FT], ACT.Silu).then_inc(s_cond, 1)
            for tt in range(TT + CT):
                dst = h[:, 0:4, tt * P:(tt + 1) * P] if tt < TT else ctx_t[:, 0:4, (tt - TT) * P:(tt - TT + 1) * P]
                act.wait_ge(s_turn, 2 * tt + 1)
                nc.scalar.copy(dst, bank[:, 2 * (tt % 2), :].rearrange("p (f c) -> p f c", c=P)).then_inc(s_xpa, 1)
                if tt + 2 < TT + CT:
                    act.wait_ge(s_turn, 2 * tt + 2)
                    load_x(tt + 2)
            act.wait_ge(s_xpa, TT + CT)
            act.wait_ge(s_xpd, TT + CT)
            act.dma_start(h_spill, h[:, :, :]).then_inc(s_spill, 16)

            act.wait_ge(s_const, 1)
            nc.scalar.activation(sp_t[:, 1, :], sp_t[:, 0, :], ACT.Exp, scale=-1.0).then_inc(s_act, 1)

            with act.Fori(0, 2 * MODS) as c:
                act.wait_ge(s_modmm, c * FT + (4 + FT))
                for a in range(2):
                    nc.scalar.copy(mod_row[:, a * HALF:(a + 1) * HALF], bank[0:2, a, :]).then_inc(s_modrow, 1)

            act.wait_ge(s_rpb, 48)
            for n in (0, 1, 2):
                for f in range(FT):
                    square(n, f)
                rms(n)
                if n == 0:
                    act.wait_ge(s_const, 3)
                for f in range(FT):
                    modulate(n, f)

            act.wait_ge(s_spill, 16)
            act.wait_ge(s_norm, 8 * (N_CTX + 1))
            with act.Fori(0, LT) as i:
                def out_of(g):
                    act.wait_ge(s_proj, 10 * i + g + 1)

                act.wait_ge(s_conv, i + 1)
                for g, (dst, w) in enumerate(((CTX + 5, HALF), (CTX + 5 + HALF, HALF), (2, CTX))):
                    out_of(g)
                    nc.scalar.copy(x_pad[:, dst:dst + w], bank[:, g % 5, 0:w]).then_inc(s_projev, 1)
                act.wait_ge(s_qk, 80 * i + 16)
                for g in range(3, 8):
                    out_of(g)
                    w = CTX if g == 7 else HALF
                    nc.scalar.activation(qk_out[:, g - 3, 0:w], bank[:, g % 5, 0:w], ACT.Copy,
                                         scale=-(64 ** -0.5) if g < 5 else 1.0).then_inc(s_projev, 1)
                    act.wait_ge(s_projev, 10 * i + (5 + g + 1))
                    alone(act)
                    dst = (q_spill[bass.ds(i, 1), :, (g - 3) * HALF:(g - 2) * HALF] if g < 5 else
                           k_spill[bass.ds(i, 1), :, 0:CTX] if g == 7 else
                           k_spill[bass.ds(i, 1), :, CTX + (g - 5) * HALF:CTX + (g - 4) * HALF])
                    act.dma_start(dst.rearrange("a p n -> p (a n)"), qk_out[:, g - 3, 0:w]).then_inc(s_qk, 16)
                act.wait_ge(s_lru, i + 1)
                for g in (8, 9):
                    out_of(g)
                    nc.scalar.activation(g_gelu[:, (g - 8) * HALF:(g - 7) * HALF], bank[:, g % 5, :],
                                         ACT.Gelu_apprx_tanh).then_inc(s_projev, 1)
                for g in range(12):
                    m, lo = g // 3, (g % 3) * HALF
                    w = min(HALF, KEYS - lo)
                    act.wait_ge(s_gate, 12 * i + g + 1)
                    alone(act)
                    nc.scalar.activation((lru_i if m % 2 else lru_r)[:, m // 2, lo:lo + w], bank[:, 5 + g % 3, 0:w], ACT.Tanh,
                                         bias=half_b[:, bass.ds(i + (m % 2 * 8 + m // 2 * LT), 1)], scale=0.5).then_inc(s_gatev, 1)
                act.wait_ge(s_gatev, 12 * i + 15)
                alone(act)
                for d in range(2):
                    sp = sp2[:, bass.ds(i + d * LT, 1)]
                    nc.scalar.activation(lru_r[:, d, :], lru_r[:, d, :], ACT.Tanh, bias=sp, scale=sp).then_inc(s_s, 1)
                act.wait_ge(s_s, 2 * i + 2)
                act.wait_ge(s_rfree, i + 1)
                for d in range(2):
                    nc.scalar.activation(lru_q[:, d, :], lru_r[:, d, :], ACT.Sqrt).then_inc(s_rs, 1)

            for tt in range(V_TILES):
                act.wait_ge(s_v, tt + 1)
                nc.scalar.copy(v_tok[:, tt, :], bank[:, tt % 4, :]).then_inc(s_vev, 1)

            for j in range(LT):
                act.wait_ge(s_rin[j % 2], 16 * (j // 2 + 1))
                nc.scalar.copy(act_hi[:, LT + j, :], r_in[:, j % 2, :]).then_inc(s_ylh, 1)

            N = 4 * TT

            def exps(i, s):
                wide = window((s // 2) % TT)[1]
                w = MID if wide else HALF
                o = 2 * (s % 2) * HALF
                st = stat[:, s % 4, :]
                act.wait_ge(s_min, N * i + s + 1)
                nc.scalar.activation(probs[:, s % 2, 0:w], probs[:, s % 2, 0:w], ACT.Exp, bias=st[:, 1:2], scale=-1.0,
                                     accum_out=st[:, 2:3])
                nc.scalar.activation(probs[:, s % 2, MID:WIDE], bank_f[:, o + MID:o + WIDE], ACT.Exp, bias=st[:, 1:2],
                                     scale=-1.0, accum_out=st[:, 3:4]).then_inc(s_exp, 1)

            def window_turned(i, s):
                act.wait_ge(s_pt, N * i + s + 1)
                nc.scalar.copy(probs_t[:, s % 2, 0:4, :].rearrange("p c n -> p (c n)"), bank[:, 4, :]).then_inc(s_pta, 1)

            def y_high(i, s):
                b = (s // 2) % TT
                act.wait_ge(s_yt, (N // 2) * i + s // 2 + 1)
                alone(act)
                q = (s // 2) % 4
                nc.scalar.copy(act_hi[:, bass.ds(2 * i + s // (2 * TT), 1), b * P:(b + 1) * P].rearrange("p a n -> p (a n)"),
                               bank[:, 7, q * P:(q + 1) * P]).then_inc(s_yh, 1)

            with act.Fori(0, LT // 2) as i:
                for s in range(N + 3):
                    if s < N:
                        exps(i, s)
                    if 0 <= s - 1 < N:
                        window_turned(i, s - 1)
                    if 0 <= s - 3 < N and (s - 3) % 2:
                        y_high(i, s - 3)

            norm_pair(N_F0, 0)

            def ffn_round(layer, i):
                q0 = 4 * ROUNDS * layer
                for q in range(4):
                    half, tile = divmod(q, 2)
                    act.wait_ge(s_gu, 8 * i + (2 * q0 + 2 * q + 1))
                    act.wait_ge(s_hidf, 4 * i + (q0 + q + 1))
                    nc.scalar.activation(silu_g[:, q % 2, :], bank[:, 2 * tile, :], ACT.Silu).then_inc(s_silu, 1)
                    act.wait_ge(s_hidf, 4 * i + (q0 + q + 3))
                    nc.scalar.copy(hid_hi[:, tile, half * HALF:(half + 1) * HALF], hid_f[:, q % 2, :]).then_inc(s_hidh, 1)

            with act.Fori(0, ROUNDS - 1) as i:
                ffn_round(0, i)
            ffn_round(0, ROUNDS - 1)
            norm_pair(N_S, OUT_F[0] + 16 * (ROUNDS - 1))

            def short_round(i):
                for half in range(2):
                    act.wait_ge(s_sg, 6 * i + (2 * half + 1))
                    nc.scalar.copy(cg_sb[:, half, :], bank[:, 2 * half, :]).then_inc(s_cg, 1)
                for half in range(2):
                    act.wait_ge(s_zf, 2 * i + half + 3)
                    nc.scalar.copy(z_hi[:, half * HALF:(half + 1) * HALF], z_f[:, half, :]).then_inc(s_zh, 1)

            with act.Fori(0, FT - 1) as i:
                short_round(i)
            short_round(FT - 1)
            norm_pair(N_F1, OUT_S + 16 * (FT - 1))

            with act.Fori(0, ROUNDS - 1) as i:
                ffn_round(1, i)
            ffn_round(1, ROUNDS - 1)
            norm_pair(N_END, OUT_F[1] + 16 * (ROUNDS - 1))

            for tt in range(TT):
                act.wait_ge(s_fturn, 2 * tt + 1)
                if tt >= 2:
                    act.wait_ge(s_store[tt % 2], 16 * (tt // 2))
                nc.scalar.copy(fin_rows[:, tt % 2, 0:HALF], bank[:, 2 * (tt % 2), :]).then_inc(s_fra, 1)

        @block.vector
        def _(dve):
            steps = Steps(dve, s_dve)
            V = nc.vector

            def add_squares(n, f):
                w = NORMS[n][2]
                dve.wait_ge(s_sq, 8 * n + f + 1)
                if f == 0:
                    if n:
                        dve.wait_ge(s_ss, n)
                    V.tensor_copy(sumsq[:, 0:w], sq[:, 0, 0:w]).then_inc(s_sum, 1)
                else:
                    dve.wait_ge(s_sum, 8 * n + f)
                    V.tensor_tensor(sumsq[:, 0:w], sumsq[:, 0:w], sq[:, f % 2, 0:w], ALU.add).then_inc(s_sum, 1)

            def inverse_rms(n):
                dve.wait_ge(s_sqrt, n + 1)
                if n:
                    dve.wait_ge(s_bc, n)
                w = NORMS[n][2] // P
                steps.run(V.reciprocal(std[:, 1, 0:w], std[:, 0, 0:w]))
                for j in range(w):
                    last = V.tensor_scalar(diag[:, j, :], ident[:], std[:, 1, j:j + 1], None, ALU.mult)
                last.then_inc(s_rstd, 1)

            def scale(n, f):
                src, half, w, gain, *_ = NORMS[n]
                dve.wait_ge(s_bc, n + 1)
                if n == N_END + 1 and f < 2 or n == N_END and f >= 2 or n == N_END + 1:
                    dve.wait_ge(s_fin, 8 * (n - N_END) + f - 1)
                elif 8 * n + f >= 2 :
                    dve.wait_ge(s_nhi, 8 * n + f - 1)
                V.tensor_tensor(scaled[:, f % 2, 0:w], src[:, f, cols(n)], bank[:, 6, 0:w], ALU.mult).then_inc(s_scal, 1)

            def low(n, f):
                w, gain = NORMS[n][2:4]
                if gain is None:
                    return
                dve.wait_ge(s_nhi, 8 * n + f + 1)
                a_hi, a_lo = (ctx_hi, ctx_lo) if n == N_CTX else (act_hi, act_lo)
                V.tensor_tensor(a_lo[:, f, cols(n)], normed[:, f % 2, 0:w], a_hi[:, f, cols(n)], ALU.subtract).then_inc(s_norm, 1)

            def apply_norm(n, between=lambda f: None):
                scale(n, 0)
                scale(n, 1)
                for f in range(FT):
                    low(n, f)
                    if f + 2 < FT:
                        scale(n, f + 2)
                    between(f)

            def update(n0, idx, gate):
                half, m = divmod(idx, FT)
                dve.wait_ge(s_out, n0 + idx + 1)
                dst = h[:, m, half * HALF:(half + 1) * HALF]
                V.scalar_tensor_tensor(out=dst, in0=bank[:, 4 + m % 2, :], scalar=mods[:, gate, m:m + 1], in1=dst,
                                       op0=ALU.mult, op1=ALU.add).then_inc(s_hup, 1)

            def last_updates(n0, gate, n):
                for f in range(FT):
                    update(n0, f, gate)
                    if f:
                        add_squares(n, f - 1)
                add_squares(n, FT - 1)
                update(n0, FT, gate)
                update(n0, FT + 1, gate)
                inverse_rms(n)
                update(n0, FT + 2, gate)
                add_squares(n + 1, 0)
                add_squares(n + 1, 1)

                def between(f):
                    if f + 3 < FT:
                        update(n0, FT + f + 3, gate)
                    if f + 2 < FT:
                        add_squares(n + 1, f + 2)

                apply_norm(n, between)
                inverse_rms(n + 1)
                apply_norm(n + 1)

            for s, credits in ((s_conv, 1), (s_lru, 1), (s_modset, 2), (s_ptd, 1), (s_on, 2), (s_yl, 4), (s_hup, 2),
                               (s_hidf, 2), (s_zf, 2)):
                dve.sem_inc(s, credits)

            dve.wait_ge(s_par_t, 1)
            V.tensor_copy(par[:], bank[:, 0, 0:124]).then_inc(s_param, 1)
            V.tensor_copy(mod_bias[:, :, :].rearrange("p a f -> p (a f)"), bank[:, 0, 128:224]).then_inc(s_param, 1)
            for tt in range(TT + CT):
                dst = h[:, 4:8, tt * P:(tt + 1) * P] if tt < TT else ctx_t[:, 4:8, (tt - TT) * P:(tt - TT + 1) * P]
                dve.wait_ge(s_turn, 2 * tt + 2)
                V.tensor_copy(dst, bank[:, 2 * (tt % 2) + 1, :].rearrange("p (f c) -> p f c", c=P)).then_inc(s_xpd, 1)
            dve.wait_ge(s_param, 2)
            lam = par[:, PAR["lam"]:PAR["lam"] + 8]
            steps.run(V.tensor_scalar(sp_t[:, 2, :], lam, -1.0, None, ALU.mult))
            V.tensor_tensor(sp_t[:, 0, :], sp_t[:, 2, :], lam, ALU.max).then_inc(s_const, 1)
            steps.run(V.tensor_scalar(half_b[:], par[:, PAR["br"]:PAR["br"] + 16], 0.5, None, ALU.mult))
            dve.wait_ge(s_act, 1)
            e, y, y2, acc = (sp_t[:, k, :] for k in (1, 3, 4, 0))
            steps.run(V.tensor_scalar(y2, e, 2.0, None, ALU.add))
            steps.run(V.reciprocal(y, y2))
            steps.run(V.tensor_tensor(y, e, y, ALU.mult))
            steps.run(V.tensor_tensor(y2, y, y, ALU.mult))
            steps.run(V.tensor_scalar(acc, y2, 1.0 / 17, 1.0 / 15, ALU.mult, ALU.add))
            for k in (13, 11, 9, 7, 5, 3, 1):
                steps.run(V.tensor_tensor(acc, acc, y2, ALU.mult))
                steps.run(V.tensor_scalar(acc, acc, 1.0 / k, None, ALU.add))
            steps.run(V.tensor_tensor(acc, acc, y, ALU.mult))
            steps.run(V.tensor_scalar(sp_t[:, 2, :], sp_t[:, 2, :], 0.0, 2.0, ALU.max, ALU.mult))
            V.scalar_tensor_tensor(out=sp2[:], in0=acc, scalar=4.0, in1=sp_t[:, 2, :], op0=ALU.mult, op1=ALU.add).then_inc(s_const, 1)

            with dve.Fori(0, 2 * MODS) as c:
                dve.wait_ge(s_modt, c + 1)
                summed = bank[:, 2, 0:2 * FT].rearrange("p (m j) -> p m j", j=2)
                for j, dst in enumerate((mods, mods_ctx)):
                    V.tensor_tensor(dst[:, bass.ds(c, 1), :].rearrange("p a f -> p (a f)"), summed[:, :, j],
                                    mod_bias[:, bass.ds(c, 1), :].rearrange("p a f -> p (a f)"), ALU.add).then_inc(s_modset, 1)
            dve.wait_ge(s_modset, 2 + 4 * MODS)
            for k, (src, which, g) in enumerate(((mods, SC1, PAR["n1"]), (mods_ctx, SC1, PAR["n1"]), (mods, SC2, PAR["n2"]),
                                                 (mods, MODS + SC1, PAR["n1"] + FT), (mods, MODS + SC2, PAR["n2"] + FT))):
                last = V.scalar_tensor_tensor(out=gains[:, k, :], in0=src[:, which, :], scalar=1.0, in1=par[:, g:g + FT],
                                              op0=ALU.add, op1=ALU.mult)
            last.then_inc(s_const, 1)

            for n in (0, 1, 2):
                for f in range(FT):
                    add_squares(n, f)
                inverse_rms(n)
                apply_norm(n)

            dve.wait_ge(s_pad, 3)
            with dve.Fori(0, LT) as i:
                steps.begin_loop(i, 15)
                dve.wait_ge(s_projev, 10 * i + 8)
                for j in range(4):
                    w = par[:, bass.ds(i + (PAR["conv_w"] + j * LT), 1)]
                    for part, (src, dst, n) in enumerate(((0, 0, CTX), (CTX + 3, CTX, SEQ))):
                        win, xc = x_pad[:, src + j:src + j + n], x_conv[:, dst:dst + n]
                        if j == 0:
                            ins = V.tensor_scalar(xc, win, w, par[:, bass.ds(i + PAR["conv_b"], 1)], ALU.mult, ALU.add)
                        else:
                            ins = V.scalar_tensor_tensor(out=xc, in0=win, scalar=w, in1=xc, op0=ALU.mult, op1=ALU.add)
                        if part:
                            ins.then_inc(s_conv, 1) if j == 3 else steps.run(ins)
                for d in range(2):
                    R, I, Q = lru_r[:, d, :], lru_i[:, d, :], lru_q[:, d, :]
                    dve.wait_ge(s_gatev, 12 * i + (3 + 6 * (d + 1)))
                    dve.wait_ge(s_conv, i + 2)
                    V.scalar_tensor_tensor(out=I, in0=I, scalar=1.0, in1=x_conv[:], op0=ALU.add, op1=ALU.mult)
                    dve.wait_ge(s_rs, 2 * i + d + 1)
                    steps.run(V.tensor_scalar(R, R, 1.0, None, ALU.add))
                    steps.run(V.reciprocal(R, R))
                    steps.run(V.tensor_tensor(Q, Q, R, ALU.mult))
                    V.tensor_tensor(I, I, Q, ALU.mult)
                    steps.run(V.tensor_scalar(R, R, 2.0, -1.0, ALU.mult, ALU.add))
                    if d == 0:
                        steps.run(V.tensor_tensor_scan(Q, R, I, 0.0, ALU.mult, ALU.add))
                    else:
                        rev, lat = slice(CTX - 1, None, -1), slice(KEYS - 1, CTX - 1, -1)
                        steps.run(V.tensor_tensor_scan(Q[:, rev], R[:, rev], I[:, rev], 0.0, ALU.mult, ALU.add))
                        steps.run(V.tensor_tensor_scan(Q[:, lat], R[:, lat], I[:, lat], Q[:, 0:1], ALU.mult, ALU.add))
                steps.run(V.tensor_tensor(lru_i[:, 0, 0:SEQ], lru_q[:, 0, CTX:], lru_q[:, 1, CTX:], ALU.add))
                dve.wait_ge(s_projev, 10 * i + 15)
                V.tensor_tensor(lru_q[:, 0, 0:SEQ], lru_i[:, 0, 0:SEQ], g_gelu[:], ALU.mult).then_inc(s_lru, 1)
            steps.end_loop(LT)

            dve.wait_ge(s_v, V_TILES)
            for j in range(LT):
                dve.wait_ge(s_ylh, j + 1)
                V.tensor_tensor(act_lo[:, LT + j, :], r_in[:, j % 2, :], act_hi[:, LT + j, :], ALU.subtract).then_inc(s_yll, 1)
            N = 4 * TT

            def min_logit(i, s):
                slot, b, hh = s // (2 * TT), (s // 2) % TT, s % 2
                k0, wide = window(b)
                w = MID if wide else HALF
                o = 2 * (s % 2) * HALF
                at0 = EDGE if wide else (k0 - 2 * b * GRID) + 6 * GRID
                st = stat[:, s % 4, :]
                if s % (2 * TT) == 0:
                    dve.wait_ge(s_bias, 4 * i + (2 * slot + 2))
                dve.wait_ge(s_sc, N * i + s + 1)
                steps.run(V.tensor_reduce(st[:, 0:1], bank_f[:, o + MID:o + WIDE], AX_X, ALU.min))
                alone(dve)
                V.tensor_tensor_reduce(out=probs[:, s % 2, 0:w], in0=bank_f[:, o:o + w], in1=bias_t[slot][:, hh, at0:at0 + w],
                                       scale=1.0, scalar=st[:, 0:1], op0=ALU.add, op1=ALU.min, accum_out=st[:, 1:2]
                                       ).then_inc(s_min, 1)

            def context_turned(i, s):
                wide = window((s // 2) % TT)[1]
                dve.wait_ge(s_pt, N * i + s + 1)
                if wide:
                    V.tensor_copy(probs_t[0:64, s % 2, 6, :], bank_f[0:64, 5 * HALF + 2 * P:5 * HALF + 3 * P])
                V.tensor_copy(probs_t[:, s % 2, 4:6, :].rearrange("p c n -> p (c n)"), bank[:, 5, 0:2 * P]).then_inc(s_ptd, 1)

            def scale_out(i, s):
                b, hh = (s // 2) % TT, s % 2
                st = stat[:, s % 4, :]
                dve.wait_ge(s_exp, N * i + s + 3)
                steps.run(V.tensor_tensor(st[:, 4:5], st[:, 2:3], st[:, 3:4], ALU.add))
                steps.run(V.reciprocal(st[:, 5:6], st[:, 4:5]))
                dve.wait_ge(s_pv, N * i + s + 1)
                V.tensor_scalar(o_tok[:, b % 2, 64 * hh:64 * hh + 64], bank[:, 6, 64 * (s % 2):64 * (s % 2) + 64],
                                st[:, 5:6], None, ALU.mult).then_inc(s_on, 1)

            def y_low(i, s):
                b = (s // 2) % TT
                dve.wait_ge(s_yh, (N // 2) * i + s // 2 + 1)
                q = (s // 2) % 4
                tile = (slice(None), bass.ds(2 * i + s // (2 * TT), 1), slice(b * P, (b + 1) * P))
                V.tensor_tensor(act_lo[tile].rearrange("p a n -> p (a n)"), bank[:, 7, q * P:(q + 1) * P],
                                act_hi[tile].rearrange("p a n -> p (a n)"), ALU.subtract).then_inc(s_yl, 1)

            with dve.Fori(0, LT // 2) as i:
                steps.begin_loop(i, 3 * N)
                for s in range(N + 3):
                    if s < N:
                        min_logit(i, s)
                    if 0 <= s - 1 < N:
                        context_turned(i, s - 1)
                    if 0 <= s - 2 < N:
                        scale_out(i, s - 2)
                    if 0 <= s - 3 < N and (s - 3) % 2:
                        y_low(i, s - 3)
            steps.end_loop(LT // 2)

            dve.wait_ge(s_reload, 16 * FT)
            last_updates(0, G1, N_F0)

            def hidden(layer, i):
                q0 = 4 * ROUNDS * layer
                for q in range(4):
                    half, tile = divmod(q, 2)
                    dve.wait_ge(s_silu, 4 * i + (q0 + q + 1))
                    dve.wait_ge(s_gu, 8 * i + (2 * q0 + 2 * q + 2))
                    V.tensor_tensor(hid_f[:, q % 2, :], silu_g[:, q % 2, :], bank[:, 2 * tile + 1, :], ALU.mult).then_inc(s_hidf, 1)
                    dve.wait_ge(s_hidh, 4 * i + (q0 + q + 1))
                    sl = slice(half * HALF, (half + 1) * HALF)
                    V.tensor_tensor(hid_lo[:, tile, sl], hid_f[:, q % 2, :], hid_hi[:, tile, sl], ALU.subtract).then_inc(s_hid, 1)

            def ffn(layer, norm):
                with dve.Fori(0, ROUNDS - 1) as i:
                    hidden(layer, i)
                    for idx in range(16):
                        update(16 * i + OUT_F[layer], idx, MODS * layer + G2)
                hidden(layer, ROUNDS - 1)
                last_updates(OUT_F[layer] + 16 * (ROUNDS - 1), MODS * layer + G2, norm)

            ffn(0, N_S)

            for lo in (0, SEQ + 1):
                V.memset(t_pad[:, lo:lo + 1], 0.0).then_inc(s_tz, 1)
            dve.wait_ge(s_tz, 2)

            def short(i):
                for half in range(2):
                    dve.wait_ge(s_cg, 2 * i + half + 1)
                    dve.wait_ge(s_sg, 6 * i + (2 * half + 2))
                    V.tensor_tensor(t_pad[:, 1 + half * HALF:1 + (half + 1) * HALF], cg_sb[:, half, :],
                                    bank[:, 2 * half + 1, :], ALU.mult).then_inc(s_t, 1)
                dve.wait_ge(s_t, 2 * i + 2)
                for j in range(3):
                    w = par[:, bass.ds(i + (PAR["short_w"] + j * FT), 1)]
                    if j == 0:
                        steps.run(V.tensor_scalar(conv_t[:], t_pad[:, 0:SEQ], w, None, ALU.mult))
                    else:
                        steps.run(V.scalar_tensor_tensor(out=conv_t[:], in0=t_pad[:, j:j + SEQ], scalar=w, in1=conv_t[:],
                                                         op0=ALU.mult, op1=ALU.add))
                for half in range(2):
                    sl = slice(half * HALF, (half + 1) * HALF)
                    dve.wait_ge(s_sg, 6 * i + (5 + half))
                    V.tensor_tensor(z_f[:, half, :], conv_t[:, sl], bank[:, half, :], ALU.mult).then_inc(s_zf, 1)
                    dve.wait_ge(s_zh, 2 * i + half + 1)
                    V.tensor_tensor(z_lo[:, sl], z_f[:, half, :], z_hi[:, sl], ALU.subtract).then_inc(s_z, 1)

            with dve.Fori(0, FT - 1) as i:
                steps.begin_loop(i, 3)
                short(i)
                for idx in range(16):
                    update(16 * i + OUT_S, idx, MODS + G1)
            steps.end_loop(FT - 1)
            short(FT - 1)
            last_updates(OUT_S + 16 * (FT - 1), MODS + G1, N_F1)

            ffn(1, N_END)

            for tt in range(TT):
                dve.wait_ge(s_fturn, 2 * tt + 2)
                if tt >= 2:
                    dve.wait_ge(s_store[tt % 2], 16 * (tt // 2))
                V.tensor_copy(fin_rows[:, tt % 2, HALF:D], bank[:, 2 * (tt % 2) + 1, :]).then_inc(s_frd, 1)


INPUTS = ("x", "c", "ctx", "c_ctx", "mod_w", "mod_b", "norm1_g", "norm2_g", "ffn_w_gu", "ffn_w_down", "e_w_in",
          "e_w_out", "e_conv_w", "e_conv_b", "e_lru_wr", "e_lru_br", "e_lru_wi", "e_lru_bi", "e_lru_lam", "e_rpb",
          "o_w_in", "o_conv_w", "o_w_out", "final_g")


def kernel(**inputs):
    import numpy as np
    import concourse.bacc as bacc
    from concourse.bass_utils import run_bass_kernel_spmd

    nc = bacc.Bacc("TRN2", target_bir_lowering=False, num_devices=1)
    arrays, tensors = {}, {}
    for name in INPUTS:
        a = np.ascontiguousarray(inputs[name])
        arrays["in_" + name] = a
        tensors[name] = nc.dram_tensor("in_" + name, a.shape, F32, kind="ExternalInput").ap()
    tensors["out"] = nc.dram_tensor("out", inputs["x"].shape, F32, kind="ExternalOutput").ap()
    backbone(nc, tensors)
    result = run_bass_kernel_spmd(nc, [arrays], core_ids=[0])
    return result.results[0]["out"]
```

```python
from contextlib import ExitStack

import concourse.bass as bass
from concourse import mybir

ALU = mybir.AluOpType
ACT = mybir.ActivationFunctionType
AX_X = mybir.AxisListType.X
F32 = mybir.dt.float32
F32R = mybir.dt.float32r

P = 128
EPS = 1e-6
FAR = 1e30
GRID = 64
HALF = 512
UNIT = 1024


class Steps:

    def __init__(self, eng, sem):
        self.eng, self.sem, self.n, self.base = eng, sem, 0, 0

    def run(self, ins):
        ins.then_inc(self.sem, 1)
        self.n += 1
        self.eng.wait_ge(self.sem, self.base + self.n)

    def begin_loop(self, i, per):
        self.start, self.base, self.per = self.n, i * per, per

    def end_loop(self, rounds):
        assert self.n - self.start == self.per, (self.n - self.start, self.per)
        self.n, self.base = self.start + rounds * self.per, 0


def backbone(nc, t):
    x, context, out = t["x"], t["ctx"], t["out"]
    _, SEQ, D = x.shape
    CTX = context.shape[1]
    FT = D // P
    TT = SEQ // P
    CT = CTX // P
    KEYS = CTX + SEQ
    LT = t["e_conv_b"].shape[1] // P
    HID = t["ffn_w_down"].shape[1]
    ROUNDS = HID // (2 * P)
    _, HEADS, NR, NC = t["e_rpb"].shape
    MODS = 6
    SH1, SC1, G1, SH2, SC2, G2 = range(MODS)
    assert (SEQ, D, CTX, LT, HEADS, NR, NC) == (2 * HALF, 1024, 256, 4, 8, 15, 31)

    es = ExitStack()
    with es:
        def sem(name):
            return es.enter_context(nc.semaphore(name))

        def keep(name, shape, dt=F32):
            return es.enter_context(nc.sbuf_tensor(name, shape, dt))

        def at(kb, name, shape, dt=F32):
            with ExitStack() as s:
                if kb:
                    s.enter_context(nc.sbuf_tensor("below_" + name, [P, int(kb * 256)], F32))
                return s.enter_context(nc.sbuf_tensor(name, shape, dt))

        h_spill = nc.dram_tensor("h_spill", (P, FT, SEQ), F32, kind="Internal").ap()
        q_spill = nc.dram_tensor("q_spill", (LT, P, SEQ), F32, kind="Internal").ap()
        k_spill = nc.dram_tensor("k_spill", (LT, P, KEYS), F32, kind="Internal").ap()
        v_spill = nc.dram_tensor("v_spill", (P, TT + CT, LT * P), F32, kind="Internal").ap()
        r_spill = nc.dram_tensor("r_spill", (LT, P, SEQ), F32, kind="Internal").ap()
        PAD = 64
        RPB = HEADS * NR * NC
        rpb_pad = nc.dram_tensor("rpb_pad", (1, PAD + RPB + PAD), F32, kind="Internal").ap()
        rpb_wide = nc.dram_tensor("rpb_wide", (HEADS, NR, GRID, GRID), F32, kind="Internal").ap()

        probs_w = [at(64 + 12 + 16 * j, f"probs{j + 2}", [P, 832]) for j in range(2)]
        act_hi = keep("act_hi", [P, FT, SEQ], F32R)
        mod_ring = at(0, "mod_ring", [P, 4, UNIT])
        mod_row = at(16, "mod_row", [2, UNIT])
        fin = at(0, "fin", [P, FT, SEQ])
        act_lo = keep("act_lo", [P, FT, SEQ], F32R)
        w_hi4 = keep("w_hi4", [P, 4, UNIT], F32R)
        w_lo4 = keep("w_lo4", [P, 4, UNIT], F32R)
        raw = keep("raw", [P, 2, UNIT])
        ident = keep("ident", [P, P])
        ones = keep("ones", [P, P])
        mod_bias = keep("mod_bias", [P, 2 * MODS, FT])
        mods = keep("mods", [P, 2 * MODS, FT])
        mods_ctx = keep("mods_ctx", [P, 2, FT])
        par = keep("par", [P, 124])
        cond = keep("cond", [P, FT, 2])
        gains = keep("gains", [P, 5, FT])
        half_b = keep("half_b", [P, 16])
        sp2 = keep("sp2", [P, 8])
        sp4 = keep("sp4", [P, 8])
        sp_t = keep("sp_t", [P, 5, 8])
        eps_t = keep("eps_t", [P, 1])
        std = keep("std", [P, 2, 4])

        h = at(0, "h", [P, FT, SEQ])
        w_hi2 = at(32, "w_hi2", [P, 2, UNIT], F32R)
        w_lo2 = at(40, "w_lo2", [P, 2, UNIT], F32R)
        sq = at(48, "sq", [P, 2, HALF])
        sumsq = at(52, "sumsq", [P, HALF])
        diag = at(54, "diag", [P, 4, P])
        scaled = at(56, "scaled", [P, 2, HALF])
        normed = at(60, "normed", [P, 2, HALF])
        x_in = at(64, "x_in", [P, 2, D])
        ctx_t = at(72, "ctx_t", [P, FT, CTX])
        par_rows = at(80, "par_rows", [124, P])
        b_rows = at(80.5, "b_rows", [96, P])
        zero_row = at(81, "zero_row", [1, PAD])
        hid_hi = at(64, "hid_hi", [P, 2, SEQ], F32R)
        hid_lo = at(72, "hid_lo", [P, 2, SEQ], F32R)
        silu_g = at(80, "silu_g", [P, 2, HALF])
        hid_f = at(84, "hid_f", [P, 2, HALF])
        mod_in_f = at(88, "mod_in_f", [P, 2, UNIT])
        mod_acc_f = at(60, "mod_acc_f", [P, UNIT])
        z_hi = at(64, "z_hi", [P, 2, SEQ], F32R)
        z_lo = at(72, "z_lo", [P, 2, SEQ], F32R)
        cg_sb = at(80, "cg_sb", [P, 2, HALF])
        conv_t = at(84, "conv_t", [P, SEQ])
        z_f = at(88, "z_f", [P, 2, HALF])
        t_pad = at(92, "t_pad", [P, SEQ + 2])
        fin_rows = at(88, "fin_rows", [P, 2, D])
        lru_r = at(0, "lru_r", [P, 2, KEYS])
        lru_i = at(10, "lru_i", [P, 2, KEYS])
        lru_q = at(20, "lru_q", [P, 2, KEYS])
        gate_w = at(30, "gate_w", [P, 4, P])
        mod_in_p = at(32, "mod_in_p", [P, 2, UNIT])
        mod_acc_p = at(44, "mod_acc_p", [P, UNIT])
        g_gelu = at(40, "g_gelu", [P, SEQ])
        qk_out = at(48, "qk_out", [P, 5, HALF])
        v_tok = at(48, "v_tok", [P, TT + CT, LT * P])
        x_pad = at(68, "x_pad", [P, KEYS + 6])
        x_conv = at(73.5, "x_conv", [P, KEYS])
        ctx_hi = at(80, "ctx_hi", [P, FT, CTX], F32R)
        ctx_lo = at(88, "ctx_lo", [P, FT, CTX], F32R)
        EDGE = 14 * GRID
        MID = 9 * GRID
        WIDE = MID + CTX
        assert WIDE == 832 and WIDE <= UNIT
        k_raw = at(0, "k_raw", [P, KEYS])
        q_raw = at(5, "q_raw", [P, SEQ])
        v_raw = at(9, "v_raw", [P, TT + CT, P])
        bias_t = at(14, "bias_t", [P, 2, EDGE + MID])
        probs = [at(25.5 + 3.25 * j, f"probs{j}", [P, WIDE]) for j in range(2)] + probs_w
        r_in = at(32, "r_in", [P, 2, SEQ])
        pt_hi = at(32, "pt_hi", [P, 2, 7, P], F32R)
        pt_lo = at(39, "pt_lo", [P, 2, 7, P], F32R)
        stat = at(46, "stat", [P, 4, 6])
        v_hi = at(48, "v_hi", [P, 2, TT + CT, P], F32R)
        v_lo = at(58, "v_lo", [P, 2, TT + CT, P], F32R)
        q_st = at(68, "q_st", [P, 2, SEQ], F32R)
        k_hi = at(76, "k_hi", [P, 2, KEYS], F32R)
        k_lo = at(86, "k_lo", [P, 2, KEYS], F32R)

        bank = es.enter_context(nc.psum_tensor("bank", [P, 8, HALF], F32))
        bank_f = bank[:, :, :].rearrange("p b n -> p (b n)")

        def w_slot(s):
            return (w_hi4[:, s, :], w_lo4[:, s, :]) if s < 4 else (w_hi2[:, s - 4, :], w_lo2[:, s - 4, :])

        U_P = 0
        U_V = U_P + 4 * LT
        U_O = U_V + 4
        U_F0 = U_O + 2 * FT
        U_S = U_F0 + 6 * ROUNDS
        U_F1 = U_S + 4 * FT
        U_END = U_F1 + 6 * ROUNDS

        s_par, s_ident, s_turn, s_par_t = sem("par_landed"), sem("ident_made"), sem("x_turned"), sem("par_turned")
        s_cond, s_param = sem("cond_ready"), sem("par_placed")
        s_x = (sem("x_landed0"), sem("x_landed1"))
        s_xpa, s_xpd = sem("x_placed_by_act"), sem("x_placed_by_dve")
        s_mod = [sem(f"mod_landed{j}") for j in range(4)]
        s_modmm, s_modrow, s_modt, s_modset = sem("mod_summed"), sem("mod_row_ready"), sem("mod_turned"), sem("mod_set")
        s_mu = (sem("mod_unit_landed0"), sem("mod_unit_landed1"))
        s_macc, s_mfin, s_mset = sem("mod_unit_added"), sem("mod_totals_ready"), sem("mod_vector_set")
        s_const = sem("constants_ready")
        s_raw = (sem("raw_landed0"), sem("raw_landed1"))
        s_hi, s_split = sem("unit_hi"), sem("unit_split")
        s_sq, s_sum, s_ss, s_sqrt, s_rstd = sem("squared"), sem("summed"), sem("sumsq_in_psum"), sem("rms_ready"), sem("diag_ready")
        s_bc, s_scal, s_nf, s_nhi, s_norm = sem("rstd_spread"), sem("scaled_ready"), sem("normed_ready"), sem("normed_hi"), sem("norm_done")
        s_spill, s_reload = sem("h_spilled"), [sem(f"h_reloaded{j}") for j in range(3)]
        s_proj, s_projev = sem("proj_done"), sem("proj_evacuated")
        s_qk = sem("qk_stored")
        s_pad, s_conv = sem("pads_zero"), sem("x_convolved")
        s_gw, s_gwz = sem("gate_w_landed"), sem("gate_w_zero")
        s_gate, s_gatev = sem("gate_done"), sem("gate_evacuated")
        s_s, s_rs, s_lru = sem("decay_ready"), sem("root_ready"), sem("lru_done")
        s_rfree = sem("lru_result_free")
        s_rst, s_rin = sem("lru_stored"), (sem("lru_reloaded0"), sem("lru_reloaded1"))
        s_v, s_vev = sem("v_done"), sem("v_evacuated")
        s_ylh, s_yll = sem("lru_hi"), sem("lru_lo")
        s_rpb, s_zero = sem("rpb_padded"), sem("zero_row_ready")
        s_wide = sem("bias_widened")
        s_braw = sem("bias_landed")
        s_bias = sem("bias_built")
        s_bstep = sem("pool_step")
        s_vst, s_vraw, s_vp = sem("v_stored"), sem("v_landed"), sem("v_split")
        s_hraw, s_hd, s_hstep = sem("qk_landed"), sem("qk_split"), sem("qk_hi")
        s_sc, s_min, s_exp = sem("scores_done"), sem("min_ready"), sem("probs_ready")
        s_pn, s_pt = sem("probs_normalized"), sem("probs_turned")
        s_pth, s_ptl = sem("turned_hi"), sem("turned_lo")
        s_pv, s_yh, s_yl = sem("pv_done"), sem("y_hi"), sem("y_lo")
        s_out, s_hup = sem("out_done"), sem("h_updated")
        s_gu, s_silu, s_hidf = sem("gate_up_done"), sem("silu_ready"), sem("hidden_ready")
        s_hidh, s_hid = sem("hidden_hi"), sem("hidden_split")
        s_sg, s_cg, s_t, s_cv = sem("short_done"), sem("cg_ready"), sem("t_ready"), sem("short_convolved")
        s_zf, s_zh, s_z = sem("z_ready"), sem("z_hi_ready"), sem("z_split")
        s_tz = sem("t_pads_zero")
        s_fin, s_fturn, s_store = sem("fin_ready"), sem("fin_turned"), (sem("stored0"), sem("stored1"))
        s_fra, s_frd = sem("fin_row_by_act"), sem("fin_row_by_dve")
        s_dve, s_act = sem("dve_step"), sem("exp_ready")
        s_alone = sem("waits_alone")

        def alone(eng):
            eng.sem_inc(s_alone, 1)

        NORMS = ([(h, 0, HALF, 0, mods, SH1), (h, 1, HALF, 0, mods, SH1), (ctx_t, 0, CTX, 1, mods_ctx, SH1)]
                 + [(h, a, HALF, 2, mods, SH2) for a in (0, 1)]
                 + [(h, a, HALF, 3, mods, MODS + SH1) for a in (0, 1)]
                 + [(h, a, HALF, 4, mods, MODS + SH2) for a in (0, 1)]
                 + [(h, a, HALF, None, None, None) for a in (0, 1)])
        N_X, N_CTX, N_F0, N_S, N_F1, N_END = 0, 2, 3, 5, 7, 9

        def cols(n):
            a, half, w, *_ = NORMS[n]
            return slice(half * HALF, half * HALF + w)

        SPREAD = (6, 5, 4) + (6,) * 8

        PAR = dict(n1=0, n2=16, nf=32, conv_w=40, conv_b=56, br=60, bi=68, lam=76, short_w=84, c=108)

        def window(b):
            lo = [min(max(r - 4, 0), SEQ // GRID - 8) for r in (2 * b, 2 * b + 1)]
            return lo[0] * GRID, lo[0] != lo[1]

        V_TILES = TT + CT
        V_ORDER = list(range(TT, V_TILES)) + list(range(TT))
        STEPS = TT * HEADS // 2

        def used_p(i, j):
            return s_proj, 10 * i + (3, 5, 8, 10)[j]

        def used_o(j):
            return s_out, j + 1

        def used_f(layer, i, j):
            if j < 4:
                return s_gu, 8 * ROUNDS * layer + 8 * i + 5 + j
            return s_out, OUT_F[layer] + 16 * i + 16

        def used_s(i, j):
            return (s_sg, 12 * i + (3, 4, 6, 9, 10, 12)[j]) if j < 6 else (s_out, OUT_S + 16 * i + 16)

        OUT_F = (2 * FT, 2 * FT + 16 * (ROUNDS + FT // 2))
        OUT_S = 2 * FT + 16 * ROUNDS

        block = es.enter_context(nc.Block())

        @block.sync
        def _(sp):
            w_in, w_out = t["e_w_in"][0], t["e_w_out"][0]
            AW = LT * P

            def load_unit(u, parity, src):
                if not isinstance(u, int) or u >= 2:
                    sp.wait_ge(s_split, u - 1)
                    if not isinstance(u, int):
                        alone(sp)
                dst = raw[:, parity, :]
                if len(src.shape) == 3:
                    dst = dst.rearrange("p (k m) -> p k m", k=src.shape[1])
                sp.dma_start(dst, src).then_inc(s_raw[parity], 16)

            def column_unit(w, col):
                return w[:, bass.ds(col, P)].rearrange("(k p) m -> p k m", p=P)

            r = 0
            for src in (t["norm1_g"].rearrange("l (r c) -> (l r) c", c=P),
                        t["norm2_g"].rearrange("l (r c) -> (l r) c", c=P),
                        t["final_g"].rearrange("(r c) -> r c", c=P),
                        t["e_conv_w"][0].rearrange("j (r c) -> (j r) c", c=P),
                        t["e_conv_b"][0].rearrange("(r c) -> r c", c=P),
                        t["e_lru_br"][0].rearrange("d (r c) -> (d r) c", c=P),
                        t["e_lru_bi"][0].rearrange("d (r c) -> (d r) c", c=P),
                        t["e_lru_lam"][0].rearrange("d (r c) -> (d r) c", c=P),
                        t["o_conv_w"][0].rearrange("j (r c) -> (j r) c", c=P),
                        t["c"][0].rearrange("(r c) -> r c", c=P),
                        t["c_ctx"].rearrange("(r c) -> r c", c=P)):
                sp.dma_start(par_rows[r:r + src.shape[0], :], src).then_inc(s_par, 16)
                r += src.shape[0]
            assert r == 124
            sp.dma_start(b_rows[:], t["mod_b"].rearrange("l (r c) -> (l r) c", c=P)).then_inc(s_par, 16)

            order_p = (3 * AW, 0, AW, 4 * AW)
            for j in range(2):
                load_unit(j, j, column_unit(w_in, order_p[j]))
            sp.wait_ge(s_zero, 1)
            sp.dma_start(rpb_pad[0:1, 0:PAD], zero_row[:]).then_inc(s_rpb, 16)
            sp.dma_start(rpb_pad[0:1, PAD + RPB:], zero_row[:]).then_inc(s_rpb, 16)
            sp.dma_start(rpb_pad[0:1, PAD:PAD + RPB], t["e_rpb"].rearrange("a h r c -> a (h r c)")).then_inc(s_rpb, 16)

            mod_w = t["mod_w"].rearrange("l (k p) (w n) -> l w k p n", p=P, n=UNIT)
            for c in range(2):
                for k in range(FT):
                    sp.wait_ge(s_modmm, c * FT + k + 1)
                    sp.dma_start(mod_ring[:, k % 4, :], mod_w[0, c, k]).then_inc(s_mod[k % 4], 16)
            for j in range(2, 4):
                load_unit(j, j % 2, column_unit(w_in, order_p[j]))

            def load_mod(ring, layer, which, n, k):
                sp.wait_ge(s_macc, 8 * n + (k + 1))
                if not isinstance(n, int):
                    alone(sp)
                sp.dma_start(ring[:, k % 2, :], mod_w[layer, bass.ds(which, 1), k].rearrange("a p n -> p (a n)")).then_inc(s_mu[k % 2], 16)

            for head in range(HEADS):
                src = bass.AP(tensor=rpb_pad.tensor, offset=PAD + head * NR * NC + NC // 2, ap=[[NC, NR], [-1, GRID], [1, GRID]])
                if head == 0:
                    sp.wait_ge(s_rpb, 48)
                sp.dma_start(rpb_wide[head], src).then_inc(s_wide, 16)

            def load_gates(i):
                for d in range(2):
                    for g, w in enumerate((t["e_lru_wr"], t["e_lru_wi"])):
                        for a in range(2):
                            sp.dma_start(gate_w[64 * a:64 * a + 64, 2 * d + g, 64 * a:64 * a + 64],
                                         w[0, d, bass.ds(2 * i + a, 1)].rearrange("a p n -> p (a n)")).then_inc(s_gw, 16)

            def load_mod_p(n, k):
                load_mod(mod_in_p, 0, n + 2, n, k)

            sp.wait_ge(s_gwz, 1)
            load_gates(0)
            with sp.Fori(1, LT) as i:
                for j in range(4):
                    load_unit(4 * i + j, j % 2, column_unit(w_in, i * P + order_p[j]))
                    for k in (2 * j, 2 * j + 1):
                        load_mod_p(i - 1, k)
                sp.wait_ge(s_gate, i * 12)
                alone(sp)
                load_gates(i)
            wv = w_in.rearrange("(k p) n -> p k n", p=P)
            for j in range(4):
                load_unit(U_V + j, j % 2, wv[:, 2 * j:2 * j + 2, 2 * AW:3 * AW])
                for k in (2 * j, 2 * j + 1):
                    load_mod_p(LT - 1, k)

            def load_bias(head):
                for a in range(2):
                    sp.dma_start(bias_t[64 * a:64 * a + 64, head % 2, 0:EDGE].rearrange("p (j c) -> p j c", c=GRID),
                                 rpb_wide[head, 1 - a:15 - a].rearrange("j c k -> c j k")).then_inc(s_braw, 16)

            def load_head(head):
                pair, hh = divmod(head, 2)
                for a in range(2):
                    half = slice(64 * a, 64 * a + 64)
                    sp.dma_start(k_raw[half, :], k_spill[pair, 64 * hh:64 * hh + 64, :]).then_inc(s_hraw, 16)
                    sp.dma_start(q_raw[half, :], q_spill[pair, 64 * hh:64 * hh + 64, :]).then_inc(s_hraw, 16)

            def load_values(pair):
                sp.dma_start(v_raw[:], v_spill[:, :, pair * P:(pair + 1) * P]).then_inc(s_vraw, 16)

            for j in range(2):
                load_unit(U_O + j, j % 2, column_unit(w_out, j * P))
            sp.wait_ge(s_wide, 16 * HEADS)
            sp.wait_ge(s_qk, 16 + 80 * LT)
            sp.wait_ge(s_rfree, 1 + LT)
            load_head(0)
            load_bias(0)
            for j in range(2):
                sp.dma_start(r_in[:, j, :], r_spill[j]).then_inc(s_rin[j], 16)
            sp.wait_ge(s_hd, 1)
            load_head(1)
            for j in range(2, LT):
                sp.wait_ge(s_yll, j - 1)
                sp.dma_start(r_in[:, j % 2, :], r_spill[j]).then_inc(s_rin[j % 2], 16)
            sp.wait_ge(s_bias, 1)
            load_bias(1)
            sp.wait_ge(s_vst, 16 * (TT + CT))
            load_values(0)
            for j in range(2, 5):
                load_unit(U_O + j, j % 2, column_unit(w_out, j * P))
            for head in range(2, HEADS):
                if head % 2 == 0:
                    sp.wait_ge(s_vp, head // 2)
                    load_values(head // 2)
                sp.wait_ge(s_hd, head)
                load_head(head)
                sp.wait_ge(s_min, 8 * (head - 1))
                sp.wait_ge(s_bias, head)
                load_bias(head)
            sp.wait_ge(s_hd, HEADS)
            sp.wait_ge(s_vp, LT)
            sp.dma_start(h[:, 0:3, :], h_spill[:, 0:3, :]).then_inc(s_reload[0], 16)
            sp.wait_ge(s_min, TT * HEADS)
            sp.dma_start(h[:, 3:6, :], h_spill[:, 3:6, :]).then_inc(s_reload[1], 16)
            sp.wait_ge(s_pt, TT * HEADS)
            sp.dma_start(h[:, 6:8, :], h_spill[:, 6:8, :]).then_inc(s_reload[2], 16)
            for j in range(5, 2 * FT):
                load_unit(U_O + j, j % 2, column_unit(w_out, (j % FT) * P))

            def ffn_loads(layer, u0, i, mod=None):
                gu, down = t["ffn_w_gu"][layer], t["ffn_w_down"][layer]
                for j, off in enumerate((0, HID, P, HID + P)):
                    load_unit(6 * i + (u0 + j), j % 2, column_unit(gu, i * (2 * P) + off))
                    if mod is not None:
                        for k in (2 * j, 2 * j + 1):
                            load_mod(mod_in_f, 1, mod, mod + LT, k)
                for j in range(2):
                    load_unit(6 * i + (u0 + 4 + j), j % 2, down[bass.ds(i * (2 * P) + j * P, P), :])

            ffn_loads(0, U_F0, 0)
            with sp.Fori(1, 1 + MODS) as i:
                ffn_loads(0, U_F0, i, i - 1)
            with sp.Fori(1 + MODS, ROUNDS) as i:
                ffn_loads(0, U_F0, i)
            with sp.Fori(0, FT // 2) as i:
                for j, off in enumerate((D, 2 * D, 0, D + P, 2 * D + P, P)):
                    load_unit(8 * i + (U_S + j), j % 2, column_unit(t["o_w_in"][0], i * (2 * P) + off))
                for j in range(2):
                    load_unit(8 * i + (U_S + 6 + j), j % 2, t["o_w_out"][0][bass.ds(i * (2 * P) + j * P, P), :])
            with sp.Fori(0, ROUNDS) as i:
                ffn_loads(1, U_F1, i)

            for tt in range(TT):
                sp.wait_ge(s_fra, tt + 1)
                sp.wait_ge(s_frd, tt + 1)
                sp.dma_start(out[0, tt * P:(tt + 1) * P, :], fin_rows[:, tt % 2, :]).then_inc(s_store[tt % 2], 16)
            for tt in range(2):
                sp.wait_ge(s_store[tt], 16 * TT // 2)

        @block.gpsimd
        def _(pool):
            steps = Steps(pool, s_bstep)
            steps.run(nc.gpsimd.memset(ident[:], 0.0))
            nc.gpsimd.affine_select(out=ident[:], in_=ident[:], compare_op=ALU.not_equal, fill=1.0, base=0,
                                    pattern=[[-1, P]], channel_multiplier=1).then_inc(s_ident, 1)
            nc.gpsimd.memset(eps_t[:], EPS).then_inc(s_ident, 1)
            nc.gpsimd.memset(ones[:], 1.0).then_inc(s_ident, 1)
            nc.gpsimd.memset(zero_row[:], 0.0).then_inc(s_zero, 1)
            pool.sem_inc(s_rfree, 1)
            pool.wait_ge(s_ident, 3)

            def split(u, slot, parity, free=None):
                w_hi, w_lo = w_slot(slot)
                pool.wait_ge(s_raw[parity], 8 * u + (16 - 8 * parity))
                if free is not None:
                    pool.wait_ge(*free)
                nc.gpsimd.tensor_tensor(w_hi, raw[:, parity, :], ones[:, 0:1].to_broadcast([P, UNIT]),
                                        ALU.mult).then_inc(s_hi, 1)
                pool.wait_ge(s_hi, u + 1)
                nc.gpsimd.tensor_tensor(w_lo, raw[:, parity, :], w_hi, ALU.subtract).then_inc(s_split, 1)

            def store_lru(i):
                pool.wait_ge(s_lru, i + 2)
                nc.gpsimd.dma_start(r_spill[i], lru_q[:, 0, 0:SEQ]).then_inc(s_rst, 16)
                pool.wait_ge(s_rst, 16 * (i + 1))
                pool.sem_inc(s_rfree, 1)

            for j in range(4):
                split(j, j, j % 2)
            pool.wait_ge(s_spill, 16)
            pool.wait_ge(s_norm, 8 * (N_CTX + 1))
            nc.gpsimd.memset(gate_w[:], 0.0).then_inc(s_gwz, 1)
            for lo, w in ((0, 2), (CTX + 2, 3), (KEYS + 5, 1)):
                nc.gpsimd.memset(x_pad[:, lo:lo + w], 0.0).then_inc(s_pad, 1)
            for i in range(1, LT):
                for j in range(4):
                    split(4 * i + j, j, j % 2, used_p(i - 1, j))
                    if j == 1 and i >= 2:
                        store_lru(i - 2)
            for j in range(4):
                split(U_V + j, j, j % 2, used_p(LT - 1, j))
                if j == 1:
                    store_lru(LT - 2)
            store_lru(LT - 1)

            def build_bias(head):
                pool.wait_ge(s_braw, 32 * (head + 1))
                edge = bias_t[:, head % 2, 0:EDGE].rearrange("p (j c) -> p j c", c=GRID)
                mid = bias_t[:, head % 2, EDGE:EDGE + MID].rearrange("p (j c) -> p j c", c=GRID)
                steps.run(nc.gpsimd.tensor_scalar(edge, edge, -1.0, None, ALU.mult))
                for r in (0, 64):
                    steps.run(nc.gpsimd.affine_select(
                        out=edge[r:r + 64, :, 0:48], in_=edge[r:r + 64, :, 0:48], compare_op=ALU.is_ge,
                        fill=FAR, base=8, pattern=[[0, 14], [1, 48]], channel_multiplier=-1))
                    steps.run(nc.gpsimd.affine_select(
                        out=edge[r:r + 64, :, 16:64], in_=edge[r:r + 64, :, 16:64], compare_op=ALU.is_ge,
                        fill=FAR, base=7 - 16, pattern=[[0, 14], [-1, 48]], channel_multiplier=1))
                steps.run(nc.gpsimd.tensor_copy(mid, edge[:, 2:11, :]))
                steps.run(nc.gpsimd.memset(mid[0:64, 8, :], FAR))
                nc.gpsimd.memset(mid[64:P, 0, :], FAR).then_inc(s_bias, 1)
                pool.wait_ge(s_bias, head + 1)

            def high(dst, src, n):
                return nc.gpsimd.tensor_tensor(dst, src, ones[:, 0:1].to_broadcast([P, n]), ALU.mult)

            def split_head(head):
                slot = head % 2
                pool.wait_ge(s_hraw, 64 * (head + 1))
                if head >= 2:
                    pool.wait_ge(s_sc, 8 * (head - 1))
                else:
                    pool.wait_ge(s_v, CT)
                high(k_hi[:, slot, :], k_raw[:], KEYS).then_inc(s_hstep, 1)
                high(q_st[:, slot, :], q_raw[:], SEQ).then_inc(s_hstep, 1)
                pool.wait_ge(s_hstep, 3 * head + 2)
                nc.gpsimd.tensor_tensor(k_lo[:, slot, :], k_raw[:], k_hi[:, slot, :], ALU.subtract).then_inc(s_hstep, 1)
                pool.wait_ge(s_hstep, 3 * head + 3)
                nc.gpsimd.tensor_tensor(q_st[64:P, slot, :], q_raw[64:P, :], q_st[64:P, slot, :], ALU.subtract).then_inc(s_hd, 1)
                pool.wait_ge(s_hd, head + 1)

            def split_values(pair):
                slot = pair % 2
                pool.wait_ge(s_vraw, 16 * (pair + 1))
                if pair >= 2:
                    pool.wait_ge(s_pv, 16 * (pair - 1))
                src, hi, lo = (a.rearrange("p t c -> p (t c)") for a in (v_raw[:, :, :], v_hi[:, slot], v_lo[:, slot]))
                steps.run(high(hi, src, KEYS))
                nc.gpsimd.tensor_tensor(lo, src, hi, ALU.subtract).then_inc(s_vp, 1)

            split_head(0)
            build_bias(0)
            split_head(1)
            build_bias(1)
            split_values(0)
            for j in range(3):
                split(U_O + j, j, j % 2, (s_v, V_TILES))
            for head in range(2, HEADS):
                if head % 2 == 0:
                    split_values(head // 2)
                split_head(head)
                build_bias(head)
            split(U_O + 3, 3, 1, (s_pt, TT * HEADS))
            for j in range(4, 2 * FT):
                split(U_O + j, j % 4, j % 2, used_o(j - 4))
            for j in range(6):
                split(U_F0 + j, j, j % 2, used_o(12 + j) if j < 4 else None)
            with pool.Fori(1, ROUNDS) as i:
                for j in range(6):
                    split(6 * i + (U_F0 + j), j, j % 2, used_f(0, i - 1, j))
            for j in range(8):
                split(U_S + j, j % 4, j % 2, used_f(0, ROUNDS - 1, j) if j < 4 else used_s(0, j - 4))
            with pool.Fori(1, FT // 2) as i:
                for j in range(8):
                    split(8 * i + (U_S + j), j % 4, j % 2, used_s(i - 1, j + 4) if j < 4 else used_s(i, j - 4))
            for j in range(6):
                split(U_F1 + j, j, j % 2, used_s(FT // 2 - 1, j + 4) if j < 4 else used_f(0, ROUNDS - 1, j))
            with pool.Fori(1, ROUNDS) as i:
                for j in range(6):
                    split(6 * i + (U_F1 + j), j, j % 2, used_f(1, i - 1, j))

        @block.tensor
        def _(pe):
            def product(dst, w, x_hi, x_lo, first, last):
                w_hi, w_lo = w
                pe.matmul(dst, w_hi, x_hi, start=first, stop=False)
                pe.matmul(dst, w_lo, x_hi, start=False, stop=False)
                return pe.matmul(dst, w_hi, x_lo, start=False, stop=last)

            def columns(dst, slot, a_hi, a_lo, sl, norm=None):
                w_hi, w_lo = w_slot(slot)
                for k in range(FT):
                    if norm is not None:
                        pe.wait_ge(s_norm, 8 * norm + k + 1)
                    w = (w_hi[:, k * P:(k + 1) * P], w_lo[:, k * P:(k + 1) * P])
                    mm = product(dst, w, a_hi[:, k, sl], a_lo[:, k, sl], k == 0, k == FT - 1)
                return mm

            def norm_sum(n):
                pe.wait_ge(s_sum, 8 * (n + 1))
                for j in range(NORMS[n][2] // P):
                    mm = pe.matmul(bank[:, 7, j:j + 1], sumsq[:, j * P:(j + 1) * P], ones[:, 0:1], start=True, stop=True)
                mm.then_inc(s_ss, 1)

            def norm_spread(n):
                pe.wait_ge(s_rstd, n + 1)
                for j in range(NORMS[n][2] // P):
                    mm = pe.matmul(bank[:, SPREAD[n], j * P:(j + 1) * P], ones[:, :], diag[:, j, :], start=True, stop=True)
                mm.then_inc(s_bc, 1)

            def mod_totals(n, acc):
                pe.wait_ge(s_macc, 8 * n + 10)
                for m in range(FT):
                    mm = pe.matmul(bank[:, 7, m:m + 1], acc[:, m * P:(m + 1) * P], ones[:, 0:1], start=True, stop=True)
                mm.then_inc(s_mfin, 1)

            def out_groups(n0, group, norm=None, mod=None):
                for idx in range(16):
                    half, m = divmod(idx, FT)
                    pe.wait_ge(s_hup, n0 + idx + 1)
                    group(half, m, bank[:, 4 + m % 2, :]).then_inc(s_out, 1)
                    if mod is not None and idx == 8:
                        mod_totals(mod, mod_acc_f)
                    if norm is not None and idx == 9:
                        norm_sum(norm)
                    if norm is not None and idx == 11:
                        norm_spread(norm)
                if norm is not None:
                    norm_sum(norm + 1)
                    norm_spread(norm + 1)

            pe.sem_inc(s_modmm, 4)
            pe.sem_inc(s_mfin, 1)
            pe.wait_ge(s_ident, 3)
            pe.wait_ge(s_par, 16 * 12)
            pe.transpose(bank[:, 0, 0:124], par_rows[:], ident[0:124, 0:124])
            pe.transpose(bank[:, 0, 128:224], b_rows[:], ident[0:96, 0:96]).then_inc(s_par_t, 1)
            pe.wait_ge(s_param, 2)
            for tt in range(TT + CT):
                pe.wait_ge(s_x[tt % 2], 16 * (tt // 2 + 1))
                if tt >= 2:
                    pe.wait_ge(s_xpa, tt - 1)
                    pe.wait_ge(s_xpd, tt - 1)
                for f in range(FT):
                    b = 2 * (tt % 2) + f // 4
                    mm = pe.transpose(bank[:, b, (f % 4) * P:(f % 4 + 1) * P], x_in[:, tt % 2, f * P:(f + 1) * P], ident[:])
                    if f % 4 == 3:
                        mm.then_inc(s_turn, 1)

            for n in (0, 1, 2):
                norm_sum(n)
                norm_spread(n)

            pe.wait_ge(s_cond, 2)
            pe.wait_ge(s_xpa, TT + CT)
            pe.wait_ge(s_xpd, TT + CT)
            with pe.Fori(0, 2) as c:
                for k in range(FT):
                    pe.wait_ge(s_mod[k % 4], c * 32 + 16 * (k // 4 + 1))
                    for a in range(2):
                        mm = pe.matmul(bank[0:2, a, :], cond[:, k, :], mod_ring[:, k % 4, a * HALF:(a + 1) * HALF],
                                       start=(k == 0), stop=(k == FT - 1))
                    mm.then_inc(s_modmm, 1)
                pe.wait_ge(s_modrow, 2 * c + 2)
                pe.wait_ge(s_modset, 2 * c + 2)
                alone(pe)
                for m in range(FT):
                    mm = pe.transpose(bank[:, 2, 2 * m:2 * m + 2], mod_row[:, m * P:(m + 1) * P], ident[0:2, 0:2])
                mm.then_inc(s_modt, 1)

            pe.wait_ge(s_modset, 2 + 2 * 2)
            GROUPS = ((0, 0), (0, 1), (0, 2), (1, 0), (1, 1), (2, 0), (2, 1), (2, 2), (3, 0), (3, 1))

            def project_in(i):
                for g, (unit, part) in enumerate(GROUPS):
                    if part == 0:
                        pe.wait_ge(s_split, 4 * i + unit + 1)
                    pe.wait_ge(s_projev, 10 * i + g + 1)
                    if part == 2:
                        mm = columns(bank[:, g % 5, 0:CTX], unit, ctx_hi, ctx_lo, slice(0, CTX), N_CTX)
                    else:
                        mm = columns(bank[:, g % 5, :], unit, act_hi, act_lo, slice(part * HALF, (part + 1) * HALF), part)
                    mm.then_inc(s_proj, 1)

            def gates(i):
                pe.wait_ge(s_conv, i + 2)
                pe.wait_ge(s_gw, i * 128 + 128)
                for g in range(12):
                    lo = (g % 3) * HALF
                    w = min(HALF, KEYS - lo)
                    pe.wait_ge(s_gatev, 12 * i + g + 1)
                    pe.matmul(bank[:, 5 + g % 3, 0:w], gate_w[:, g // 3, :], x_conv[:, lo:lo + w],
                              start=True, stop=True).then_inc(s_gate, 1)

            project_in(0)
            gates(0)
            with pe.Fori(1, LT) as i:
                project_in(i)
                pe.wait_ge(s_gatev, 12 * i + 3)
                mod_totals(i - 1, mod_acc_p)
                pe.wait_ge(s_mset, i)
                gates(i)

            pe.wait_ge(s_projev, 5 + 10 * LT)
            pe.wait_ge(s_split, U_V + 4)
            for n, tt in enumerate(V_ORDER):
                if n >= 4:
                    pe.wait_ge(s_vev, n - 3)
                a_hi, a_lo, c0 = (act_hi, act_lo, tt * P) if tt < TT else (ctx_hi, ctx_lo, (tt - TT) * P)
                for k in range(FT):
                    w_hi, w_lo = w_slot(k // 2)
                    sl = slice((k % 2) * HALF, (k % 2 + 1) * HALF)
                    mm = product(bank[:, n % 4, :], (a_hi[:, k, c0:c0 + P], a_lo[:, k, c0:c0 + P]),
                                 w_hi[:, sl], w_lo[:, sl], k == 0, k == FT - 1)
                mm.then_inc(s_v, 1)
            pe.wait_ge(s_gatev, 3 + 12 * LT)
            mod_totals(LT - 1, mod_acc_p)

            pe.wait_ge(s_vev, V_TILES)

            def scores(i, s):
                hd, b = divmod(s, TT)
                k0, wide = window(b)
                if b == 0:
                    pe.wait_ge(s_hd, 4 * i + hd + 1)
                pe.wait_ge(s_exp, STEPS * i + s + 1)
                o = 2 * (s % 2) * HALF
                q = q_st[:, hd % 2, b * P:(b + 1) * P]
                parts = [(0, CTX + k0, HALF), (MID, 0, CTX)]
                if wide:
                    parts.insert(1, (HALF, CTX + k0 + HALF, MID - HALF))
                for dst, src, n in parts:
                    out_ = bank_f[:, o + dst:o + dst + n]
                    pe.matmul(out_, q, k_hi[:, hd % 2, src:src + n], start=True, stop=False)
                    mm = pe.matmul(out_, q, k_lo[:, hd % 2, src:src + n], start=False, stop=True)
                mm.then_inc(s_sc, 1)

            def turn_probs(i, s):
                wide = window(s % TT)[1]
                pe.wait_ge(s_pn, STEPS * i + s + 1)
                pe.wait_ge(s_ptl, STEPS * i + s + 1)
                for c in range(4):
                    pe.transpose(bank_f[:, 4 * HALF + c * P:4 * HALF + (c + 1) * P], probs[s % 4][:, c * P:(c + 1) * P], ident[:])
                if wide:
                    pe.transpose(bank_f[0:64, 5 * HALF + 2 * P:5 * HALF + 3 * P], probs[s % 4][:, HALF:MID], ident[:])
                for c in range(2):
                    mm = pe.transpose(bank_f[:, 5 * HALF + c * P:5 * HALF + (c + 1) * P],
                                      probs[s % 4][:, MID + c * P:MID + (c + 1) * P], ident[:])
                mm.then_inc(s_pt, 1)

            def values(i, s):
                hd, b = divmod(s, TT)
                k0, wide = window(b)
                slot = hd // 2
                pe.wait_ge(s_ptl, STEPS * i + s + 2)
                if s % (2 * TT) == 0:
                    pe.wait_ge(s_vp, 2 * i + slot + 1)
                if s % 4 == 0:
                    pe.wait_ge(s_yl, (STEPS // 4) * i + s // 4 + 1)
                chunks = [(c, k0 // P + c, P) for c in range(4)] + [(4 + c, TT + c, P) for c in range(CT)]
                if wide:
                    chunks.append((6, k0 // P + 4, 64))
                dst = bank[:, 6 + (s // 4) % 2, (s % 4) * P:(s % 4 + 1) * P]
                for n, (c, tile, rows) in enumerate(chunks):
                    mm = product(dst, (v_hi[0:rows, slot, tile, :], v_lo[0:rows, slot, tile, :]), pt_hi[0:rows, s % 2, c, :],
                                 pt_lo[0:rows, s % 2, c, :], n == 0, n == len(chunks) - 1)
                mm.then_inc(s_pv, 1)

            with pe.Fori(0, 2) as i:
                for j in range(-1, STEPS + 4):
                    if 0 <= j - 3 < STEPS:
                        turn_probs(i, j - 3)
                    if j + 1 < STEPS:
                        scores(i, j + 1)
                    if j >= 4:
                        values(i, j - 4)

            pe.wait_ge(s_yll, LT)
            pe.wait_ge(s_yl, 2 + TT * HEADS // 4)

            def project_out(half, m, dst):
                pe.wait_ge(s_split, U_O + half * FT + m + 1)
                return columns(dst, m % 4, act_hi, act_lo, slice(half * HALF, (half + 1) * HALF))

            out_groups(0, project_out, N_F0)

            def ffn_round(layer, i, u0, norm_in, norm_out=None, mod=None):
                q0 = 4 * ROUNDS * layer
                for q in range(4):
                    half, tile = divmod(q, 2)
                    pe.wait_ge(s_hidf, 4 * i + (q0 + q + 1))
                    for a in range(2):
                        if half == 0:
                            pe.wait_ge(s_split, 6 * i + (u0 + 2 * tile + a + 1))
                        columns(bank[:, 2 * tile + a, :], 2 * tile + a, act_hi, act_lo,
                                slice(half * HALF, (half + 1) * HALF), norm_in + half).then_inc(s_gu, 1)

                def down(half, m, dst):
                    if m == 0:
                        pe.wait_ge(s_split, 6 * i + (u0 + 6))
                        pe.wait_ge(s_hid, 4 * i + (q0 + 2 * half + 2))
                    sl = slice(half * HALF, (half + 1) * HALF)
                    for k in range(2):
                        w_hi, w_lo = w_slot(4 + k)
                        w = (w_hi[:, m * P:(m + 1) * P], w_lo[:, m * P:(m + 1) * P])
                        mm = product(dst, w, hid_hi[:, k, sl], hid_lo[:, k, sl], k == 0, k == 1)
                    return mm

                out_groups(16 * i + OUT_F[layer], down, norm_out, mod)

            with pe.Fori(0, MODS) as i:
                ffn_round(0, i, U_F0, N_F0, mod=i + LT)
            with pe.Fori(MODS, ROUNDS - 1) as i:
                ffn_round(0, i, U_F0, N_F0)
            ffn_round(0, ROUNDS - 1, U_F0, N_F0, N_S)

            def short_round(i, norm_out=None):
                for tile in range(2):
                    n = 4 * i + 2 * tile
                    for g, (unit, half) in enumerate(((0, 0), (1, 0), (0, 1), (1, 1), (2, 0), (2, 1))):
                        if half == 0:
                            pe.wait_ge(s_split, 8 * i + (U_S + 3 * tile + unit + 1))
                        if g < 2:
                            pe.wait_ge(s_zf, n + g + 1)
                        elif g == 4:
                            pe.wait_ge(s_cg, n + 1)
                        elif g == 5:
                            pe.wait_ge(s_t, n + 1)
                        columns(bank[:, g % 4, :], (3 * tile + unit) % 4, act_hi, act_lo,
                                slice(half * HALF, (half + 1) * HALF), N_S + half).then_inc(s_sg, 1)

                def down(half, m, dst):
                    if m == 0:
                        pe.wait_ge(s_split, 8 * i + (U_S + 8))
                        pe.wait_ge(s_z, 4 * i + half + 3)
                    sl = slice(half * HALF, (half + 1) * HALF)
                    for k in range(2):
                        w_hi, w_lo = w_slot(2 + k)
                        w = (w_hi[:, m * P:(m + 1) * P], w_lo[:, m * P:(m + 1) * P])
                        mm = product(dst, w, z_hi[:, k, sl], z_lo[:, k, sl], k == 0, k == 1)
                    return mm

                out_groups(16 * i + OUT_S, down, norm_out)

            pe.wait_ge(s_hidf, 2 + 4 * ROUNDS)
            with pe.Fori(0, FT // 2 - 1) as i:
                short_round(i)
            short_round(FT // 2 - 1, N_F1)

            pe.wait_ge(s_zf, 2 + 2 * FT)
            with pe.Fori(0, ROUNDS - 1) as i:
                ffn_round(1, i, U_F1, N_F1)
            ffn_round(1, ROUNDS - 1, U_F1, N_F1, N_END)

            pe.wait_ge(s_hidf, 2 + 8 * ROUNDS)
            for tt in range(TT):
                if tt % 4 == 0:
                    pe.wait_ge(s_fin, FT * (tt // 4 + 1))
                if tt >= 2:
                    pe.wait_ge(s_fra, tt - 1)
                    pe.wait_ge(s_frd, tt - 1)
                for f in range(FT):
                    b = 2 * (tt % 2) + f // 4
                    mm = pe.transpose(bank[:, b, (f % 4) * P:(f % 4 + 1) * P], fin[:, f, tt * P:(tt + 1) * P], ident[:])
                    if f % 4 == 3:
                        mm.then_inc(s_fturn, 1)

        @block.scalar
        def _(act):
            def square(n, f, ready=None):
                src, half, w, *_ = NORMS[n]
                if ready is not None:
                    act.wait_ge(*ready)
                if 8 * n + f >= 2:
                    act.wait_ge(s_sum, 8 * n + f - 1)
                nc.scalar.activation(sq[:, f % 2, 0:w], src[:, f, cols(n)], ACT.Square).then_inc(s_sq, 1)

            def rms(n):
                act.wait_ge(s_ss, n + 1)
                nc.scalar.activation(std[:, 0, 0:NORMS[n][2] // P], bank[:, 7, 0:NORMS[n][2] // P], ACT.Sqrt,
                                     bias=eps_t[:, 0:1], scale=1.0 / D).then_inc(s_sqrt, 1)

            def modulate(n, f):
                _, half, w, gain, shift, which = NORMS[n]
                act.wait_ge(s_scal, 8 * n + f + 1)
                if gain is None:
                    nc.scalar.activation(fin[:, f, cols(n)], scaled[:, f % 2, 0:w], ACT.Identity,
                                         scale=par[:, PAR["nf"] + f:PAR["nf"] + f + 1]).then_inc(s_fin, 1)
                    return
                if 8 * n + f >= 2:
                    act.wait_ge(s_norm, 8 * n + f - 1)
                g, b = gains[:, gain, f:f + 1], shift[:, which, f:f + 1]
                nc.scalar.activation(normed[:, f % 2, 0:w], scaled[:, f % 2, 0:w], ACT.Identity, bias=b, scale=g).then_inc(s_nf, 1)
                dst = (ctx_hi if n == N_CTX else act_hi)[:, f, cols(n)]
                nc.scalar.activation(dst, scaled[:, f % 2, 0:w], ACT.Identity, bias=b, scale=g).then_inc(s_nhi, 1)

            def norm_pair(n, n0):
                for f in range(FT):
                    square(n, f, (s_hup, n0 + f + 3))
                rms(n)
                for f in range(2):
                    square(n + 1, f, (s_hup, n0 + FT + f + 3))
                for f in range(FT):
                    modulate(n, f)
                    if f + 2 < FT:
                        square(n + 1, f + 2, (s_hup, n0 + FT + f + 5))
                rms(n + 1)
                for f in range(FT):
                    modulate(n + 1, f)

            act.sem_inc(s_projev, 5)
            act.sem_inc(s_gatev, 3)
            act.sem_inc(s_exp, 2)
            act.sem_inc(s_qk, 16)

            def load_x(tt):
                src = x[0, tt * P:(tt + 1) * P, :] if tt < TT else context[0, (tt - TT) * P:(tt - TT + 1) * P, :]
                act.dma_start(x_in[:, tt % 2, :], src).then_inc(s_x[tt % 2], 16)

            load_x(0)
            load_x(1)
            act.wait_ge(s_param, 1)
            for j in range(2):
                nc.scalar.activation(cond[:, :, j], par[:, PAR["c"] + j * FT:PAR["c"] + (j + 1) * FT], ACT.Silu).then_inc(s_cond, 1)
            for tt in range(TT + CT):
                dst = h[:, 0:4, tt * P:(tt + 1) * P] if tt < TT else ctx_t[:, 0:4, (tt - TT) * P:(tt - TT + 1) * P]
                act.wait_ge(s_turn, 2 * tt + 1)
                nc.scalar.copy(dst, bank[:, 2 * (tt % 2), :].rearrange("p (f c) -> p f c", c=P)).then_inc(s_xpa, 1)
                if tt + 2 < TT + CT:
                    act.wait_ge(s_turn, 2 * tt + 2)
                    load_x(tt + 2)
            act.wait_ge(s_xpa, TT + CT)
            act.wait_ge(s_xpd, TT + CT)
            act.dma_start(h_spill, h[:, :, :]).then_inc(s_spill, 16)

            act.wait_ge(s_const, 1)
            nc.scalar.activation(sp_t[:, 1, :], sp_t[:, 0, :], ACT.Exp, scale=-1.0).then_inc(s_act, 1)

            act.wait_ge(s_rpb, 48)
            for n in (0, 1, 2):
                for f in range(FT):
                    square(n, f)
                rms(n)

            with act.Fori(0, 2) as c:
                act.wait_ge(s_modmm, c * FT + (4 + FT))
                for a in range(2):
                    nc.scalar.copy(mod_row[:, a * HALF:(a + 1) * HALF], bank[0:2, a, :]).then_inc(s_modrow, 1)

            act.wait_ge(s_const, 2)
            for n in (0, 1, 2):
                for f in range(FT):
                    modulate(n, f)

            act.wait_ge(s_spill, 16)
            act.wait_ge(s_norm, 8 * (N_CTX + 1))
            act.wait_ge(s_const, 3)
            with act.Fori(0, LT) as i:
                def out_of(g):
                    act.wait_ge(s_proj, 10 * i + g + 1)

                act.wait_ge(s_conv, i + 1)
                for g, (dst, w) in enumerate(((CTX + 5, HALF), (CTX + 5 + HALF, HALF), (2, CTX))):
                    out_of(g)
                    nc.scalar.copy(x_pad[:, dst:dst + w], bank[:, g % 5, 0:w]).then_inc(s_projev, 1)
                act.wait_ge(s_qk, 80 * i + 16)
                for g in range(3, 8):
                    out_of(g)
                    w = CTX if g == 7 else HALF
                    nc.scalar.activation(qk_out[:, g - 3, 0:w], bank[:, g % 5, 0:w], ACT.Copy,
                                         scale=-(64 ** -0.5) if g < 5 else 1.0).then_inc(s_projev, 1)
                    act.wait_ge(s_projev, 10 * i + (5 + g + 1))
                    alone(act)
                    dst = (q_spill[bass.ds(i, 1), :, (g - 3) * HALF:(g - 2) * HALF] if g < 5 else
                           k_spill[bass.ds(i, 1), :, 0:CTX] if g == 7 else
                           k_spill[bass.ds(i, 1), :, CTX + (g - 5) * HALF:CTX + (g - 4) * HALF])
                    act.dma_start(dst.rearrange("a p n -> p (a n)"), qk_out[:, g - 3, 0:w]).then_inc(s_qk, 16)
                act.wait_ge(s_lru, i + 1)
                for g in (8, 9):
                    out_of(g)
                    nc.scalar.activation(g_gelu[:, (g - 8) * HALF:(g - 7) * HALF], bank[:, g % 5, :],
                                         ACT.Gelu_apprx_tanh).then_inc(s_projev, 1)
                for g in range(12):
                    m, lo = g // 3, (g % 3) * HALF
                    w = min(HALF, KEYS - lo)
                    act.wait_ge(s_gate, 12 * i + g + 1)
                    alone(act)
                    nc.scalar.activation((lru_i if m % 2 else lru_r)[:, m // 2, lo:lo + w], bank[:, 5 + g % 3, 0:w], ACT.Tanh,
                                         bias=half_b[:, bass.ds(i + (m % 2 * 8 + m // 2 * LT), 1)], scale=0.5).then_inc(s_gatev, 1)
                act.wait_ge(s_gatev, 12 * i + 15)
                act.wait_ge(s_rfree, i + 1)
                alone(act)
                for d in range(2):
                    sp = sp2[:, bass.ds(i + d * LT, 1)]
                    nc.scalar.activation(lru_q[:, d, :], lru_r[:, d, :], ACT.Tanh, bias=sp, scale=sp).then_inc(s_s, 1)
                for d in range(2):
                    sp = sp4[:, bass.ds(i + d * LT, 1)]
                    nc.scalar.activation(lru_r[:, d, :], lru_r[:, d, :], ACT.Exp, bias=sp, scale=sp).then_inc(s_s, 1)
                act.wait_ge(s_s, 4 * i + 4)
                alone(act)
                for d in range(2):
                    nc.scalar.activation(lru_q[:, d, :], lru_q[:, d, :], ACT.Sqrt).then_inc(s_rs, 1)

            act.wait_ge(s_qk, 16 + 80 * LT)
            for n, tt in enumerate(V_ORDER):
                act.wait_ge(s_v, n + 1)
                nc.scalar.copy(v_tok[:, tt, :], bank[:, n % 4, :]).then_inc(s_vev, 1)
                act.wait_ge(s_vev, n + 1)
                act.dma_start(v_spill[:, tt, :], v_tok[:, tt, :]).then_inc(s_vst, 16)

            for j in range(LT):
                act.wait_ge(s_rin[j % 2], 16 * (j // 2 + 1))
                nc.scalar.copy(act_hi[:, LT + j, :], r_in[:, j % 2, :]).then_inc(s_ylh, 1)

            act.wait_ge(s_yll, LT)

            def exps(i, s):
                w = MID if window(s % TT)[1] else HALF
                o = 2 * (s % 2) * HALF
                st = stat[:, s % 4, :]
                act.wait_ge(s_min, STEPS * i + s + 1)
                nc.scalar.activation(probs[s % 4][:, 0:w], probs[s % 4][:, 0:w], ACT.Exp, bias=st[:, 1:2], scale=-1.0,
                                     accum_out=st[:, 2:3])
                nc.scalar.activation(probs[s % 4][:, MID:WIDE], bank_f[:, o + MID:o + WIDE], ACT.Exp, bias=st[:, 1:2],
                                     scale=-1.0, accum_out=st[:, 3:4]).then_inc(s_exp, 1)

            def turned_high(i, s):
                act.wait_ge(s_pt, STEPS * i + s + 1)
                nc.scalar.copy(pt_hi[:, s % 2, 0:4, :].rearrange("p c n -> p (c n)"), bank[:, 4, :]).then_inc(s_pth, 1)
                if window(s % TT)[1]:
                    nc.scalar.copy(pt_hi[0:64, s % 2, 6, :], bank[0:64, 5, 2 * P:3 * P])
                nc.scalar.copy(pt_hi[:, s % 2, 4:6, :].rearrange("p c n -> p (c n)"), bank[:, 5, 0:2 * P]).then_inc(s_pth, 1)

            def y_high(i, s):
                hd, q = s // TT, (s // 4) % 2
                rows = slice(64 * (hd % 2), 64 * (hd % 2) + 64)
                act.wait_ge(s_pv, STEPS * i + s + 1)
                alone(act)
                nc.scalar.copy(act_hi[rows, bass.ds(2 * i + hd // 2, 1), q * HALF:(q + 1) * HALF].rearrange("p a n -> p (a n)"),
                               bank[rows, 6 + q, :]).then_inc(s_yh, 1)

            with act.Fori(0, 2) as i:
                for j in range(STEPS + 4):
                    if 0 <= j - 3 < STEPS:
                        turned_high(i, j - 3)
                    if j < STEPS:
                        exps(i, j)
                    if j >= 4 and (j - 4) % 4 == 3:
                        y_high(i, j - 4)

            act.wait_ge(s_const, 4)
            norm_pair(N_F0, 0)

            def ffn_round(layer, i):
                q0 = 4 * ROUNDS * layer
                for q in range(4):
                    half, tile = divmod(q, 2)
                    act.wait_ge(s_gu, 8 * i + (2 * q0 + 2 * q + 1))
                    act.wait_ge(s_hidf, 4 * i + (q0 + q + 1))
                    nc.scalar.activation(silu_g[:, q % 2, :], bank[:, 2 * tile, :], ACT.Silu).then_inc(s_silu, 1)
                    act.wait_ge(s_hidf, 4 * i + (q0 + q + 3))
                    nc.scalar.copy(hid_hi[:, tile, half * HALF:(half + 1) * HALF], hid_f[:, q % 2, :]).then_inc(s_hidh, 1)

            with act.Fori(0, ROUNDS - 1) as i:
                ffn_round(0, i)
            ffn_round(0, ROUNDS - 1)
            act.wait_ge(s_const, 5)
            norm_pair(N_S, OUT_F[0] + 16 * (ROUNDS - 1))

            def short_round(i):
                for tile in range(2):
                    n = 4 * i + 2 * tile
                    for half in range(2):
                        act.wait_ge(s_sg, 12 * i + (6 * tile + 2 * half + 1))
                        nc.scalar.copy(cg_sb[:, half, :], bank[:, 2 * half, :]).then_inc(s_cg, 1)
                    for half in range(2):
                        act.wait_ge(s_zf, n + half + 3)
                        nc.scalar.copy(z_hi[:, tile, half * HALF:(half + 1) * HALF], z_f[:, half, :]).then_inc(s_zh, 1)

            with act.Fori(0, FT // 2 - 1) as i:
                short_round(i)
            short_round(FT // 2 - 1)
            norm_pair(N_F1, OUT_S + 16 * (FT // 2 - 1))

            with act.Fori(0, ROUNDS - 1) as i:
                ffn_round(1, i)
            ffn_round(1, ROUNDS - 1)
            norm_pair(N_END, OUT_F[1] + 16 * (ROUNDS - 1))

            for tt in range(TT):
                act.wait_ge(s_fturn, 2 * tt + 1)
                if tt >= 2:
                    act.wait_ge(s_store[tt % 2], 16 * (tt // 2))
                nc.scalar.copy(fin_rows[:, tt % 2, 0:HALF], bank[:, 2 * (tt % 2), :]).then_inc(s_fra, 1)

        @block.vector
        def _(dve):
            steps = Steps(dve, s_dve)
            V = nc.vector

            def add_squares(n, f):
                w = NORMS[n][2]
                dve.wait_ge(s_sq, 8 * n + f + 1)
                if f == 0:
                    if n:
                        dve.wait_ge(s_ss, n)
                    V.tensor_copy(sumsq[:, 0:w], sq[:, 0, 0:w]).then_inc(s_sum, 1)
                else:
                    dve.wait_ge(s_sum, 8 * n + f)
                    V.tensor_tensor(sumsq[:, 0:w], sumsq[:, 0:w], sq[:, f % 2, 0:w], ALU.add).then_inc(s_sum, 1)

            def inverse_rms(n):
                dve.wait_ge(s_sqrt, n + 1)
                if n:
                    dve.wait_ge(s_bc, n)
                w = NORMS[n][2] // P
                steps.run(V.reciprocal(std[:, 1, 0:w], std[:, 0, 0:w]))
                for j in range(w):
                    last = V.tensor_scalar(diag[:, j, :], ident[:], std[:, 1, j:j + 1], None, ALU.mult)
                last.then_inc(s_rstd, 1)

            def scale(n, f):
                src, half, w, gain, *_ = NORMS[n]
                dve.wait_ge(s_bc, n + 1)
                if n == N_END + 1 and f < 2 or n == N_END and f >= 2 or n == N_END + 1:
                    dve.wait_ge(s_fin, 8 * (n - N_END) + f - 1)
                elif 8 * n + f >= 2 :
                    dve.wait_ge(s_nhi, 8 * n + f - 1)
                V.tensor_tensor(scaled[:, f % 2, 0:w], src[:, f, cols(n)], bank[:, SPREAD[n], 0:w], ALU.mult).then_inc(s_scal, 1)

            def low(n, f):
                w, gain = NORMS[n][2:4]
                if gain is None:
                    return
                dve.wait_ge(s_nhi, 8 * n + f + 1)
                a_hi, a_lo = (ctx_hi, ctx_lo) if n == N_CTX else (act_hi, act_lo)
                V.tensor_tensor(a_lo[:, f, cols(n)], normed[:, f % 2, 0:w], a_hi[:, f, cols(n)], ALU.subtract).then_inc(s_norm, 1)

            def apply_norm(n, between=lambda f: None):
                scale(n, 0)
                scale(n, 1)
                for f in range(FT):
                    low(n, f)
                    if f + 2 < FT:
                        scale(n, f + 2)
                    between(f)

            def update(n0, idx, gate):
                half, m = divmod(idx, FT)
                dve.wait_ge(s_out, n0 + idx + 1)
                dst = h[:, m, half * HALF:(half + 1) * HALF]
                V.scalar_tensor_tensor(out=dst, in0=bank[:, 4 + m % 2, :], scalar=mods[:, gate, m:m + 1], in1=dst,
                                       op0=ALU.mult, op1=ALU.add).then_inc(s_hup, 1)

            def mod_unit(n, k, ring, acc):
                dve.wait_ge(s_mu[k % 2], 64 * n + 16 * (k // 2 + 1))
                if k == 0:
                    dve.wait_ge(s_mfin, n + 1)
                    ins = V.tensor_scalar(acc[:], ring[:, 0, :], cond[:, 0, 0:1], None, ALU.mult)
                else:
                    dve.wait_ge(s_macc, 8 * n + (k + 2))
                    ins = V.scalar_tensor_tensor(out=acc[:], in0=ring[:, k % 2, :], scalar=cond[:, k, 0:1], in1=acc[:],
                                                 op0=ALU.mult, op1=ALU.add)
                ins.then_inc(s_macc, 1)

            def mod_set(n, row):
                dve.wait_ge(s_mfin, n + 2)
                V.tensor_tensor(mods[:, bass.ds(row, 1), :].rearrange("p a f -> p (a f)"), bank[:, 7, 0:FT],
                                mod_bias[:, bass.ds(row, 1), :].rearrange("p a f -> p (a f)"), ALU.add).then_inc(s_mset, 1)

            def set_gains(*sets):
                for k, src, which, g in sets:
                    last = V.scalar_tensor_tensor(out=gains[:, k, :], in0=src[:, which, :], scalar=1.0, in1=par[:, g:g + FT],
                                                  op0=ALU.add, op1=ALU.mult)
                last.then_inc(s_const, 1)

            def last_updates(n0, gate, n):
                for f in range(FT):
                    if n == N_F0 and f in (0, 3, 6):
                        dve.wait_ge(s_reload[f // 3], 16)
                    update(n0, f, gate)
                    if f:
                        add_squares(n, f - 1)
                add_squares(n, FT - 1)
                update(n0, FT, gate)
                update(n0, FT + 1, gate)
                inverse_rms(n)
                update(n0, FT + 2, gate)
                add_squares(n + 1, 0)
                add_squares(n + 1, 1)

                def between(f):
                    if f + 3 < FT:
                        update(n0, FT + f + 3, gate)
                    if f + 2 < FT:
                        add_squares(n + 1, f + 2)

                apply_norm(n, between)
                inverse_rms(n + 1)
                apply_norm(n + 1)

            for s, credits in ((s_conv, 1), (s_lru, 1), (s_modset, 2), (s_macc, 2), (s_ptl, 1), (s_yl, 2), (s_hup, 2),
                               (s_hidf, 2), (s_zf, 2)):
                dve.sem_inc(s, credits)

            dve.wait_ge(s_par_t, 1)
            V.tensor_copy(par[:], bank[:, 0, 0:124]).then_inc(s_param, 1)
            V.tensor_copy(mod_bias[:, :, :].rearrange("p a f -> p (a f)"), bank[:, 0, 128:224]).then_inc(s_param, 1)
            for tt in range(TT + CT):
                dst = h[:, 4:8, tt * P:(tt + 1) * P] if tt < TT else ctx_t[:, 4:8, (tt - TT) * P:(tt - TT + 1) * P]
                dve.wait_ge(s_turn, 2 * tt + 2)
                V.tensor_copy(dst, bank[:, 2 * (tt % 2) + 1, :].rearrange("p (f c) -> p f c", c=P)).then_inc(s_xpd, 1)
            dve.wait_ge(s_param, 2)
            lam = par[:, PAR["lam"]:PAR["lam"] + 8]
            steps.run(V.tensor_scalar(sp_t[:, 2, :], lam, -1.0, None, ALU.mult))
            V.tensor_tensor(sp_t[:, 0, :], sp_t[:, 2, :], lam, ALU.max).then_inc(s_const, 1)
            steps.run(V.tensor_scalar(half_b[:], par[:, PAR["br"]:PAR["br"] + 16], 0.5, None, ALU.mult))
            for n in (0, 1, 2):
                for f in range(FT):
                    add_squares(n, f)
                inverse_rms(n)
            with dve.Fori(0, 2) as c:
                dve.wait_ge(s_modt, c + 1)
                summed = bank[:, 2, 0:2 * FT].rearrange("p (m j) -> p m j", j=2)
                for j, dst in enumerate((mods, mods_ctx)):
                    V.tensor_tensor(dst[:, bass.ds(c, 1), :].rearrange("p a f -> p (a f)"), summed[:, :, j],
                                    mod_bias[:, bass.ds(c, 1), :].rearrange("p a f -> p (a f)"), ALU.add).then_inc(s_modset, 1)
            dve.wait_ge(s_modset, 2 + 2 * 2)
            set_gains((0, mods, SC1, PAR["n1"]), (1, mods_ctx, SC1, PAR["n1"]))
            for n in (0, 1, 2):
                apply_norm(n)

            dve.wait_ge(s_act, 1)
            e, y, y2, acc = (sp_t[:, k, :] for k in (1, 3, 4, 0))
            steps.run(V.tensor_scalar(y2, e, 2.0, None, ALU.add))
            steps.run(V.reciprocal(y, y2))
            steps.run(V.tensor_tensor(y, e, y, ALU.mult))
            steps.run(V.tensor_tensor(y2, y, y, ALU.mult))
            steps.run(V.tensor_scalar(acc, y2, 1.0 / 17, 1.0 / 15, ALU.mult, ALU.add))
            for k in (13, 11, 9, 7, 5, 3, 1):
                steps.run(V.tensor_tensor(acc, acc, y2, ALU.mult))
                steps.run(V.tensor_scalar(acc, acc, 1.0 / k, None, ALU.add))
            steps.run(V.tensor_tensor(acc, acc, y, ALU.mult))
            steps.run(V.tensor_scalar(sp_t[:, 2, :], sp_t[:, 2, :], 0.0, 2.0, ALU.max, ALU.mult))
            steps.run(V.scalar_tensor_tensor(out=sp2[:], in0=acc, scalar=4.0, in1=sp_t[:, 2, :], op0=ALU.mult, op1=ALU.add))
            V.tensor_scalar(sp4[:], sp2[:], -2.0, None, ALU.mult).then_inc(s_const, 1)

            def convolve(i):
                dve.wait_ge(s_projev, 10 * i + 8)
                for j in range(4):
                    w = par[:, bass.ds(i + (PAR["conv_w"] + j * LT), 1)]
                    for part, (src, dst, n) in enumerate(((0, 0, CTX), (CTX + 3, CTX, SEQ))):
                        win, xc = x_pad[:, src + j:src + j + n], x_conv[:, dst:dst + n]
                        if j == 0:
                            ins = V.tensor_scalar(xc, win, w, par[:, bass.ds(i + PAR["conv_b"], 1)], ALU.mult, ALU.add)
                        else:
                            ins = V.scalar_tensor_tensor(out=xc, in0=win, scalar=w, in1=xc, op0=ALU.mult, op1=ALU.add)
                        if part:
                            ins.then_inc(s_conv, 1) if j == 3 else steps.run(ins)

            def recur(i):
                for k in range(2):
                    mod_unit(i, k, mod_in_p, mod_acc_p)
                for d in range(2):
                    R, I, Q = lru_r[:, d, :], lru_i[:, d, :], lru_q[:, d, :]
                    dve.wait_ge(s_gatev, 12 * i + (3 + 6 * (d + 1)))
                    dve.wait_ge(s_conv, i + 2)
                    V.scalar_tensor_tensor(out=I, in0=I, scalar=1.0, in1=x_conv[:], op0=ALU.add, op1=ALU.mult)
                    dve.wait_ge(s_rs, 2 * i + d + 1)
                    steps.run(V.scalar_tensor_tensor(out=Q, in0=R, scalar=1.0, in1=Q, op0=ALU.add, op1=ALU.mult))
                    steps.run(V.tensor_tensor(I, I, Q, ALU.mult))
                    if d == 0:
                        steps.run(V.tensor_tensor_scan(Q, R, I, 0.0, ALU.mult, ALU.add))
                    else:
                        rev, lat = slice(CTX - 1, None, -1), slice(KEYS - 1, CTX - 1, -1)
                        steps.run(V.tensor_tensor_scan(Q[:, rev], R[:, rev], I[:, rev], 0.0, ALU.mult, ALU.add))
                        steps.run(V.tensor_tensor_scan(Q[:, lat], R[:, lat], I[:, lat], Q[:, 0:1], ALU.mult, ALU.add))
                    for k in range(3 * d + 2, 3 * d + 5):
                        mod_unit(i, k, mod_in_p, mod_acc_p)
                steps.run(V.tensor_tensor(lru_i[:, 0, 0:SEQ], lru_q[:, 0, CTX:], lru_q[:, 1, CTX:], ALU.add))
                dve.wait_ge(s_projev, 10 * i + 15)
                V.scalar_tensor_tensor(out=lru_q[:, 0, 0:SEQ], in0=lru_i[:, 0, 0:SEQ], scalar=0.5, in1=g_gelu[:],
                                       op0=ALU.mult, op1=ALU.mult).then_inc(s_lru, 1)

            dve.wait_ge(s_pad, 3)
            convolve(0)
            recur(0)
            with dve.Fori(1, LT) as i:
                steps.begin_loop(i - 1, 11)
                convolve(i)
                mod_set(i - 1, i + 1)
                recur(i)
            steps.end_loop(LT - 1)
            mod_set(LT - 1, LT + 1)
            dve.wait_ge(s_mset, LT)
            set_gains((2, mods, SC2, PAR["n2"]))

            dve.wait_ge(s_v, V_TILES)
            for j in range(LT):
                dve.wait_ge(s_ylh, j + 1)
                V.tensor_tensor(act_lo[:, LT + j, :], r_in[:, j % 2, :], act_hi[:, LT + j, :], ALU.subtract).then_inc(s_yll, 1)
            dve.wait_ge(s_yll, LT)

            def min_logit(i, s):
                hd, b = divmod(s, TT)
                k0, wide = window(b)
                w = MID if wide else HALF
                o = 2 * (s % 2) * HALF
                at0 = EDGE if wide else (k0 - 2 * b * GRID) + 6 * GRID
                st = stat[:, s % 4, :]
                if b == 0:
                    dve.wait_ge(s_bias, 4 * i + hd + 1)
                dve.wait_ge(s_sc, STEPS * i + s + 1)
                steps.run(V.tensor_reduce(st[:, 0:1], bank_f[:, o + MID:o + WIDE], AX_X, ALU.min))
                alone(dve)
                V.tensor_tensor_reduce(out=probs[s % 4][:, 0:w], in0=bank_f[:, o:o + w], in1=bias_t[:, hd % 2, at0:at0 + w],
                                       scale=1.0, scalar=st[:, 0:1], op0=ALU.add, op1=ALU.min, accum_out=st[:, 1:2]
                                       ).then_inc(s_min, 1)

            def normalize(i, s):
                st = stat[:, s % 4, :]
                dve.wait_ge(s_exp, STEPS * i + s + 3)
                steps.run(V.tensor_tensor(st[:, 4:5], st[:, 2:3], st[:, 3:4], ALU.add))
                steps.run(V.reciprocal(st[:, 5:6], st[:, 4:5]))
                parts = ((0, WIDE),) if window(s % TT)[1] else ((0, HALF), (MID, WIDE))
                for lo, hi in parts:
                    last = V.tensor_scalar(probs[s % 4][:, lo:hi], probs[s % 4][:, lo:hi], st[:, 5:6], None, ALU.mult)
                last.then_inc(s_pn, 1)

            def turned_low(i, s):
                parts = [(slice(0, P), slice(0, 4), bank[:, 4, :])]
                if window(s % TT)[1]:
                    parts.append((slice(0, 64), slice(6, 7), bank[0:64, 5, 2 * P:3 * P]))
                parts.append((slice(0, P), slice(4, 6), bank[:, 5, 0:2 * P]))
                for n, (rows, chunks, src) in enumerate(parts):
                    if n < 2:
                        dve.wait_ge(s_pth, 2 * STEPS * i + (2 * s + n + 1))
                    hi, lo = (a[rows, s % 2, chunks, :].rearrange("p c n -> p (c n)") for a in (pt_hi, pt_lo))
                    last = V.tensor_tensor(lo, src, hi, ALU.subtract)
                last.then_inc(s_ptl, 1)

            def y_low(i, s):
                hd, q = s // TT, (s // 4) % 2
                rows = slice(64 * (hd % 2), 64 * (hd % 2) + 64)
                tile = (rows, bass.ds(2 * i + hd // 2, 1), slice(q * HALF, (q + 1) * HALF))
                dve.wait_ge(s_yh, (STEPS // 4) * i + s // 4 + 1)
                V.tensor_tensor(act_lo[tile].rearrange("p a n -> p (a n)"), bank[rows, 6 + q, :],
                                act_hi[tile].rearrange("p a n -> p (a n)"), ALU.subtract).then_inc(s_yl, 1)

            with dve.Fori(0, 2) as i:
                steps.begin_loop(i, 3 * STEPS)
                for j in range(STEPS + 5):
                    if j < STEPS:
                        min_logit(i, j)
                    if 0 <= j - 1 < STEPS:
                        normalize(i, j - 1)
                    if j >= 5 and (j - 5) % 4 == 3:
                        y_low(i, j - 5)
                    if 0 <= j - 3 < STEPS:
                        turned_low(i, j - 3)
            steps.end_loop(2)

            last_updates(0, G1, N_F0)

            def hidden(layer, i, mod=None):
                q0 = 4 * ROUNDS * layer
                for q in range(4):
                    half, tile = divmod(q, 2)
                    dve.wait_ge(s_silu, 4 * i + (q0 + q + 1))
                    dve.wait_ge(s_gu, 8 * i + (2 * q0 + 2 * q + 2))
                    V.tensor_tensor(hid_f[:, q % 2, :], silu_g[:, q % 2, :], bank[:, 2 * tile + 1, :], ALU.mult).then_inc(s_hidf, 1)
                    dve.wait_ge(s_hidh, 4 * i + (q0 + q + 1))
                    sl = slice(half * HALF, (half + 1) * HALF)
                    V.tensor_tensor(hid_lo[:, tile, sl], hid_f[:, q % 2, :], hid_hi[:, tile, sl], ALU.subtract).then_inc(s_hid, 1)
                    if mod is not None:
                        for k in (2 * q, 2 * q + 1):
                            mod_unit(mod, k, mod_in_f, mod_acc_f)

            def ffn(layer, norm):
                first = 0 if layer else MODS
                with dve.Fori(first, ROUNDS - 1) as i:
                    hidden(layer, i)
                    for idx in range(16):
                        update(16 * i + OUT_F[layer], idx, MODS * layer + G2)
                hidden(layer, ROUNDS - 1)
                last_updates(OUT_F[layer] + 16 * (ROUNDS - 1), MODS * layer + G2, norm)

            with dve.Fori(0, MODS) as i:
                hidden(0, i, LT + i)
                for idx in range(16):
                    update(16 * i + OUT_F[0], idx, G2)
                    if idx == 9:
                        mod_set(i + LT, i + MODS)
            dve.wait_ge(s_mset, LT + MODS)
            set_gains((3, mods, MODS + SC1, PAR["n1"] + FT), (4, mods, MODS + SC2, PAR["n2"] + FT))
            ffn(0, N_S)

            for lo in (0, SEQ + 1):
                V.memset(t_pad[:, lo:lo + 1], 0.0).then_inc(s_tz, 1)
            dve.wait_ge(s_tz, 2)

            def short(i):
                for tile in range(2):
                    n, g = 4 * i + 2 * tile, 12 * i + 6 * tile
                    for half in range(2):
                        dve.wait_ge(s_cg, n + half + 1)
                        dve.wait_ge(s_sg, g + (2 * half + 2))
                        V.tensor_tensor(t_pad[:, 1 + half * HALF:1 + (half + 1) * HALF], cg_sb[:, half, :],
                                        bank[:, 2 * half + 1, :], ALU.mult).then_inc(s_t, 1)
                    dve.wait_ge(s_t, n + 2)
                    for j in range(3):
                        w = par[:, bass.ds(2 * i + (PAR["short_w"] + j * FT + tile), 1)]
                        if j == 0:
                            steps.run(V.tensor_scalar(conv_t[:], t_pad[:, 0:SEQ], w, None, ALU.mult))
                        else:
                            steps.run(V.scalar_tensor_tensor(out=conv_t[:], in0=t_pad[:, j:j + SEQ], scalar=w, in1=conv_t[:],
                                                             op0=ALU.mult, op1=ALU.add))
                    for half in range(2):
                        sl = slice(half * HALF, (half + 1) * HALF)
                        dve.wait_ge(s_sg, g + (5 + half))
                        V.tensor_tensor(z_f[:, half, :], conv_t[:, sl], bank[:, half, :], ALU.mult).then_inc(s_zf, 1)
                        dve.wait_ge(s_zh, n + half + 1)
                        V.tensor_tensor(z_lo[:, tile, sl], z_f[:, half, :], z_hi[:, tile, sl], ALU.subtract).then_inc(s_z, 1)

            with dve.Fori(0, FT // 2 - 1) as i:
                steps.begin_loop(i, 6)
                short(i)
                for idx in range(16):
                    update(16 * i + OUT_S, idx, MODS + G1)
            steps.end_loop(FT // 2 - 1)
            short(FT // 2 - 1)
            last_updates(OUT_S + 16 * (FT // 2 - 1), MODS + G1, N_F1)

            ffn(1, N_END)

            for tt in range(TT):
                dve.wait_ge(s_fturn, 2 * tt + 2)
                if tt >= 2:
                    dve.wait_ge(s_store[tt % 2], 16 * (tt // 2))
                V.tensor_copy(fin_rows[:, tt % 2, HALF:D], bank[:, 2 * (tt % 2) + 1, :]).then_inc(s_frd, 1)


INPUTS = ("x", "c", "ctx", "c_ctx", "mod_w", "mod_b", "norm1_g", "norm2_g", "ffn_w_gu", "ffn_w_down", "e_w_in",
          "e_w_out", "e_conv_w", "e_conv_b", "e_lru_wr", "e_lru_br", "e_lru_wi", "e_lru_bi", "e_lru_lam", "e_rpb",
          "o_w_in", "o_conv_w", "o_w_out", "final_g")


def kernel(**inputs):
    import numpy as np
    import concourse.bacc as bacc
    from concourse.bass_utils import run_bass_kernel_spmd

    nc = bacc.Bacc("TRN2", target_bir_lowering=False, num_devices=1)
    arrays, tensors = {}, {}
    for name in INPUTS:
        a = np.ascontiguousarray(inputs[name])
        arrays["in_" + name] = a
        tensors[name] = nc.dram_tensor("in_" + name, a.shape, F32, kind="ExternalInput").ap()
    tensors["out"] = nc.dram_tensor("out", inputs["x"].shape, F32, kind="ExternalOutput").ap()
    backbone(nc, tensors)
    result = run_bass_kernel_spmd(nc, [arrays], core_ids=[0])
    return result.results[0]["out"]
```

```python
from contextlib import ExitStack

import concourse.bass as bass
from concourse import mybir

ALU = mybir.AluOpType
ACT = mybir.ActivationFunctionType
AX_X = mybir.AxisListType.X
F32 = mybir.dt.float32
F32R = mybir.dt.float32r

P = 128
EPS = 1e-6
FAR = 1e30
GRID = 64
HALF = 512
UNIT = 1024


class Steps:

    def __init__(self, eng, sem):
        self.eng, self.sem, self.n, self.base = eng, sem, 0, 0

    def run(self, ins):
        ins.then_inc(self.sem, 1)
        self.n += 1
        self.eng.wait_ge(self.sem, self.base + self.n)

    def begin_loop(self, i, per):
        self.start, self.base, self.per = self.n, i * per, per

    def end_loop(self, rounds):
        assert self.n - self.start == self.per, (self.n - self.start, self.per)
        self.n, self.base = self.start + rounds * self.per, 0


def backbone(nc, t):
    x, context, out = t["x"], t["ctx"], t["out"]
    _, SEQ, D = x.shape
    CTX = context.shape[1]
    FT = D // P
    TT = SEQ // P
    CT = CTX // P
    KEYS = CTX + SEQ
    LT = t["e_conv_b"].shape[1] // P
    HID = t["ffn_w_down"].shape[1]
    ROUNDS = HID // (2 * P)
    _, HEADS, NR, NC = t["e_rpb"].shape
    MODS = 6
    SH1, SC1, G1, SH2, SC2, G2 = range(MODS)
    assert (SEQ, D, CTX, LT, HEADS, NR, NC) == (2 * HALF, 1024, 256, 4, 8, 15, 31)

    es = ExitStack()
    with es:
        def sem(name):
            return es.enter_context(nc.semaphore(name))

        def keep(name, shape, dt=F32):
            return es.enter_context(nc.sbuf_tensor(name, shape, dt))

        def at(kb, name, shape, dt=F32):
            with ExitStack() as s:
                if kb:
                    s.enter_context(nc.sbuf_tensor("below_" + name, [P, int(kb * 256)], F32))
                return s.enter_context(nc.sbuf_tensor(name, shape, dt))

        h_spill = nc.dram_tensor("h_spill", (P, FT, SEQ), F32, kind="Internal").ap()
        q_spill = nc.dram_tensor("q_spill", (LT, P, SEQ), F32, kind="Internal").ap()
        k_spill = nc.dram_tensor("k_spill", (LT, P, KEYS), F32, kind="Internal").ap()
        v_spill = nc.dram_tensor("v_spill", (P, TT + CT, LT * P), F32, kind="Internal").ap()
        r_spill = nc.dram_tensor("r_spill", (LT, P, SEQ), F32, kind="Internal").ap()
        PAD = 64
        RPB = HEADS * NR * NC
        rpb_pad = nc.dram_tensor("rpb_pad", (1, PAD + RPB + PAD), F32, kind="Internal").ap()
        rpb_wide = nc.dram_tensor("rpb_wide", (HEADS, NR, GRID, GRID), F32, kind="Internal").ap()

        probs_w = [at(64 + 12 + 16 * j, f"probs{j + 2}", [P, 832]) for j in range(2)]
        r_in = [at(64 + 8 + 16 * j, f"r_in{j}", [P, UNIT]) for j in range(2)]
        stat = at(64 + 12 + 3.25, "stat", [P, 4, 6])
        pt_lo = [at(64 + 16 * j, f"pt_lo{j}", [P, 8, 2, P], F32R) for j in range(2)]
        act_hi = keep("act_hi", [P, FT, SEQ], F32R)
        mod_ring = at(0, "mod_ring", [P, 4, UNIT])
        mod_row = at(16, "mod_row", [2, 2, UNIT])
        act_lo = keep("act_lo", [P, FT, SEQ], F32R)
        w_hi4 = keep("w_hi4", [P, 4, UNIT], F32R)
        w_lo4 = keep("w_lo4", [P, 4, UNIT], F32R)
        raw = keep("raw", [P, 2, UNIT])
        ident = keep("ident", [P, P])
        ones = keep("ones", [P, P])
        mod_bias = keep("mod_bias", [P, 2 * MODS, FT])
        mods = keep("mods", [P, 2 * MODS, FT])
        mods_ctx = keep("mods_ctx", [P, 2, FT])
        par = keep("par", [P, 124])
        cond = keep("cond", [P, FT, 2])
        gains = keep("gains", [P, 5, FT])
        half_b = keep("half_b", [P, 16])
        sp2 = keep("sp2", [P, 8])
        sp4 = keep("sp4", [P, 8])
        sp_t = keep("sp_t", [P, 5, 8])
        eps_t = keep("eps_t", [P, 1])
        std = keep("std", [P, 2, 4])
        fin_scale = keep("fin_scale", [P, TT])

        h = at(0, "h", [P, FT, SEQ])
        w_hi2 = at(32, "w_hi2", [P, 2, UNIT], F32R)
        w_lo2 = at(40, "w_lo2", [P, 2, UNIT], F32R)
        sq = at(48, "sq", [P, 2, HALF])
        sumsq = at(52, "sumsq", [P, HALF])
        diag = at(54, "diag", [P, 4, P])
        scaled = at(56, "scaled", [P, 2, HALF])
        normed = at(60, "normed", [P, 2, HALF])
        x_in = at(32, "x_in", [P, TT + CT, D])
        ctx_t = at(72, "ctx_t", [P, FT, CTX])
        par_rows = at(80, "par_rows", [124, P])
        b_rows = at(80.5, "b_rows", [96, P])
        zero_row = at(81, "zero_row", [1, PAD])
        hid_hi = at(64, "hid_hi", [P, 2, SEQ], F32R)
        hid_lo = at(72, "hid_lo", [P, 2, SEQ], F32R)
        silu_g = at(80, "silu_g", [P, 2, HALF])
        hid_f = at(84, "hid_f", [P, 2, HALF])
        mod_in_f = at(88, "mod_in_f", [P, 2, UNIT])
        mod_acc_f = at(60, "mod_acc_f", [P, UNIT])
        z_hi = at(64, "z_hi", [P, 2, SEQ], F32R)
        z_lo = at(72, "z_lo", [P, 2, SEQ], F32R)
        cg_sb = at(80, "cg_sb", [P, 2, HALF])
        conv_t = at(84, "conv_t", [P, SEQ])
        z_f = at(88, "z_f", [P, 2, HALF])
        t_pad = at(92, "t_pad", [P, SEQ + 2])
        gain_diag = at(60, "gain_diag", [P, FT, P])
        fin_rows = at(88, "fin_rows", [P, 2, D])
        lru_r = at(0, "lru_r", [P, 2, KEYS])
        lru_i = at(10, "lru_i", [P, 2, KEYS])
        lru_q = at(20, "lru_q", [P, 2, KEYS])
        gate_w = at(30, "gate_w", [P, 4, P])
        mod_in_p = at(32, "mod_in_p", [P, 2, UNIT])
        mod_acc_p = at(44, "mod_acc_p", [P, UNIT])
        g_gelu = at(40, "g_gelu", [P, SEQ])
        qk_out = at(48, "qk_out", [P, 5, HALF])
        v_tok = at(48, "v_tok", [P, TT + CT, LT * P])
        x_pad = at(68, "x_pad", [P, KEYS + 6])
        x_conv = at(73.5, "x_conv", [P, KEYS])
        ctx_hi = at(80, "ctx_hi", [P, FT, CTX], F32R)
        ctx_lo = at(88, "ctx_lo", [P, FT, CTX], F32R)
        EDGE = 14 * GRID
        MID = 9 * GRID
        WIDE = MID + CTX
        assert WIDE == 832 and WIDE <= UNIT
        k_raw = at(0, "k_raw", [P, KEYS])
        q_raw = at(5, "q_raw", [P, SEQ])
        v_raw = at(9, "v_raw", [P, TT + CT, P])
        bias_t = at(14, "bias_t", [P, 2, EDGE + MID])
        probs = [at(25.5 + 3.25 * j, f"probs{j}", [P, WIDE]) for j in range(2)] + probs_w
        pt_hi = [at(32 + 8 * j, f"pt_hi{j}", [P, 8, 2, P], F32R) for j in range(2)]
        inv_diag = at(96, "inv_diag", [P, 4, P])
        v_hi = at(48, "v_hi", [P, 2, TT + CT, P], F32R)
        v_lo = at(58, "v_lo", [P, 2, TT + CT, P], F32R)
        q_st = at(68, "q_st", [P, 2, SEQ], F32R)
        k_hi = at(76, "k_hi", [P, 2, KEYS], F32R)
        k_lo = at(86, "k_lo", [P, 2, KEYS], F32R)

        bank = es.enter_context(nc.psum_tensor("bank", [P, 8, HALF], F32))
        bank_f = bank[:, :, :].rearrange("p b n -> p (b n)")

        def w_slot(s):
            return (w_hi4[:, s, :], w_lo4[:, s, :]) if s < 4 else (w_hi2[:, s - 4, :], w_lo2[:, s - 4, :])

        U_P = 0
        U_V = U_P + 4 * LT
        U_O = U_V + 4
        U_F0 = U_O + 2 * FT
        U_S = U_F0 + 6 * ROUNDS
        U_F1 = U_S + 4 * FT
        U_END = U_F1 + 6 * ROUNDS

        s_par, s_ident, s_turn, s_par_t = sem("par_landed"), sem("ident_made"), sem("x_turned"), sem("par_turned")
        s_cond, s_param = sem("cond_ready"), sem("par_placed")
        s_x = [sem(f"x_landed{j}") for j in range(TT + CT)]
        s_xpa, s_xpd = sem("x_placed_by_act"), sem("x_placed_by_dve")
        s_mod = [sem(f"mod_landed{j}") for j in range(4)]
        s_modmm, s_modrow, s_modt, s_modset = sem("mod_summed"), sem("mod_row_ready"), sem("mod_turned"), sem("mod_set")
        s_mu = (sem("mod_unit_landed0"), sem("mod_unit_landed1"))
        s_macc, s_mfin, s_mset = sem("mod_unit_added"), sem("mod_totals_ready"), sem("mod_vector_set")
        s_const = sem("constants_ready")
        s_raw = (sem("raw_landed0"), sem("raw_landed1"))
        s_hi, s_split = sem("unit_hi"), sem("unit_split")
        s_sq, s_sum, s_ss, s_sqrt, s_rstd = sem("squared"), sem("summed"), sem("sumsq_in_psum"), sem("rms_ready"), sem("diag_ready")
        s_bc, s_scal, s_nhi, s_norm = sem("rstd_spread"), sem("scaled_ready"), sem("normed_hi"), sem("norm_done")
        s_spill, s_reload = sem("h_spilled"), [sem(f"h_reloaded{j}") for j in range(3)]
        s_proj, s_projev = sem("proj_done"), sem("proj_evacuated")
        s_qk = sem("qk_stored")
        s_pad, s_conv = sem("pads_zero"), sem("x_convolved")
        s_gw, s_gwz = sem("gate_w_landed"), sem("gate_w_zero")
        s_gate, s_gatev = sem("gate_done"), sem("gate_evacuated")
        s_s, s_rs, s_lru = sem("decay_ready"), sem("root_ready"), sem("lru_done")
        s_rfree = sem("lru_result_free")
        s_rst, s_rin = sem("lru_stored"), (sem("lru_reloaded0"), sem("lru_reloaded1"))
        s_v, s_vev = sem("v_done"), sem("v_evacuated")
        s_ylh, s_yll = sem("lru_hi"), sem("lru_lo")
        s_rpb, s_zero = sem("rpb_padded"), sem("zero_row_ready")
        s_wide = sem("bias_widened")
        s_braw = sem("bias_landed")
        s_bias = sem("bias_built")
        s_bstep = sem("pool_step")
        s_vst, s_vraw, s_vp = sem("v_stored"), sem("v_landed"), sem("v_split")
        s_hraw, s_hd, s_hstep = sem("qk_landed"), sem("qk_split"), sem("qk_hi")
        s_sc, s_min, s_exp = sem("scores_done"), sem("min_ready"), sem("probs_ready")
        s_pn, s_pt = sem("inverse_sum_ready"), sem("probs_turned")
        s_pth, s_ptl = sem("turned_hi"), sem("turned_lo")
        s_pv, s_yh, s_yl = sem("pv_done"), sem("y_hi"), sem("y_lo")
        s_out, s_hup = sem("out_done"), sem("h_updated")
        s_gu, s_silu, s_hidf = sem("gate_up_done"), sem("silu_ready"), sem("hidden_ready")
        s_hidh, s_hid = sem("hidden_hi"), sem("hidden_split")
        s_sg, s_cg, s_t = sem("short_done"), sem("cg_ready"), sem("t_ready")
        s_zf, s_zh, s_z = sem("z_ready"), sem("z_hi_ready"), sem("z_split")
        s_tz, s_gdiag = sem("t_pads_zero"), sem("gain_diag_ready")
        s_fscale, s_fturn, s_store = sem("fin_scale_ready"), sem("fin_turned"), (sem("stored0"), sem("stored1"))
        s_fra, s_frd = sem("fin_row_by_act"), sem("fin_row_by_dve")
        s_dve, s_act = sem("dve_step"), sem("exp_ready")
        s_alone = sem("waits_alone")

        def alone(eng):
            eng.sem_inc(s_alone, 1)

        NORMS = ([(h, 0, HALF, 0, mods, SH1), (h, 1, HALF, 0, mods, SH1), (ctx_t, 0, CTX, 1, mods_ctx, SH1)]
                 + [(h, a, HALF, 2, mods, SH2) for a in (0, 1)]
                 + [(h, a, HALF, 3, mods, MODS + SH1) for a in (0, 1)]
                 + [(h, a, HALF, 4, mods, MODS + SH2) for a in (0, 1)]
                 + [(h, a, HALF, None, None, None) for a in (0, 1)])
        N_X, N_CTX, N_F0, N_S, N_F1, N_END = 0, 2, 3, 5, 7, 9

        def cols(n):
            a, half, w, *_ = NORMS[n]
            return slice(half * HALF, half * HALF + w)

        SPREAD = (6, 5, 7) + (6,) * 8

        PAR = dict(n1=0, n2=16, nf=32, conv_w=40, conv_b=56, br=60, bi=68, lam=76, short_w=84, c=108)

        def window(b):
            lo = [min(max(r - 4, 0), SEQ // GRID - 8) for r in (2 * b, 2 * b + 1)]
            return lo[0] * GRID, lo[0] != lo[1]

        V_TILES = TT + CT
        V_ORDER = list(range(TT, V_TILES)) + list(range(TT))
        STEPS = TT * HEADS // 2

        def chunks(s):
            first = window(s % TT)[0] // P
            base = window(s % TT - s % 2)[0] // P
            return first - base, base

        GROUPS = ((0, 0), (1, 0), (0, 1), (1, 1), (0, 2), (2, 0), (2, 1), (2, 2), (3, 0), (3, 1))

        def used_p(i, j):
            return s_proj, 10 * i + (5, 4, 8, 10)[j]

        def used_o(j):
            return s_out, j + 1

        def used_f(layer, i, j):
            if j < 4:
                return s_gu, 8 * ROUNDS * layer + 8 * i + 5 + j
            return s_out, OUT_F[layer] + 16 * i + 16

        def used_s(i, j):
            return (s_sg, 12 * i + (3, 4, 6, 9, 10, 12)[j]) if j < 6 else (s_out, OUT_S + 16 * i + 16)

        OUT_F = (2 * FT, 2 * FT + 16 * (ROUNDS + FT // 2))
        OUT_S = 2 * FT + 16 * ROUNDS

        block = es.enter_context(nc.Block())

        @block.sync
        def _(sp):
            w_in, w_out = t["e_w_in"][0], t["e_w_out"][0]
            AW = LT * P

            def load_unit(u, parity, src):
                if not isinstance(u, int) or u >= 2:
                    sp.wait_ge(s_split, u - 1)
                    if not isinstance(u, int):
                        alone(sp)
                dst = raw[:, parity, :]
                if len(src.shape) == 3:
                    dst = dst.rearrange("p (k m) -> p k m", k=src.shape[1])
                sp.dma_start(dst, src).then_inc(s_raw[parity], 16)

            def column_unit(w, col):
                return w[:, bass.ds(col, P)].rearrange("(k p) m -> p k m", p=P)

            r = 0
            for src in (t["norm1_g"].rearrange("l (r c) -> (l r) c", c=P),
                        t["norm2_g"].rearrange("l (r c) -> (l r) c", c=P),
                        t["final_g"].rearrange("(r c) -> r c", c=P),
                        t["e_conv_w"][0].rearrange("j (r c) -> (j r) c", c=P),
                        t["e_conv_b"][0].rearrange("(r c) -> r c", c=P),
                        t["e_lru_br"][0].rearrange("d (r c) -> (d r) c", c=P),
                        t["e_lru_bi"][0].rearrange("d (r c) -> (d r) c", c=P),
                        t["e_lru_lam"][0].rearrange("d (r c) -> (d r) c", c=P),
                        t["o_conv_w"][0].rearrange("j (r c) -> (j r) c", c=P),
                        t["c"][0].rearrange("(r c) -> r c", c=P),
                        t["c_ctx"].rearrange("(r c) -> r c", c=P)):
                sp.dma_start(par_rows[r:r + src.shape[0], :], src).then_inc(s_par, 16)
                r += src.shape[0]
            assert r == 124
            sp.dma_start(b_rows[:], t["mod_b"].rearrange("l (r c) -> (l r) c", c=P)).then_inc(s_par, 16)

            order_p = (3 * AW, 0, AW, 4 * AW)
            for j in range(2):
                load_unit(j, j, column_unit(w_in, order_p[j]))
            sp.wait_ge(s_zero, 1)
            sp.dma_start(rpb_pad[0:1, 0:PAD], zero_row[:]).then_inc(s_rpb, 16)
            sp.dma_start(rpb_pad[0:1, PAD + RPB:], zero_row[:]).then_inc(s_rpb, 16)
            sp.dma_start(rpb_pad[0:1, PAD:PAD + RPB], t["e_rpb"].rearrange("a h r c -> a (h r c)")).then_inc(s_rpb, 16)

            for j in range(2, 4):
                load_unit(j, j % 2, column_unit(w_in, order_p[j]))

            mod_w = t["mod_w"].rearrange("l (k p) (w n) -> l w k p n", p=P, n=UNIT)
            for c in range(2):
                for k in range(FT):
                    sp.wait_ge(s_modmm, c * FT + k + 1)
                    sp.dma_start(mod_ring[:, k % 4, :], mod_w[0, c, k]).then_inc(s_mod[k % 4], 16)

            def load_mod(ring, layer, which, n, k):
                sp.wait_ge(s_macc, 8 * n + (k + 1))
                if not isinstance(n, int):
                    alone(sp)
                sp.dma_start(ring[:, k % 2, :], mod_w[layer, bass.ds(which, 1), k].rearrange("a p n -> p (a n)")).then_inc(s_mu[k % 2], 16)

            for head in range(HEADS):
                src = bass.AP(tensor=rpb_pad.tensor, offset=PAD + head * NR * NC + NC // 2, ap=[[NC, NR], [-1, GRID], [1, GRID]])
                if head == 0:
                    sp.wait_ge(s_rpb, 48)
                sp.dma_start(rpb_wide[head], src).then_inc(s_wide, 16)

            def load_gates(i):
                for d in range(2):
                    for g, w in enumerate((t["e_lru_wr"], t["e_lru_wi"])):
                        for a in range(2):
                            sp.dma_start(gate_w[64 * a:64 * a + 64, 2 * d + g, 64 * a:64 * a + 64],
                                         w[0, d, bass.ds(2 * i + a, 1)].rearrange("a p n -> p (a n)")).then_inc(s_gw, 16)

            def load_mod_p(n, k):
                load_mod(mod_in_p, 0, n + 2, n, k)

            sp.wait_ge(s_gwz, 1)
            load_gates(0)
            with sp.Fori(1, LT) as i:
                for j in range(4):
                    load_unit(4 * i + j, j % 2, column_unit(w_in, i * P + order_p[j]))
                    for k in (2 * j, 2 * j + 1):
                        load_mod_p(i - 1, k)
                sp.wait_ge(s_gate, i * 12)
                alone(sp)
                load_gates(i)
            wv = w_in.rearrange("(k p) n -> p k n", p=P)
            for j in range(4):
                load_unit(U_V + j, j % 2, wv[:, 2 * j:2 * j + 2, 2 * AW:3 * AW])
            for k in range(FT):
                load_mod_p(LT - 1, k)

            def load_bias(head):
                for a in range(2):
                    sp.dma_start(bias_t[64 * a:64 * a + 64, head % 2, 0:EDGE].rearrange("p (j c) -> p j c", c=GRID),
                                 rpb_wide[head, 1 - a:15 - a].rearrange("j c k -> c j k")).then_inc(s_braw, 16)

            def load_head(head):
                pair, hh = divmod(head, 2)
                for a in range(2):
                    half = slice(64 * a, 64 * a + 64)
                    sp.dma_start(k_raw[half, :], k_spill[pair, 64 * hh:64 * hh + 64, :]).then_inc(s_hraw, 16)
                    sp.dma_start(q_raw[half, :], q_spill[pair, 64 * hh:64 * hh + 64, :]).then_inc(s_hraw, 16)

            def load_values(pair):
                sp.dma_start(v_raw[:], v_spill[:, :, pair * P:(pair + 1) * P]).then_inc(s_vraw, 16)

            for j in range(2):
                load_unit(U_O + j, j % 2, column_unit(w_out, j * P))
            sp.wait_ge(s_wide, 16 * HEADS)
            sp.wait_ge(s_qk, 16 + 80 * LT)
            sp.wait_ge(s_rfree, 1 + LT)
            load_head(0)
            load_bias(0)
            sp.wait_ge(s_hd, 1)
            load_head(1)
            sp.wait_ge(s_vst, 16 * (TT + CT))
            load_values(0)
            sp.wait_ge(s_bias, 1)
            load_bias(1)
            sp.wait_ge(s_v, V_TILES)
            for j in range(2):
                sp.dma_start(r_in[j][:], r_spill[j]).then_inc(s_rin[j], 16)
            for head in range(2, HEADS):
                if head % 2 == 0:
                    sp.wait_ge(s_vp, head // 2)
                    load_values(head // 2)
                sp.wait_ge(s_hd, head)
                load_head(head)
                sp.wait_ge(s_min, 8 * (head - 1))
                sp.wait_ge(s_bias, head)
                load_bias(head)
                if head in (3, 4):
                    sp.wait_ge(s_yll, head - 2)
                    sp.dma_start(r_in[head - 3][:], r_spill[head - 1]).then_inc(s_rin[head - 3], 16)
            sp.wait_ge(s_hd, HEADS)
            sp.wait_ge(s_vp, LT)
            sp.dma_start(h[:, 0:3, :], h_spill[:, 0:3, :]).then_inc(s_reload[0], 16)
            sp.wait_ge(s_min, TT * HEADS)
            sp.dma_start(h[:, 3:6, :], h_spill[:, 3:6, :]).then_inc(s_reload[1], 16)
            sp.wait_ge(s_pt, 2 * TT * HEADS)
            sp.dma_start(h[:, 6:8, :], h_spill[:, 6:8, :]).then_inc(s_reload[2], 16)
            for j in range(2, 2 * FT):
                load_unit(U_O + j, j % 2, column_unit(w_out, (j % FT) * P))

            def ffn_loads(layer, u0, i, mod=None):
                gu, down = t["ffn_w_gu"][layer], t["ffn_w_down"][layer]
                for j, off in enumerate((0, HID, P, HID + P)):
                    load_unit(6 * i + (u0 + j), j % 2, column_unit(gu, i * (2 * P) + off))
                    if mod is not None:
                        for k in (2 * j, 2 * j + 1):
                            load_mod(mod_in_f, 1, mod, mod + LT, k)
                for j in range(2):
                    load_unit(6 * i + (u0 + 4 + j), j % 2, down[bass.ds(i * (2 * P) + j * P, P), :])

            ffn_loads(0, U_F0, 0)
            with sp.Fori(1, 1 + MODS) as i:
                ffn_loads(0, U_F0, i, i - 1)
            with sp.Fori(1 + MODS, ROUNDS) as i:
                ffn_loads(0, U_F0, i)
            with sp.Fori(0, FT // 2) as i:
                for j, off in enumerate((D, 2 * D, 0, D + P, 2 * D + P, P)):
                    load_unit(8 * i + (U_S + j), j % 2, column_unit(t["o_w_in"][0], i * (2 * P) + off))
                for j in range(2):
                    load_unit(8 * i + (U_S + 6 + j), j % 2, t["o_w_out"][0][bass.ds(i * (2 * P) + j * P, P), :])
            with sp.Fori(0, ROUNDS) as i:
                ffn_loads(1, U_F1, i)

            for tt in range(TT):
                sp.wait_ge(s_fra, tt + 1)
                sp.wait_ge(s_frd, tt + 1)
                sp.dma_start(out[0, tt * P:(tt + 1) * P, :], fin_rows[:, tt % 2, :]).then_inc(s_store[tt % 2], 16)
            for tt in range(2):
                sp.wait_ge(s_store[tt], 16 * TT // 2)

        @block.gpsimd
        def _(pool):
            steps = Steps(pool, s_bstep)
            steps.run(nc.gpsimd.memset(ident[:], 0.0))
            nc.gpsimd.affine_select(out=ident[:], in_=ident[:], compare_op=ALU.not_equal, fill=1.0, base=0,
                                    pattern=[[-1, P]], channel_multiplier=1).then_inc(s_ident, 1)
            nc.gpsimd.memset(eps_t[:], EPS).then_inc(s_ident, 1)
            nc.gpsimd.memset(ones[:], 1.0).then_inc(s_ident, 1)
            nc.gpsimd.memset(zero_row[:], 0.0).then_inc(s_zero, 1)
            pool.sem_inc(s_rfree, 1)
            pool.wait_ge(s_ident, 3)

            def split(u, slot, parity, free=None):
                w_hi, w_lo = w_slot(slot)
                pool.wait_ge(s_raw[parity], 8 * u + (16 - 8 * parity))
                if free is not None:
                    pool.wait_ge(*free)
                nc.gpsimd.tensor_tensor(w_hi, raw[:, parity, :], ones[:, 0:1].to_broadcast([P, UNIT]),
                                        ALU.mult).then_inc(s_hi, 1)
                pool.wait_ge(s_hi, u + 1)
                nc.gpsimd.tensor_tensor(w_lo, raw[:, parity, :], w_hi, ALU.subtract).then_inc(s_split, 1)

            def store_lru(i):
                pool.wait_ge(s_lru, i + 2)
                nc.gpsimd.dma_start(r_spill[i], lru_q[:, 0, 0:SEQ]).then_inc(s_rst, 16)
                pool.wait_ge(s_rst, 16 * (i + 1))
                pool.sem_inc(s_rfree, 1)

            for j in range(4):
                split(j, j, j % 2)
            pool.wait_ge(s_spill, 16)
            pool.wait_ge(s_norm, 8 * (N_CTX + 1))
            nc.gpsimd.memset(gate_w[:], 0.0).then_inc(s_gwz, 1)
            for lo, w in ((0, 2), (CTX + 2, 3), (KEYS + 5, 1)):
                nc.gpsimd.memset(x_pad[:, lo:lo + w], 0.0).then_inc(s_pad, 1)
            for i in range(1, LT):
                for j in range(4):
                    split(4 * i + j, j, j % 2, used_p(i - 1, j))
                    if j == 1 and i >= 2:
                        store_lru(i - 2)
            for j in range(4):
                split(U_V + j, j, j % 2, used_p(LT - 1, j))
                if j == 1:
                    store_lru(LT - 2)
            store_lru(LT - 1)

            def build_bias(head):
                pool.wait_ge(s_braw, 32 * (head + 1))
                edge = bias_t[:, head % 2, 0:EDGE].rearrange("p (j c) -> p j c", c=GRID)
                mid = bias_t[:, head % 2, EDGE:EDGE + MID].rearrange("p (j c) -> p j c", c=GRID)
                steps.run(nc.gpsimd.tensor_scalar(edge, edge, -1.0, None, ALU.mult))
                for r in (0, 64):
                    steps.run(nc.gpsimd.affine_select(
                        out=edge[r:r + 64, :, 0:48], in_=edge[r:r + 64, :, 0:48], compare_op=ALU.is_ge,
                        fill=FAR, base=8, pattern=[[0, 14], [1, 48]], channel_multiplier=-1))
                    steps.run(nc.gpsimd.affine_select(
                        out=edge[r:r + 64, :, 16:64], in_=edge[r:r + 64, :, 16:64], compare_op=ALU.is_ge,
                        fill=FAR, base=7 - 16, pattern=[[0, 14], [-1, 48]], channel_multiplier=1))
                steps.run(nc.gpsimd.tensor_copy(mid, edge[:, 2:11, :]))
                steps.run(nc.gpsimd.memset(mid[0:64, 8, :], FAR))
                nc.gpsimd.memset(mid[64:P, 0, :], FAR).then_inc(s_bias, 1)
                pool.wait_ge(s_bias, head + 1)

            def high(dst, src, n):
                return nc.gpsimd.tensor_tensor(dst, src, ones[:, 0:1].to_broadcast([P, n]), ALU.mult)

            def split_head(head):
                slot = head % 2
                pool.wait_ge(s_hraw, 64 * (head + 1))
                if head >= 2:
                    pool.wait_ge(s_sc, 8 * (head - 1))
                else:
                    pool.wait_ge(s_v, CT)
                high(k_hi[:, slot, :], k_raw[:], KEYS).then_inc(s_hstep, 1)
                high(q_st[:, slot, :], q_raw[:], SEQ).then_inc(s_hstep, 1)
                pool.wait_ge(s_hstep, 3 * head + 2)
                nc.gpsimd.tensor_tensor(k_lo[:, slot, :], k_raw[:], k_hi[:, slot, :], ALU.subtract).then_inc(s_hstep, 1)
                pool.wait_ge(s_hstep, 3 * head + 3)
                nc.gpsimd.tensor_tensor(q_st[64:P, slot, :], q_raw[64:P, :], q_st[64:P, slot, :], ALU.subtract).then_inc(s_hd, 1)
                pool.wait_ge(s_hd, head + 1)

            def split_values(pair):
                slot = pair % 2
                pool.wait_ge(s_vraw, 16 * (pair + 1))
                if pair >= 2:
                    pool.wait_ge(s_pv, 8 * (pair - 1))
                src, hi, lo = (a.rearrange("p t c -> p (t c)") for a in (v_raw[:, :, :], v_hi[:, slot], v_lo[:, slot]))
                steps.run(high(hi, src, KEYS))
                nc.gpsimd.tensor_tensor(lo, src, hi, ALU.subtract).then_inc(s_vp, 1)

            split_head(0)
            build_bias(0)
            split_values(0)
            split_head(1)
            build_bias(1)
            def split_lru(j):
                pool.wait_ge(s_rin[j % 2], 16 * (j // 2 + 1))
                high(act_hi[:, LT + j, :], r_in[j % 2][:], SEQ).then_inc(s_ylh, 1)
                pool.wait_ge(s_ylh, j + 1)
                nc.gpsimd.tensor_tensor(act_lo[:, LT + j, :], r_in[j % 2][:], act_hi[:, LT + j, :], ALU.subtract).then_inc(s_yll, 1)

            for head in range(2, HEADS):
                if head % 2 == 0:
                    split_values(head // 2)
                split_head(head)
                build_bias(head)
                if head < 6:
                    split_lru(head - 2)
            split(U_O, 2, 0)
            split(U_O + 1, 3, 1, (s_pt, 2 * TT * HEADS))
            for j in range(2, 4):
                split(U_O + j, j - 2, j % 2, (s_pv, TT * HEADS // 2))
            for j in range(4, 2 * FT):
                split(U_O + j, (j + 2) % 4, j % 2, used_o(j - 4))
            for j in range(6):
                split(U_F0 + j, j, j % 2, used_o(12 + (j + 2) % 4) if j < 4 else None)
            with pool.Fori(1, ROUNDS) as i:
                for j in range(6):
                    split(6 * i + (U_F0 + j), j, j % 2, used_f(0, i - 1, j))
            for j in range(8):
                split(U_S + j, j % 4, j % 2, used_f(0, ROUNDS - 1, j) if j < 4 else used_s(0, j - 4))
            with pool.Fori(1, FT // 2) as i:
                for j in range(8):
                    split(8 * i + (U_S + j), j % 4, j % 2, used_s(i - 1, j + 4) if j < 4 else used_s(i, j - 4))
            for j in range(6):
                split(U_F1 + j, j, j % 2, used_s(FT // 2 - 1, j + 4) if j < 4 else used_f(0, ROUNDS - 1, j))
            with pool.Fori(1, ROUNDS) as i:
                for j in range(6):
                    split(6 * i + (U_F1 + j), j, j % 2, used_f(1, i - 1, j))

        @block.tensor
        def _(pe):
            def product(dst, w, x_hi, x_lo, first, last):
                w_hi, w_lo = w
                pe.matmul(dst, w_hi, x_hi, start=first, stop=False)
                pe.matmul(dst, w_lo, x_hi, start=False, stop=False)
                return pe.matmul(dst, w_hi, x_lo, start=False, stop=last)

            def columns(dst, slot, a_hi, a_lo, sl, norm=None):
                w_hi, w_lo = w_slot(slot)
                for k in range(FT):
                    if norm is not None:
                        pe.wait_ge(s_norm, 8 * norm + k + 1)
                    w = (w_hi[:, k * P:(k + 1) * P], w_lo[:, k * P:(k + 1) * P])
                    mm = product(dst, w, a_hi[:, k, sl], a_lo[:, k, sl], k == 0, k == FT - 1)
                return mm

            def norm_sum(n):
                pe.wait_ge(s_sum, 8 * (n + 1))
                for j in range(NORMS[n][2] // P):
                    mm = pe.matmul(bank[:, 7, j:j + 1], sumsq[:, j * P:(j + 1) * P], ones[:, 0:1], start=True, stop=True)
                mm.then_inc(s_ss, 1)

            def norm_spread(n):
                pe.wait_ge(s_rstd, n + 1)
                for j in range(NORMS[n][2] // P):
                    mm = pe.matmul(bank[:, SPREAD[n], j * P:(j + 1) * P], ones[:, :], diag[:, j, :], start=True, stop=True)
                mm.then_inc(s_bc, 1)

            def mod_totals(n, acc):
                pe.wait_ge(s_macc, 8 * n + 10)
                for m in range(FT):
                    mm = pe.matmul(bank[:, 7, m:m + 1], acc[:, m * P:(m + 1) * P], ones[:, 0:1], start=True, stop=True)
                mm.then_inc(s_mfin, 1)

            def out_groups(n0, group, norm=None, mod=None):
                for idx in range(16):
                    half, m = divmod(idx, FT)
                    pe.wait_ge(s_hup, n0 + idx + 1)
                    group(half, m, bank[:, 4 + m % 2, :]).then_inc(s_out, 1)
                    if mod is not None and idx == 12:
                        mod_totals(mod, mod_acc_f)
                    if norm is not None and idx == 9:
                        norm_sum(norm)
                    if norm is not None and norm != N_END and idx == 11:
                        norm_spread(norm)
                if norm is not None and norm != N_END:
                    norm_sum(norm + 1)

            pe.sem_inc(s_modmm, 4)
            pe.sem_inc(s_mfin, 1)
            pe.wait_ge(s_ident, 3)
            pe.wait_ge(s_par, 16 * 12)
            pe.transpose(bank[:, 0, 0:124], par_rows[:], ident[0:124, 0:124])
            pe.transpose(bank[:, 0, 128:224], b_rows[:], ident[0:96, 0:96]).then_inc(s_par_t, 1)
            pe.wait_ge(s_param, 2)
            for tt in range(TT + CT):
                pe.wait_ge(s_x[tt], 16)
                if tt >= 2:
                    pe.wait_ge(s_xpa, tt - 1)
                    pe.wait_ge(s_xpd, tt - 1)
                for f in range(FT):
                    b = 2 * (tt % 2) + f // 4
                    mm = pe.transpose(bank[:, b, (f % 4) * P:(f % 4 + 1) * P], x_in[:, tt, f * P:(f + 1) * P], ident[:])
                    if f % 4 == 3:
                        mm.then_inc(s_turn, 1)

            pe.wait_ge(s_cond, 2)
            pe.wait_ge(s_xpa, TT + CT)
            pe.wait_ge(s_xpd, TT + CT)
            between = {8: (norm_sum, 0), 10: (norm_spread, 0), 11: (norm_sum, 1), 13: (norm_spread, 1), 14: (norm_sum, 2)}
            for u in range(2 * FT):
                c, k = divmod(u, FT)
                pe.wait_ge(s_mod[k % 4], c * 32 + 16 * (k // 4 + 1))
                for a in range(2):
                    mm = pe.matmul(bank[0:2, 2 * c + a, :], cond[:, k, :], mod_ring[:, k % 4, a * HALF:(a + 1) * HALF],
                                   start=(k == 0), stop=(k == FT - 1))
                mm.then_inc(s_modmm, 1)
                if u in between:
                    step, n = between[u]
                    step(n)
            norm_spread(2)
            for c in range(2):
                pe.wait_ge(s_modrow, 2 * c + 2)
                if c:
                    pe.wait_ge(s_modset, 2)
                for m in range(FT):
                    mm = pe.transpose(bank[:, 4, 2 * (c * FT + m):2 * (c * FT + m) + 2], mod_row[:, c, m * P:(m + 1) * P],
                                      ident[0:2, 0:2])
                mm.then_inc(s_modt, 1)

            pe.wait_ge(s_modset, 2 * 2)
            def project_in(i):
                for g, (unit, part) in enumerate(GROUPS):
                    if part == 0:
                        pe.wait_ge(s_split, 4 * i + unit + 1)
                    pe.wait_ge(s_projev, 10 * i + g + 1)
                    if part == 2:
                        mm = columns(bank[:, g % 5, 0:CTX], unit, ctx_hi, ctx_lo, slice(0, CTX), N_CTX)
                    else:
                        mm = columns(bank[:, g % 5, :], unit, act_hi, act_lo, slice(part * HALF, (part + 1) * HALF), part)
                    mm.then_inc(s_proj, 1)

            def gates(i):
                pe.wait_ge(s_conv, i + 2)
                pe.wait_ge(s_gw, i * 128 + 128)
                for g in range(12):
                    lo = (g % 3) * HALF
                    w = min(HALF, KEYS - lo)
                    pe.wait_ge(s_gatev, 12 * i + g + 1)
                    pe.matmul(bank[:, 5 + g % 3, 0:w], gate_w[:, g // 3, :], x_conv[:, lo:lo + w],
                              start=True, stop=True).then_inc(s_gate, 1)

            project_in(0)
            gates(0)
            with pe.Fori(1, LT) as i:
                project_in(i)
                pe.wait_ge(s_gatev, 12 * i + 3)
                mod_totals(i - 1, mod_acc_p)
                pe.wait_ge(s_mset, i)
                gates(i)

            pe.wait_ge(s_projev, 5 + 10 * LT)
            pe.wait_ge(s_split, U_V + 4)
            for n, tt in enumerate(V_ORDER):
                if n >= 4:
                    pe.wait_ge(s_vev, n - 3)
                a_hi, a_lo, c0 = (act_hi, act_lo, tt * P) if tt < TT else (ctx_hi, ctx_lo, (tt - TT) * P)
                for k in range(FT):
                    w_hi, w_lo = w_slot(k // 2)
                    sl = slice((k % 2) * HALF, (k % 2 + 1) * HALF)
                    mm = product(bank[:, n % 4, :], (a_hi[:, k, c0:c0 + P], a_lo[:, k, c0:c0 + P]),
                                 w_hi[:, sl], w_lo[:, sl], k == 0, k == FT - 1)
                mm.then_inc(s_v, 1)
            pe.wait_ge(s_gatev, 3 + 12 * LT)
            mod_totals(LT - 1, mod_acc_p)

            pe.wait_ge(s_vev, V_TILES)

            def scores(i, s):
                hd, b = divmod(s, TT)
                k0, wide = window(b)
                if b == 0:
                    pe.wait_ge(s_hd, 4 * i + hd + 1)
                pe.wait_ge(s_exp, STEPS * i + s + 1)
                o = 2 * (s % 2) * HALF
                q = q_st[:, hd % 2, b * P:(b + 1) * P]
                parts = [(0, CTX + k0, HALF), (MID, 0, CTX)]
                if wide:
                    parts.insert(1, (HALF, CTX + k0 + HALF, MID - HALF))
                for dst, src, n in parts:
                    out_ = bank_f[:, o + dst:o + dst + n]
                    pe.matmul(out_, q, k_hi[:, hd % 2, src:src + n], start=True, stop=False)
                    mm = pe.matmul(out_, q, k_lo[:, hd % 2, src:src + n], start=False, stop=True)
                mm.then_inc(s_sc, 1)

            def turn_probs(i, s):
                wide = window(s % TT)[1]
                pe.wait_ge(s_pn, STEPS * i + s + 1)

                def turn(dst, src):
                    return pe.matmul(dst, probs[s % 4][:, src], inv_diag[:, s % 4, :], start=True, stop=True)

                pe.wait_ge(s_ptl, 2 * STEPS * i + 2 * s + 1)
                for c in range(4):
                    mm = turn(bank[:, 4, c * P:(c + 1) * P], slice(c * P, (c + 1) * P))
                mm.then_inc(s_pt, 1)
                pe.wait_ge(s_ptl, 2 * STEPS * i + 2 * s + 2)
                if wide:
                    turn(bank[0:64, 5, 2 * P:3 * P], slice(HALF, MID))
                for c in range(2):
                    mm = turn(bank[:, 5, c * P:(c + 1) * P], slice(MID + c * P, MID + (c + 1) * P))
                mm.then_inc(s_pt, 1)

            def values(i, s):
                slot, buf = s // (2 * TT), (s // 2) % 2
                pe.wait_ge(s_ptl, 2 * STEPS * i + 2 * s + 6)
                if s % (2 * TT) == 0:
                    pe.wait_ge(s_vp, 2 * i + slot + 1)
                if s % 4 == 0:
                    pe.wait_ge(s_yl, (STEPS // 4) * i + s // 4 + 1)
                parts = [(6 + c, TT + c, P, 0, 2) for c in range(CT)]
                rows = [[P * (0 <= c - chunks(s + k)[0] < 4) or 64 * (window((s + k) % TT)[1] and c - chunks(s + k)[0] == 4)
                         for c in range(6)] for k in range(2)]
                base = chunks(s)[1]
                for c in range(6):
                    if rows[0][c] and rows[0][c] == rows[1][c]:
                        parts.append((c, base + c, rows[0][c], 0, 2))
                    else:
                        parts += [(c, base + c, rows[k][c], k, 1) for k in range(2) if rows[k][c]]
                col = (s % 4) * P
                for n, (c, tile, rs, k, steps_) in enumerate(parts):
                    mm = product(bank[:, 6 + (s // 4) % 2, col + k * P:col + (k + steps_) * P],
                                 (v_hi[0:rs, slot, tile, :], v_lo[0:rs, slot, tile, :]),
                                 *(a[0:rs, c, k:k + steps_, :].rearrange("p s n -> p (s n)") for a in (pt_hi[buf], pt_lo[buf])),
                                 n == 0, n == len(parts) - 1)
                mm.then_inc(s_pv, 1)

            with pe.Fori(0, 2) as i:
                for j in range(-1, STEPS + 4):
                    if 0 <= j - 3 < STEPS:
                        turn_probs(i, j - 3)
                    if j + 1 < STEPS:
                        scores(i, j + 1)
                    if j >= 4 and j % 2:
                        values(i, j - 5)

            pe.wait_ge(s_yll, LT)
            pe.wait_ge(s_yl, 2 + TT * HEADS // 4)

            def project_out(half, m, dst):
                pe.wait_ge(s_split, U_O + half * FT + m + 1)
                return columns(dst, (m + 2) % 4, act_hi, act_lo, slice(half * HALF, (half + 1) * HALF))

            out_groups(0, project_out, N_F0)

            def ffn_round(layer, i, u0, norm_in, norm_out=None, mod=None, first=False):
                q0 = 4 * ROUNDS * layer
                for q in range(4):
                    half, tile = divmod(q, 2)
                    pe.wait_ge(s_hidf, 4 * i + (q0 + q + 1))
                    for a in range(2):
                        if half == 0:
                            pe.wait_ge(s_split, 6 * i + (u0 + 2 * tile + a + 1))
                        columns(bank[:, 2 * tile + a, :], 2 * tile + a, act_hi, act_lo,
                                slice(half * HALF, (half + 1) * HALF), norm_in + half).then_inc(s_gu, 1)
                        if first and q == 0 and a == 0:
                            norm_spread(norm_in + 1)

                def down(half, m, dst):
                    if m == 0:
                        pe.wait_ge(s_split, 6 * i + (u0 + 6))
                        pe.wait_ge(s_hid, 4 * i + (q0 + 2 * half + 2))
                    sl = slice(half * HALF, (half + 1) * HALF)
                    for k in range(2):
                        w_hi, w_lo = w_slot(4 + k)
                        w = (w_hi[:, m * P:(m + 1) * P], w_lo[:, m * P:(m + 1) * P])
                        mm = product(dst, w, hid_hi[:, k, sl], hid_lo[:, k, sl], k == 0, k == 1)
                    return mm

                out_groups(16 * i + OUT_F[layer], down, norm_out, mod)

            ffn_round(0, 0, U_F0, N_F0, mod=LT, first=True)
            with pe.Fori(1, MODS) as i:
                ffn_round(0, i, U_F0, N_F0, mod=i + LT)
            with pe.Fori(MODS, ROUNDS - 1) as i:
                ffn_round(0, i, U_F0, N_F0)
            ffn_round(0, ROUNDS - 1, U_F0, N_F0, N_S)

            def short_round(i, norm_out=None, first=False):
                for tile in range(2):
                    n = 4 * i + 2 * tile
                    for g, (unit, half) in enumerate(((0, 0), (1, 0), (0, 1), (1, 1), (2, 0), (2, 1))):
                        if half == 0:
                            pe.wait_ge(s_split, 8 * i + (U_S + 3 * tile + unit + 1))
                        if g < 2:
                            pe.wait_ge(s_zf, n + g + 1)
                        elif g == 4:
                            pe.wait_ge(s_cg, n + 1)
                        elif g == 5:
                            pe.wait_ge(s_t, n + 1)
                        columns(bank[:, g % 4, :], (3 * tile + unit) % 4, act_hi, act_lo,
                                slice(half * HALF, (half + 1) * HALF), N_S + half).then_inc(s_sg, 1)
                        if first and tile == 0 and g == 0:
                            norm_spread(N_S + 1)

                def down(half, m, dst):
                    if m == 0:
                        pe.wait_ge(s_split, 8 * i + (U_S + 8))
                        pe.wait_ge(s_z, 4 * i + half + 3)
                    sl = slice(half * HALF, (half + 1) * HALF)
                    for k in range(2):
                        w_hi, w_lo = w_slot(2 + k)
                        w = (w_hi[:, m * P:(m + 1) * P], w_lo[:, m * P:(m + 1) * P])
                        mm = product(dst, w, z_hi[:, k, sl], z_lo[:, k, sl], k == 0, k == 1)
                    return mm

                out_groups(16 * i + OUT_S, down, norm_out)

            pe.wait_ge(s_hidf, 2 + 4 * ROUNDS)
            short_round(0, first=True)
            with pe.Fori(1, FT // 2 - 1) as i:
                short_round(i)
            short_round(FT // 2 - 1, N_F1)

            pe.wait_ge(s_zf, 2 + 2 * FT)
            ffn_round(1, 0, U_F1, N_F1, first=True)
            with pe.Fori(1, ROUNDS - 1) as i:
                ffn_round(1, i, U_F1, N_F1)
            ffn_round(1, ROUNDS - 1, U_F1, N_F1, N_END)

            pe.wait_ge(s_hidf, 2 + 8 * ROUNDS)
            pe.wait_ge(s_gdiag, 1)
            for tt in range(TT):
                if tt == TT // 2:
                    pe.wait_ge(s_hup, 2 + OUT_F[1] + 16 * ROUNDS)
                elif tt == 0:
                    pe.wait_ge(s_hup, 2 + OUT_F[1] + 16 * ROUNDS - FT)
                if tt >= 2:
                    pe.wait_ge(s_fra, tt - 1)
                    pe.wait_ge(s_frd, tt - 1)
                for f in range(FT):
                    b = 2 * (tt % 2) + f // 4
                    mm = pe.matmul(bank[:, b, (f % 4) * P:(f % 4 + 1) * P], h[:, f, tt * P:(tt + 1) * P], gain_diag[:, f, :],
                                   start=True, stop=True)
                    if f % 4 == 3:
                        mm.then_inc(s_fturn, 1)
                if tt == 0:
                    norm_sum(N_END + 1)

        @block.scalar
        def _(act):
            def square(n, f, ready=None):
                src, half, w, *_ = NORMS[n]
                if ready is not None:
                    act.wait_ge(*ready)
                if 8 * n + f >= 2:
                    act.wait_ge(s_sum, 8 * n + f - 1)
                nc.scalar.activation(sq[:, f % 2, 0:w], src[:, f, cols(n)], ACT.Square).then_inc(s_sq, 1)

            def rms(n):
                act.wait_ge(s_ss, n + 1)
                nc.scalar.activation(std[:, 0, 0:NORMS[n][2] // P], bank[:, 7, 0:NORMS[n][2] // P], ACT.Sqrt,
                                     bias=eps_t[:, 0:1], scale=1.0 / D).then_inc(s_sqrt, 1)

            def modulate(n, f):
                _, half, w, gain, shift, which = NORMS[n]
                act.wait_ge(s_scal, 8 * n + f + 1)
                if 8 * n + f >= 2:
                    act.wait_ge(s_norm, 8 * n + f - 1)
                g, b = gains[:, gain, f:f + 1], shift[:, which, f:f + 1]
                nc.scalar.activation(normed[:, f % 2, 0:w], scaled[:, f % 2, 0:w], ACT.Identity, bias=b, scale=g)
                dst = (ctx_hi if n == N_CTX else act_hi)[:, f, cols(n)]
                nc.scalar.activation(dst, scaled[:, f % 2, 0:w], ACT.Identity, bias=b, scale=g).then_inc(s_nhi, 1)

            def norm_pair(n, n0):
                for f in range(FT):
                    square(n, f, (s_hup, n0 + f + 3))
                rms(n)
                for f in range(2):
                    square(n + 1, f, (s_hup, n0 + FT + f + 3))
                for f in range(FT):
                    if n != N_END:
                        modulate(n, f)
                    if f + 2 < FT:
                        square(n + 1, f + 2, (s_hup, n0 + FT + f + 5))
                rms(n + 1)
                if n != N_END:
                    for f in range(FT):
                        modulate(n + 1, f)

            act.sem_inc(s_projev, 5)
            act.sem_inc(s_gatev, 3)
            act.sem_inc(s_exp, 2)
            act.sem_inc(s_qk, 16)

            for tt in range(TT + CT):
                src = x[0, tt * P:(tt + 1) * P, :] if tt < TT else context[0, (tt - TT) * P:(tt - TT + 1) * P, :]
                if tt == 2:
                    act.wait_ge(s_par, 16 * 12)
                act.dma_start(x_in[:, tt, :], src).then_inc(s_x[tt], 16)
            act.wait_ge(s_param, 1)
            for j in range(2):
                nc.scalar.activation(cond[:, :, j], par[:, PAR["c"] + j * FT:PAR["c"] + (j + 1) * FT], ACT.Silu).then_inc(s_cond, 1)
            for tt in range(TT + CT):
                dst = h[:, 0:4, tt * P:(tt + 1) * P] if tt < TT else ctx_t[:, 0:4, (tt - TT) * P:(tt - TT + 1) * P]
                act.wait_ge(s_turn, 2 * tt + 1)
                nc.scalar.copy(dst, bank[:, 2 * (tt % 2), :].rearrange("p (f c) -> p f c", c=P)).then_inc(s_xpa, 1)
            act.wait_ge(s_xpa, TT + CT)
            act.wait_ge(s_xpd, TT + CT)
            act.wait_ge(s_const, 1)
            nc.scalar.activation(sp_t[:, 1, :], sp_t[:, 0, :], ACT.Exp, scale=-1.0).then_inc(s_act, 1)

            act.wait_ge(s_rpb, 48)
            for n in (0, 1, 2):
                for f in range(FT):
                    square(n, f)
                rms(n)

            for c in range(2):
                act.wait_ge(s_modmm, 4 + FT * (c + 1))
                for a in range(2):
                    nc.scalar.copy(mod_row[:, c, a * HALF:(a + 1) * HALF], bank[0:2, 2 * c + a, :]).then_inc(s_modrow, 1)
            act.dma_start(h_spill, h[:, :, :]).then_inc(s_spill, 16)

            act.wait_ge(s_const, 2)
            for n in (0, 1, 2):
                for f in range(FT):
                    modulate(n, f)

            act.wait_ge(s_spill, 16)
            act.wait_ge(s_norm, 8 * (N_CTX + 1))
            act.wait_ge(s_const, 3)
            with act.Fori(0, LT) as i:
                def out_of(g):
                    act.wait_ge(s_proj, 10 * i + g + 1)

                act.wait_ge(s_conv, i + 1)
                for g, (unit, part) in enumerate(GROUPS[:8]):
                    out_of(g)
                    w = CTX if part == 2 else HALF
                    if unit == 0:
                        dst = 2 if part == 2 else CTX + 5 + part * HALF
                        nc.scalar.copy(x_pad[:, dst:dst + w], bank[:, g % 5, 0:w]).then_inc(s_projev, 1)
                        continue
                    if g == 1:
                        act.wait_ge(s_qk, 80 * i + 16)
                    o = 2 * (unit - 1) + part
                    nc.scalar.activation(qk_out[:, o, 0:w], bank[:, g % 5, 0:w], ACT.Copy,
                                         scale=-(64 ** -0.5) if unit == 1 else 1.0).then_inc(s_projev, 1)
                    act.wait_ge(s_projev, 10 * i + (5 + g + 1))
                    alone(act)
                    at0 = 0 if part == 2 else (CTX if unit == 2 else 0) + part * HALF
                    dst = (q_spill if unit == 1 else k_spill)[bass.ds(i, 1), :, at0:at0 + w]
                    act.dma_start(dst.rearrange("a p n -> p (a n)"), qk_out[:, o, 0:w]).then_inc(s_qk, 16)
                act.wait_ge(s_lru, i + 1)
                for g in (8, 9):
                    out_of(g)
                    nc.scalar.activation(g_gelu[:, (g - 8) * HALF:(g - 7) * HALF], bank[:, g % 5, :],
                                         ACT.Gelu_apprx_tanh).then_inc(s_projev, 1)
                for g in range(12):
                    m, lo = g // 3, (g % 3) * HALF
                    w = min(HALF, KEYS - lo)
                    act.wait_ge(s_gate, 12 * i + g + 1)
                    alone(act)
                    nc.scalar.activation((lru_i if m % 2 else lru_r)[:, m // 2, lo:lo + w], bank[:, 5 + g % 3, 0:w], ACT.Tanh,
                                         bias=half_b[:, bass.ds(i + (m % 2 * 8 + m // 2 * LT), 1)], scale=0.5).then_inc(s_gatev, 1)
                act.wait_ge(s_gatev, 12 * i + 15)
                act.wait_ge(s_rfree, i + 1)
                alone(act)
                for d in range(2):
                    sp = sp2[:, bass.ds(i + d * LT, 1)]
                    nc.scalar.activation(lru_q[:, d, :], lru_r[:, d, :], ACT.Tanh, bias=sp, scale=sp).then_inc(s_s, 1)
                for d in range(2):
                    sp = sp4[:, bass.ds(i + d * LT, 1)]
                    nc.scalar.activation(lru_r[:, d, :], lru_r[:, d, :], ACT.Exp, bias=sp, scale=sp).then_inc(s_s, 1)
                act.wait_ge(s_s, 4 * i + 4)
                alone(act)
                for d in range(2):
                    nc.scalar.activation(lru_q[:, d, :], lru_q[:, d, :], ACT.Sqrt).then_inc(s_rs, 1)

            act.wait_ge(s_qk, 16 + 80 * LT)
            for n, tt in enumerate(V_ORDER):
                act.wait_ge(s_v, n + 1)
                nc.scalar.copy(v_tok[:, tt, :], bank[:, n % 4, :]).then_inc(s_vev, 1)
                act.wait_ge(s_vev, n + 1)
                act.dma_start(v_spill[:, tt, :], v_tok[:, tt, :]).then_inc(s_vst, 16)

            def exps(i, s):
                w = MID if window(s % TT)[1] else HALF
                o = 2 * (s % 2) * HALF
                st = stat[:, s % 4, :]
                act.wait_ge(s_min, STEPS * i + s + 1)
                nc.scalar.activation(probs[s % 4][:, 0:w], probs[s % 4][:, 0:w], ACT.Exp, bias=st[:, 1:2], scale=-1.0,
                                     accum_out=st[:, 2:3])
                nc.scalar.activation(probs[s % 4][:, MID:WIDE], bank_f[:, o + MID:o + WIDE], ACT.Exp, bias=st[:, 1:2],
                                     scale=-1.0, accum_out=st[:, 3:4]).then_inc(s_exp, 1)

            def turned_high(i, s):
                act.wait_ge(s_pt, 2 * STEPS * i + 2 * s + 1)
                pt, c = pt_hi[(s // 2) % 2][:, :, s % 2, :], chunks(s)[0]
                nc.scalar.copy(pt[:, c:c + 4, :], bank[:, 4, :].rearrange("p (c n) -> p c n", n=P)).then_inc(s_pth, 1)
                act.wait_ge(s_pt, 2 * STEPS * i + 2 * s + 2)
                if window(s % TT)[1]:
                    nc.scalar.copy(pt[0:64, c + 4, :], bank[0:64, 5, 2 * P:3 * P])
                nc.scalar.copy(pt[:, 6:8, :], bank[:, 5, 0:2 * P].rearrange("p (c n) -> p c n", n=P)).then_inc(s_pth, 1)

            def y_high(i, s):
                hd, q = s // TT, (s // 4) % 2
                rows = slice(64 * (hd % 2), 64 * (hd % 2) + 64)
                act.wait_ge(s_pv, (STEPS // 2) * i + s // 2 + 1)
                alone(act)
                nc.scalar.copy(act_hi[rows, bass.ds(2 * i + hd // 2, 1), q * HALF:(q + 1) * HALF].rearrange("p a n -> p (a n)"),
                               bank[rows, 6 + q, :]).then_inc(s_yh, 1)

            with act.Fori(0, 2) as i:
                for j in range(STEPS + 4):
                    if 0 <= j - 3 < STEPS:
                        turned_high(i, j - 3)
                    if j < STEPS:
                        exps(i, j)
                    if j >= 4 and (j - 4) % 4 == 3:
                        y_high(i, j - 4)

            act.wait_ge(s_const, 4)
            norm_pair(N_F0, 0)

            def ffn_round(layer, i):
                q0 = 4 * ROUNDS * layer
                for q in range(4):
                    half, tile = divmod(q, 2)
                    act.wait_ge(s_gu, 8 * i + (2 * q0 + 2 * q + 1))
                    act.wait_ge(s_hidf, 4 * i + (q0 + q + 1))
                    nc.scalar.activation(silu_g[:, q % 2, :], bank[:, 2 * tile, :], ACT.Silu).then_inc(s_silu, 1)
                    act.wait_ge(s_hidf, 4 * i + (q0 + q + 3))
                    nc.scalar.copy(hid_hi[:, tile, half * HALF:(half + 1) * HALF], hid_f[:, q % 2, :]).then_inc(s_hidh, 1)

            with act.Fori(0, ROUNDS - 1) as i:
                ffn_round(0, i)
            ffn_round(0, ROUNDS - 1)
            act.wait_ge(s_const, 5)
            norm_pair(N_S, OUT_F[0] + 16 * (ROUNDS - 1))

            def short_round(i):
                for tile in range(2):
                    n = 4 * i + 2 * tile
                    for half in range(2):
                        act.wait_ge(s_sg, 12 * i + (6 * tile + 2 * half + 1))
                        nc.scalar.copy(cg_sb[:, half, :], bank[:, 2 * half, :]).then_inc(s_cg, 1)
                    for half in range(2):
                        act.wait_ge(s_zf, n + half + 3)
                        nc.scalar.copy(z_hi[:, tile, half * HALF:(half + 1) * HALF], z_f[:, half, :]).then_inc(s_zh, 1)

            with act.Fori(0, FT // 2 - 1) as i:
                short_round(i)
            short_round(FT // 2 - 1)
            norm_pair(N_F1, OUT_S + 16 * (FT // 2 - 1))

            with act.Fori(0, ROUNDS - 1) as i:
                ffn_round(1, i)
            ffn_round(1, ROUNDS - 1)
            norm_pair(N_END, OUT_F[1] + 16 * (ROUNDS - 1))

            for tt in range(TT):
                act.wait_ge(s_fscale, tt // 4 + 1)
                act.wait_ge(s_fturn, 2 * tt + 1)
                if tt >= 2:
                    act.wait_ge(s_store[tt % 2], 16 * (tt // 2))
                nc.scalar.activation(fin_rows[:, tt % 2, 0:HALF], bank[:, 2 * (tt % 2), :], ACT.Copy,
                                     scale=fin_scale[:, tt:tt + 1]).then_inc(s_fra, 1)

        @block.vector
        def _(dve):
            steps = Steps(dve, s_dve)
            V = nc.vector

            def add_squares(n, f):
                w = NORMS[n][2]
                dve.wait_ge(s_sq, 8 * n + f + 1)
                if f == 0:
                    if n:
                        dve.wait_ge(s_ss, n)
                    V.tensor_copy(sumsq[:, 0:w], sq[:, 0, 0:w]).then_inc(s_sum, 1)
                else:
                    dve.wait_ge(s_sum, 8 * n + f)
                    V.tensor_tensor(sumsq[:, 0:w], sumsq[:, 0:w], sq[:, f % 2, 0:w], ALU.add).then_inc(s_sum, 1)

            def inverse_rms(n):
                dve.wait_ge(s_sqrt, n + 1)
                if 0 < n < N_END:
                    dve.wait_ge(s_bc, n)
                w = NORMS[n][2] // P
                if n >= N_END:
                    V.reciprocal(fin_scale[:, w * (n - N_END):w * (n - N_END + 1)], std[:, 0, 0:w]).then_inc(s_fscale, 1)
                    return
                steps.run(V.reciprocal(std[:, 1, 0:w], std[:, 0, 0:w]))
                for j in range(w):
                    last = V.tensor_scalar(diag[:, j, :], ident[:], std[:, 1, j:j + 1], None, ALU.mult)
                last.then_inc(s_rstd, 1)

            def scale(n, f):
                src, half, w, gain, *_ = NORMS[n]
                dve.wait_ge(s_bc, n + 1)
                if 8 * n + f >= 2:
                    dve.wait_ge(s_nhi, 8 * n + f - 1)
                V.tensor_tensor(scaled[:, f % 2, 0:w], src[:, f, cols(n)], bank[:, SPREAD[n], 0:w], ALU.mult).then_inc(s_scal, 1)

            def low(n, f):
                w = NORMS[n][2]
                dve.wait_ge(s_nhi, 8 * n + f + 1)
                a_hi, a_lo = (ctx_hi, ctx_lo) if n == N_CTX else (act_hi, act_lo)
                V.tensor_tensor(a_lo[:, f, cols(n)], normed[:, f % 2, 0:w], a_hi[:, f, cols(n)], ALU.subtract).then_inc(s_norm, 1)

            def apply_norm(n, between=lambda f: None):
                scale(n, 0)
                scale(n, 1)
                for f in range(FT):
                    low(n, f)
                    if f + 2 < FT:
                        scale(n, f + 2)
                    between(f)

            def update(n0, idx, gate):
                half, m = divmod(idx, FT)
                dve.wait_ge(s_out, n0 + idx + 1)
                dst = h[:, m, half * HALF:(half + 1) * HALF]
                V.scalar_tensor_tensor(out=dst, in0=bank[:, 4 + m % 2, :], scalar=mods[:, gate, m:m + 1], in1=dst,
                                       op0=ALU.mult, op1=ALU.add).then_inc(s_hup, 1)

            def mod_unit(n, k, ring, acc):
                dve.wait_ge(s_mu[k % 2], 64 * n + 16 * (k // 2 + 1))
                if k == 0:
                    dve.wait_ge(s_mfin, n + 1)
                    ins = V.tensor_scalar(acc[:], ring[:, 0, :], cond[:, 0, 0:1], None, ALU.mult)
                else:
                    dve.wait_ge(s_macc, 8 * n + (k + 2))
                    ins = V.scalar_tensor_tensor(out=acc[:], in0=ring[:, k % 2, :], scalar=cond[:, k, 0:1], in1=acc[:],
                                                 op0=ALU.mult, op1=ALU.add)
                ins.then_inc(s_macc, 1)

            def mod_set(n, row):
                dve.wait_ge(s_mfin, n + 2)
                V.tensor_tensor(mods[:, bass.ds(row, 1), :].rearrange("p a f -> p (a f)"), bank[:, 7, 0:FT],
                                mod_bias[:, bass.ds(row, 1), :].rearrange("p a f -> p (a f)"), ALU.add).then_inc(s_mset, 1)

            def set_gains(*sets):
                for k, src, which, g in sets:
                    last = V.scalar_tensor_tensor(out=gains[:, k, :], in0=src[:, which, :], scalar=1.0, in1=par[:, g:g + FT],
                                                  op0=ALU.add, op1=ALU.mult)
                last.then_inc(s_const, 1)

            def last_updates(n0, gate, n):
                for f in range(FT):
                    if n == N_F0 and f in (0, 3, 6):
                        dve.wait_ge(s_reload[f // 3], 16)
                    update(n0, f, gate)
                    if f:
                        add_squares(n, f - 1)
                add_squares(n, FT - 1)
                update(n0, FT, gate)
                update(n0, FT + 1, gate)
                inverse_rms(n)
                update(n0, FT + 2, gate)
                add_squares(n + 1, 0)
                add_squares(n + 1, 1)

                def between(f):
                    if f + 3 < FT:
                        update(n0, FT + f + 3, gate)
                    if f + 2 < FT:
                        add_squares(n + 1, f + 2)

                if n == N_END:
                    for f in range(FT):
                        between(f)
                    inverse_rms(n + 1)
                    return
                apply_norm(n, between)
                inverse_rms(n + 1)
                apply_norm(n + 1)

            for s, credits in ((s_conv, 1), (s_lru, 1), (s_macc, 2), (s_ptl, 2), (s_yl, 2), (s_hup, 2),
                               (s_hidf, 2), (s_zf, 2)):
                dve.sem_inc(s, credits)

            dve.wait_ge(s_par_t, 1)
            V.tensor_copy(par[:], bank[:, 0, 0:124]).then_inc(s_param, 1)
            V.tensor_copy(mod_bias[:, :, :].rearrange("p a f -> p (a f)"), bank[:, 0, 128:224]).then_inc(s_param, 1)
            for tt in range(TT + CT):
                dst = h[:, 4:8, tt * P:(tt + 1) * P] if tt < TT else ctx_t[:, 4:8, (tt - TT) * P:(tt - TT + 1) * P]
                dve.wait_ge(s_turn, 2 * tt + 2)
                V.tensor_copy(dst, bank[:, 2 * (tt % 2) + 1, :].rearrange("p (f c) -> p f c", c=P)).then_inc(s_xpd, 1)
            dve.wait_ge(s_param, 2)
            lam = par[:, PAR["lam"]:PAR["lam"] + 8]
            steps.run(V.tensor_scalar(sp_t[:, 2, :], lam, -1.0, None, ALU.mult))
            V.tensor_tensor(sp_t[:, 0, :], sp_t[:, 2, :], lam, ALU.max).then_inc(s_const, 1)
            steps.run(V.tensor_scalar(half_b[:], par[:, PAR["br"]:PAR["br"] + 16], 0.5, None, ALU.mult))
            for n in (0, 1, 2):
                for f in range(FT):
                    add_squares(n, f)
                inverse_rms(n)
            for c in range(2):
                dve.wait_ge(s_modt, c + 1)
                summed = bank[:, 4, 2 * c * FT:2 * (c + 1) * FT].rearrange("p (m j) -> p m j", j=2)
                for j, dst in enumerate((mods, mods_ctx)):
                    V.tensor_tensor(dst[:, c, :], summed[:, :, j], mod_bias[:, c, :], ALU.add).then_inc(s_modset, 1)
            dve.wait_ge(s_modset, 2 * 2)
            set_gains((0, mods, SC1, PAR["n1"]), (1, mods_ctx, SC1, PAR["n1"]))
            for n in (0, 1, 2):
                apply_norm(n)

            dve.wait_ge(s_act, 1)
            e, y, y2, acc = (sp_t[:, k, :] for k in (1, 3, 4, 0))
            steps.run(V.tensor_scalar(y2, e, 2.0, None, ALU.add))
            steps.run(V.reciprocal(y, y2))
            steps.run(V.tensor_tensor(y, e, y, ALU.mult))
            steps.run(V.tensor_tensor(y2, y, y, ALU.mult))
            steps.run(V.tensor_scalar(acc, y2, 1.0 / 17, 1.0 / 15, ALU.mult, ALU.add))
            for k in (13, 11, 9, 7, 5, 3, 1):
                steps.run(V.tensor_tensor(acc, acc, y2, ALU.mult))
                steps.run(V.tensor_scalar(acc, acc, 1.0 / k, None, ALU.add))
            steps.run(V.tensor_tensor(acc, acc, y, ALU.mult))
            steps.run(V.tensor_scalar(sp_t[:, 2, :], sp_t[:, 2, :], 0.0, 2.0, ALU.max, ALU.mult))
            steps.run(V.scalar_tensor_tensor(out=sp2[:], in0=acc, scalar=4.0, in1=sp_t[:, 2, :], op0=ALU.mult, op1=ALU.add))
            V.tensor_scalar(sp4[:], sp2[:], -2.0, None, ALU.mult).then_inc(s_const, 1)

            def convolve(i):
                dve.wait_ge(s_projev, 10 * i + 10)
                for j in range(4):
                    w = par[:, bass.ds(i + (PAR["conv_w"] + j * LT), 1)]
                    for part, (src, dst, n) in enumerate(((0, 0, CTX), (CTX + 3, CTX, SEQ))):
                        win, xc = x_pad[:, src + j:src + j + n], x_conv[:, dst:dst + n]
                        if j == 0:
                            ins = V.tensor_scalar(xc, win, w, par[:, bass.ds(i + PAR["conv_b"], 1)], ALU.mult, ALU.add)
                        else:
                            ins = V.scalar_tensor_tensor(out=xc, in0=win, scalar=w, in1=xc, op0=ALU.mult, op1=ALU.add)
                        if part:
                            ins.then_inc(s_conv, 1) if j == 3 else steps.run(ins)

            def recur(i):
                for k in range(2):
                    mod_unit(i, k, mod_in_p, mod_acc_p)
                for d in range(2):
                    R, I, Q = lru_r[:, d, :], lru_i[:, d, :], lru_q[:, d, :]
                    dve.wait_ge(s_gatev, 12 * i + (3 + 6 * (d + 1)))
                    dve.wait_ge(s_conv, i + 2)
                    V.scalar_tensor_tensor(out=I, in0=I, scalar=1.0, in1=x_conv[:], op0=ALU.add, op1=ALU.mult)
                    dve.wait_ge(s_rs, 2 * i + d + 1)
                    steps.run(V.scalar_tensor_tensor(out=Q, in0=R, scalar=1.0, in1=Q, op0=ALU.add, op1=ALU.mult))
                    steps.run(V.tensor_tensor(I, I, Q, ALU.mult))
                    if d == 0:
                        steps.run(V.tensor_tensor_scan(Q, R, I, 0.0, ALU.mult, ALU.add))
                    else:
                        rev, lat = slice(CTX - 1, None, -1), slice(KEYS - 1, CTX - 1, -1)
                        steps.run(V.tensor_tensor_scan(Q[:, rev], R[:, rev], I[:, rev], 0.0, ALU.mult, ALU.add))
                        steps.run(V.tensor_tensor_scan(Q[:, lat], R[:, lat], I[:, lat], Q[:, 0:1], ALU.mult, ALU.add))
                    for k in range(3 * d + 2, 3 * d + 5):
                        mod_unit(i, k, mod_in_p, mod_acc_p)
                steps.run(V.tensor_tensor(lru_i[:, 0, 0:SEQ], lru_q[:, 0, CTX:], lru_q[:, 1, CTX:], ALU.add))
                dve.wait_ge(s_projev, 10 * i + 15)
                V.scalar_tensor_tensor(out=lru_q[:, 0, 0:SEQ], in0=lru_i[:, 0, 0:SEQ], scalar=0.5, in1=g_gelu[:],
                                       op0=ALU.mult, op1=ALU.mult).then_inc(s_lru, 1)

            dve.wait_ge(s_pad, 3)
            convolve(0)
            recur(0)
            with dve.Fori(1, LT) as i:
                steps.begin_loop(i - 1, 11)
                convolve(i)
                mod_set(i - 1, i + 1)
                recur(i)
            steps.end_loop(LT - 1)
            mod_set(LT - 1, LT + 1)
            dve.wait_ge(s_mset, LT)
            set_gains((2, mods, SC2, PAR["n2"]))

            dve.wait_ge(s_v, V_TILES)

            def min_logit(i, s):
                hd, b = divmod(s, TT)
                k0, wide = window(b)
                w = MID if wide else HALF
                o = 2 * (s % 2) * HALF
                at0 = EDGE if wide else (k0 - 2 * b * GRID) + 6 * GRID
                st = stat[:, s % 4, :]
                if b == 0:
                    dve.wait_ge(s_bias, 4 * i + hd + 1)
                dve.wait_ge(s_sc, STEPS * i + s + 1)
                steps.run(V.tensor_reduce(st[:, 0:1], bank_f[:, o + MID:o + WIDE], AX_X, ALU.min))
                alone(dve)
                V.tensor_tensor_reduce(out=probs[s % 4][:, 0:w], in0=bank_f[:, o:o + w], in1=bias_t[:, hd % 2, at0:at0 + w],
                                       scale=1.0, scalar=st[:, 0:1], op0=ALU.add, op1=ALU.min, accum_out=st[:, 1:2]
                                       ).then_inc(s_min, 1)

            def inverse_sum(i, s):
                st = stat[:, s % 4, :]
                dve.wait_ge(s_exp, STEPS * i + s + 3)
                steps.run(V.tensor_tensor(st[:, 4:5], st[:, 2:3], st[:, 3:4], ALU.add))
                steps.run(V.reciprocal(st[:, 5:6], st[:, 4:5]))
                V.tensor_scalar(inv_diag[:, s % 4, :], ident[:], st[:, 5:6], None, ALU.mult).then_inc(s_pn, 1)

            def turned_low(i, s):
                buf, c = (s // 2) % 2, chunks(s)[0]
                parts = [(P, c, 4, bank[:, 4, :])]
                if window(s % TT)[1]:
                    parts.append((64, c + 4, 1, bank[0:64, 5, 2 * P:3 * P]))
                parts.append((P, 6, 2, bank[:, 5, 0:2 * P]))
                for n, (rows, first, count, src) in enumerate(parts):
                    if n < 2:
                        dve.wait_ge(s_pth, 2 * STEPS * i + (2 * s + n + 1))
                    hi, lo = (a[0:rows, first:first + count, s % 2, :] for a in (pt_hi[buf], pt_lo[buf]))
                    ins = V.tensor_tensor(lo, src.rearrange("p (c n) -> p c n", n=P), hi, ALU.subtract)
                    if n in (0, len(parts) - 1):
                        ins.then_inc(s_ptl, 1)

            def y_low(i, s):
                hd, q = s // TT, (s // 4) % 2
                rows = slice(64 * (hd % 2), 64 * (hd % 2) + 64)
                tile = (rows, bass.ds(2 * i + hd // 2, 1), slice(q * HALF, (q + 1) * HALF))
                dve.wait_ge(s_yh, (STEPS // 4) * i + s // 4 + 1)
                V.tensor_tensor(act_lo[tile].rearrange("p a n -> p (a n)"), bank[rows, 6 + q, :],
                                act_hi[tile].rearrange("p a n -> p (a n)"), ALU.subtract).then_inc(s_yl, 1)

            with dve.Fori(0, 2) as i:
                steps.begin_loop(i, 3 * STEPS)
                for j in range(STEPS + 5):
                    if j < STEPS:
                        min_logit(i, j)
                    if 0 <= j - 1 < STEPS:
                        inverse_sum(i, j - 1)
                    if j >= 5 and (j - 5) % 4 == 3:
                        y_low(i, j - 5)
                    if 0 <= j - 3 < STEPS:
                        turned_low(i, j - 3)
            steps.end_loop(2)

            last_updates(0, G1, N_F0)

            def hidden(layer, i, mod=None):
                q0 = 4 * ROUNDS * layer
                for q in range(4):
                    half, tile = divmod(q, 2)
                    dve.wait_ge(s_silu, 4 * i + (q0 + q + 1))
                    dve.wait_ge(s_gu, 8 * i + (2 * q0 + 2 * q + 2))
                    V.tensor_tensor(hid_f[:, q % 2, :], silu_g[:, q % 2, :], bank[:, 2 * tile + 1, :], ALU.mult).then_inc(s_hidf, 1)
                    dve.wait_ge(s_hidh, 4 * i + (q0 + q + 1))
                    sl = slice(half * HALF, (half + 1) * HALF)
                    V.tensor_tensor(hid_lo[:, tile, sl], hid_f[:, q % 2, :], hid_hi[:, tile, sl], ALU.subtract).then_inc(s_hid, 1)
                    if mod is not None:
                        for k in ((0, 1), (2, 3), (4,), ())[q]:
                            mod_unit(mod, k, mod_in_f, mod_acc_f)

            def ffn(layer, norm):
                first = 0 if layer else MODS
                with dve.Fori(first, ROUNDS - 1) as i:
                    hidden(layer, i)
                    for idx in range(16):
                        update(16 * i + OUT_F[layer], idx, MODS * layer + G2)
                hidden(layer, ROUNDS - 1)
                last_updates(OUT_F[layer] + 16 * (ROUNDS - 1), MODS * layer + G2, norm)

            with dve.Fori(0, MODS) as i:
                hidden(0, i, LT + i)
                for idx in range(16):
                    update(16 * i + OUT_F[0], idx, G2)
                    if idx in (1, 4, 7):
                        mod_unit(i + LT, 5 + idx // 3, mod_in_f, mod_acc_f)
                    if idx == 13:
                        mod_set(i + LT, i + MODS)
            dve.wait_ge(s_mset, LT + MODS)
            set_gains((3, mods, MODS + SC1, PAR["n1"] + FT), (4, mods, MODS + SC2, PAR["n2"] + FT))
            ffn(0, N_S)

            for lo in (0, SEQ + 1):
                V.memset(t_pad[:, lo:lo + 1], 0.0).then_inc(s_tz, 1)
            dve.wait_ge(s_tz, 2)

            def short(i):
                for tile in range(2):
                    n, g = 4 * i + 2 * tile, 12 * i + 6 * tile
                    for half in range(2):
                        dve.wait_ge(s_cg, n + half + 1)
                        dve.wait_ge(s_sg, g + (2 * half + 2))
                        V.tensor_tensor(t_pad[:, 1 + half * HALF:1 + (half + 1) * HALF], cg_sb[:, half, :],
                                        bank[:, 2 * half + 1, :], ALU.mult).then_inc(s_t, 1)
                    dve.wait_ge(s_t, n + 2)
                    for j in range(3):
                        w = par[:, bass.ds(2 * i + (PAR["short_w"] + j * FT + tile), 1)]
                        if j == 0:
                            steps.run(V.tensor_scalar(conv_t[:], t_pad[:, 0:SEQ], w, None, ALU.mult))
                        else:
                            steps.run(V.scalar_tensor_tensor(out=conv_t[:], in0=t_pad[:, j:j + SEQ], scalar=w, in1=conv_t[:],
                                                             op0=ALU.mult, op1=ALU.add))
                    for half in range(2):
                        sl = slice(half * HALF, (half + 1) * HALF)
                        dve.wait_ge(s_sg, g + (5 + half))
                        V.tensor_tensor(z_f[:, half, :], conv_t[:, sl], bank[:, half, :], ALU.mult).then_inc(s_zf, 1)
                        dve.wait_ge(s_zh, n + half + 1)
                        V.tensor_tensor(z_lo[:, tile, sl], z_f[:, half, :], z_hi[:, tile, sl], ALU.subtract).then_inc(s_z, 1)

            with dve.Fori(0, FT // 2 - 1) as i:
                steps.begin_loop(i, 6)
                short(i)
                for idx in range(16):
                    update(16 * i + OUT_S, idx, MODS + G1)
            steps.end_loop(FT // 2 - 1)
            short(FT // 2 - 1)
            last_updates(OUT_S + 16 * (FT // 2 - 1), MODS + G1, N_F1)

            dve.wait_ge(s_norm, 8 * N_END)
            for f in range(FT):
                last = V.tensor_scalar(gain_diag[:, f, :], ident[:], par[:, PAR["nf"] + f:PAR["nf"] + f + 1], None, ALU.mult)
            last.then_inc(s_gdiag, 1)

            ffn(1, N_END)

            dve.wait_ge(s_fscale, 2)
            for tt in range(TT):
                dve.wait_ge(s_fturn, 2 * tt + 2)
                if tt >= 2:
                    dve.wait_ge(s_store[tt % 2], 16 * (tt // 2))
                V.tensor_scalar(fin_rows[:, tt % 2, HALF:D], bank[:, 2 * (tt % 2) + 1, :], fin_scale[:, tt:tt + 1], None,
                                ALU.mult).then_inc(s_frd, 1)


INPUTS = ("x", "c", "ctx", "c_ctx", "mod_w", "mod_b", "norm1_g", "norm2_g", "ffn_w_gu", "ffn_w_down", "e_w_in",
          "e_w_out", "e_conv_w", "e_conv_b", "e_lru_wr", "e_lru_br", "e_lru_wi", "e_lru_bi", "e_lru_lam", "e_rpb",
          "o_w_in", "o_conv_w", "o_w_out", "final_g")


def kernel(**inputs):
    import numpy as np
    import concourse.bacc as bacc
    from concourse.bass_utils import run_bass_kernel_spmd

    nc = bacc.Bacc("TRN2", target_bir_lowering=False, num_devices=1)
    arrays, tensors = {}, {}
    for name in INPUTS:
        a = np.ascontiguousarray(inputs[name])
        arrays["in_" + name] = a
        tensors[name] = nc.dram_tensor("in_" + name, a.shape, F32, kind="ExternalInput").ap()
    tensors["out"] = nc.dram_tensor("out", inputs["x"].shape, F32, kind="ExternalOutput").ap()
    backbone(nc, tensors)
    result = run_bass_kernel_spmd(nc, [arrays], core_ids=[0])
    return result.results[0]["out"]
```
